# Optimizing a Trainium2 kernel written in Bass

```python
import math
import jax
import jax.numpy as jnp
from jax import lax
import numpy as np
import jax, jax.numpy as jnp

D_MODEL = 1024
BATCH = 1
SEQ = 512
DEPTH = 1

HEAD_DIM = 64
NSA_HEADS = 8
NSA_KV_GROUPS = 2
NSA_GROUP = NSA_HEADS // NSA_KV_GROUPS
NSA_WIDTH = NSA_HEADS * HEAD_DIM
NSA_KV_WIDTH = NSA_KV_GROUPS * HEAD_DIM
CMP_BLOCK = 32
CMP_STRIDE = 16
CMP_SPAN = CMP_BLOCK // CMP_STRIDE
CMP_HIDDEN = 256
SLC_BLOCK = 64
SLC_RATIO = SLC_BLOCK // CMP_STRIDE
SLC_TOPK = 16
OVERLAP_W = (1, 2, 2, 2, 1)
WINDOW = 512
WIN_QBLOCK = 128
REL_BUCKETS = 32
REL_MAX_DIST = 128
RWKV_HEADS = 8
RWKV_WIDTH = RWKV_HEADS * HEAD_DIM
LORA_W = 64
LORA_A = 64
LORA_G = 128
GN_EPS = 64e-5
D_FF = 2816
CONV_WIDTH = 3
RMS_EPS = 1e-6
NEG_INF = -1e30
FORCE = 1e9

RWKV_SIZES = (RWKV_WIDTH, RWKV_WIDTH, RWKV_WIDTH, LORA_W, LORA_A, LORA_G)
RWKV_IN_WIDTH = sum(RWKV_SIZES)
RWKV_SPLITS = tuple(np.cumsum(RWKV_SIZES)[:-1].tolist())
IN_SIZES = (NSA_WIDTH, NSA_KV_WIDTH, NSA_KV_WIDTH, NSA_KV_WIDTH, NSA_KV_WIDTH, NSA_KV_WIDTH, NSA_KV_WIDTH,
            NSA_HEADS * 3, RWKV_IN_WIDTH, D_MODEL, D_MODEL)
IN_WIDTH = sum(IN_SIZES)
IN_SPLITS = tuple(np.cumsum(IN_SIZES)[:-1].tolist())


def rmsnorm(x, g):
    xf = x.astype(jnp.float32)
    y = xf * lax.rsqrt(jnp.mean(xf * xf, axis=-1, keepdims=True) + RMS_EPS)
    return (y * g.astype(jnp.float32)).astype(x.dtype)

def t5_bucket(dist):
    n = jnp.maximum(dist, 0)
    max_exact = REL_BUCKETS // 2
    ratio = jnp.log(jnp.maximum(n, 1).astype(jnp.float32) / max_exact) / math.log(REL_MAX_DIST / max_exact)
    large = jnp.minimum(max_exact + (ratio * (REL_BUCKETS - max_exact)).astype(jnp.int32), REL_BUCKETS - 1)
    return jnp.where(n < max_exact, n, large)

def masked_softmax(s, mask, axis):
    s = jnp.where(mask, s.astype(jnp.float32), NEG_INF)
    e = jnp.exp(s - jnp.max(s, axis=axis, keepdims=True)) * mask
    return e / jnp.maximum(jnp.sum(e, axis=axis, keepdims=True), 1e-30)

def compress_blocks(kv, pe, w1, w2):
    b, s, g, dh = kv.shape
    chunks = kv.reshape(b, s // CMP_STRIDE, CMP_STRIDE, g, dh)
    n_cmp = s // CMP_STRIDE - CMP_SPAN + 1
    blocks = jnp.concatenate([chunks[:, i:i + n_cmp] for i in range(CMP_SPAN)], axis=2)
    blocks = blocks + pe[None, None, :, None, :]
    flat = blocks.transpose(0, 1, 3, 2, 4).reshape(b, n_cmp, g, CMP_BLOCK * dh)
    return jax.nn.gelu(flat @ w1) @ w2

def nsa_mixer(q, k_c, v_c, k_s, v_s, k_w, v_w, gate, rel_bias, q_norm_g, k_norm_g,
              cmp_pe_k, cmp_w1_k, cmp_w2_k, cmp_pe_v, cmp_w1_v, cmp_w2_v):
    b, s, _ = q.shape
    G, R, dh = NSA_KV_GROUPS, NSA_GROUP, HEAD_DIM
    q = rmsnorm(q.reshape(b, s, G, R, dh), q_norm_g) * (dh ** -0.5)
    k_c, v_c, k_s, v_s, k_w, v_w = [t.reshape(b, s, G, dh) for t in (k_c, v_c, k_s, v_s, k_w, v_w)]
    t_pos = jnp.arange(s)
    bias_tab = rel_bias.reshape(REL_BUCKETS, G, R)

    kc = rmsnorm(compress_blocks(k_c, cmp_pe_k, cmp_w1_k, cmp_w2_k), k_norm_g)
    vc = compress_blocks(v_c, cmp_pe_v, cmp_w1_v, cmp_w2_v)
    n_cmp = kc.shape[1]
    blk_end = jnp.arange(n_cmp) * CMP_STRIDE + CMP_BLOCK - 1
    dist_c = t_pos[:, None] - blk_end[None, :]
    bias_c = bias_tab[t5_bucket(dist_c)].transpose(2, 3, 0, 1)
    s_c = jnp.einsum('bsgrd,bcgd->bgrsc', q, kc).astype(jnp.float32) + bias_c
    p_c = masked_softmax(s_c, dist_c >= 0, axis=-1)
    o_cmp = jnp.einsum('bgrsc,bcgd->bsgrd', p_c, vc)

    n_slc = s // SLC_BLOCK
    imp_c = jnp.sum(p_c, axis=2)
    imp_pad = jnp.pad(imp_c, ((0, 0), (0, 0), (0, 0), (CMP_SPAN - 1, CMP_SPAN)))
    imp = OVERLAP_W[0] * imp_pad[..., 0:SLC_RATIO * n_slc:SLC_RATIO]
    for o in range(1, SLC_RATIO + CMP_SPAN - 1):
        imp = imp + OVERLAP_W[o] * imp_pad[..., o:o + SLC_RATIO * n_slc:SLC_RATIO]
    blk = jnp.arange(n_slc)[None, :]
    cur = (t_pos // SLC_BLOCK)[:, None]
    forced = (blk == 0) | (blk == cur) | (blk == cur - 1)
    score = jnp.where(forced, FORCE, jnp.where(blk <= cur, imp, -FORCE))
    n_sel = min(SLC_TOPK, n_slc)
    _, idx = lax.top_k(score, n_sel)
    sel_valid = idx <= cur

    nq = s // SLC_BLOCK
    k_blocks = rmsnorm(k_s, k_norm_g).reshape(b, n_slc, SLC_BLOCK, G, dh).transpose(0, 3, 1, 2, 4)
    v_blocks = v_s.reshape(b, n_slc, SLC_BLOCK, G, dh).transpose(0, 3, 1, 2, 4)
    gather = jax.vmap(jax.vmap(lambda blocks, ix: blocks[ix]))
    gi = jnp.arange(G).reshape(1, G, 1, 1, 1, 1)
    ri = jnp.arange(R).reshape(1, 1, R, 1, 1, 1)

    def slc_block(args):
        q_b, idx_b, val_b, t_b = args
        k_sel = gather(k_blocks, idx_b)
        v_sel = gather(v_blocks, idx_b)
        kpos = idx_b[..., None] * SLC_BLOCK + jnp.arange(SLC_BLOCK)
        dist = t_b[:, None, None] - kpos
        mask = (val_b[..., None] & (dist >= 0))[:, :, None]
        bias = bias_tab[t5_bucket(dist)[:, :, None], gi, ri]
        sc = jnp.einsum('bcgrd,bgcnld->bgrcnl', q_b, k_sel).astype(jnp.float32) + bias
        p = masked_softmax(sc, mask, axis=(-2, -1))
        return jnp.einsum('bgrcnl,bgcnld->bcgrd', p, v_sel)

    q_ch = jnp.moveaxis(q.reshape(b, nq, SLC_BLOCK, G, R, dh), 1, 0)
    idx_ch = jnp.moveaxis(idx.reshape(b, G, nq, SLC_BLOCK, n_sel), 2, 0)
    val_ch = jnp.moveaxis(sel_valid.reshape(b, G, nq, SLC_BLOCK, n_sel), 2, 0)
    t_ch = t_pos.reshape(nq, SLC_BLOCK)
    o_slc = jnp.moveaxis(lax.map(slc_block, (q_ch, idx_ch, val_ch, t_ch)), 0, 1).reshape(b, s, G, R, dh)

    nw = s // WIN_QBLOCK
    k_pad = jnp.pad(rmsnorm(k_w, k_norm_g), ((0, 0), (WINDOW, 0), (0, 0), (0, 0)))
    v_pad = jnp.pad(v_w, ((0, 0), (WINDOW, 0), (0, 0), (0, 0)))

    def win_block(args):
        q_b, i = args
        start = i * WIN_QBLOCK
        kw = lax.dynamic_slice_in_dim(k_pad, start, WIN_QBLOCK + WINDOW, axis=1)
        vw = lax.dynamic_slice_in_dim(v_pad, start, WIN_QBLOCK + WINDOW, axis=1)
        t_b = start + jnp.arange(WIN_QBLOCK)
        s_b = start - WINDOW + jnp.arange(WIN_QBLOCK + WINDOW)
        dist = t_b[:, None] - s_b[None, :]
        mask = (dist >= 0) & (dist < WINDOW) & (s_b[None, :] >= 0)
        bias = bias_tab[t5_bucket(dist)].transpose(2, 3, 0, 1)
        sc = jnp.einsum('bqgrd,bkgd->bgrqk', q_b, kw).astype(jnp.float32) + bias
        p = masked_softmax(sc, mask, axis=-1)
        return jnp.einsum('bgrqk,bkgd->bqgrd', p, vw)

    q_wch = jnp.moveaxis(q.reshape(b, nw, WIN_QBLOCK, G, R, dh), 1, 0)
    o_win = jnp.moveaxis(lax.map(win_block, (q_wch, jnp.arange(nw))), 0, 1).reshape(b, s, G, R, dh)

    gt = jax.nn.sigmoid(gate.reshape(b, s, G, R, 3).astype(jnp.float32))
    o = gt[..., 0:1] * o_cmp + gt[..., 1:2] * o_slc + gt[..., 2:3] * o_win
    return o.reshape(b, s, NSA_WIDTH)

def rwkv7_mixer(p_in, mu, w0, w2, a0, a2, g2, k_k, k_a, r_k, ln_g, ln_b):
    b, s, _ = p_in.shape
    H, N = RWKV_HEADS, HEAD_DIM
    shifted = jnp.pad(p_in, ((0, 0), (1, 0), (0, 0)))[:, :-1]
    xl = p_in + (shifted - p_in) * mu
    r, k, v, xw, xa, xg = jnp.split(xl, RWKV_SPLITS, axis=-1)
    w = -jax.nn.softplus(-(w0 + jnp.tanh(xw) @ w2)) - 0.5
    decay = jnp.exp(-jnp.exp(w.astype(jnp.float32)))
    a = jax.nn.sigmoid(a0 + xa @ a2)
    g = jax.nn.sigmoid(xg) @ g2
    heads = lambda t: t.reshape(b, s, H, N).astype(jnp.float32)
    r, k, v, a, decay = heads(r), heads(k), heads(v), heads(a), heads(decay)
    kk = k * k_k.reshape(H, N).astype(jnp.float32)
    kk = kk / jnp.maximum(jnp.sqrt(jnp.sum(kk * kk, axis=-1, keepdims=True)), 1e-12)
    k = k * (1.0 + (a - 1.0) * k_a.reshape(H, N).astype(jnp.float32))
    xs = tuple(jnp.moveaxis(t, 1, 0) for t in (r, decay, k, v, -kk, kk * a))

    def step(state, inp):
        r_t, w_t, k_t, v_t, a_t, b_t = inp
        sa = jnp.einsum('bhij,bhj->bhi', state, a_t)
        state = state * w_t[:, :, None, :] + sa[..., None] * b_t[:, :, None, :] + v_t[..., None] * k_t[:, :, None, :]
        return state, jnp.einsum('bhij,bhj->bhi', state, r_t)

    state0 = jnp.zeros((b, H, N, N), jnp.float32)
    _, y = lax.scan(step, state0, xs)
    y = jnp.moveaxis(y, 0, 1)
    mean = jnp.mean(y, axis=-1, keepdims=True)
    var = jnp.mean(jnp.square(y - mean), axis=-1, keepdims=True)
    y = (y - mean) * lax.rsqrt(var + GN_EPS) * ln_g.reshape(H, N) + ln_b.reshape(H, N)
    y = y + jnp.sum(r * k * r_k, axis=-1, keepdims=True) * v
    return y.reshape(b, s, RWKV_WIDTH) * g

def conv_ffn(h, w_up, conv_w, conv_b, w_down):
    u = h @ w_up
    s = u.shape[1]
    up = jnp.pad(u, ((0, 0), (CONV_WIDTH - 1, 0), (0, 0)))
    c = conv_b + conv_w[0] * up[:, 0:s]
    for j in range(1, CONV_WIDTH):
        c = c + conv_w[j] * up[:, j:j + s]
    val, gate = jnp.split(c, 2, axis=-1)
    return (jax.nn.silu(gate) * val) @ w_down

def first_inputs(seed: int = 0) -> dict:
    key = jax.random.key(seed)
    ks = iter(jax.random.split(key, 40))
    L, D = DEPTH, D_MODEL

    def nrm(shape, scale):
        return scale * jax.random.normal(next(ks), shape, jnp.float32)

    def unif(shape, lo, hi):
        return jax.random.uniform(next(ks), shape, jnp.float32, lo, hi)

    return {
        'x': nrm((BATCH, SEQ, D), 1.0),
        'attn_norm_g': 1.0 + nrm((L, D), 0.1),
        'w_in': nrm((L, D, IN_WIDTH), D ** -0.5),
        'rel_bias': nrm((REL_BUCKETS, NSA_HEADS), 0.5),
        'q_norm_g': 1.0 + nrm((L, HEAD_DIM), 0.1),
        'k_norm_g': 1.0 + nrm((L, HEAD_DIM), 0.1),
        'cmp_pe_k': nrm((L, CMP_BLOCK, HEAD_DIM), 0.1),
        'cmp_w1_k': nrm((L, CMP_BLOCK * HEAD_DIM, CMP_HIDDEN), (CMP_BLOCK * HEAD_DIM) ** -0.5),
        'cmp_w2_k': nrm((L, CMP_HIDDEN, HEAD_DIM), CMP_HIDDEN ** -0.5),
        'cmp_pe_v': nrm((L, CMP_BLOCK, HEAD_DIM), 0.1),
        'cmp_w1_v': nrm((L, CMP_BLOCK * HEAD_DIM, CMP_HIDDEN), (CMP_BLOCK * HEAD_DIM) ** -0.5),
        'cmp_w2_v': nrm((L, CMP_HIDDEN, HEAD_DIM), CMP_HIDDEN ** -0.5),
        'rwkv_mu': unif((L, RWKV_IN_WIDTH), 0.0, 1.0),
        'rwkv_w0': unif((L, RWKV_WIDTH), -6.0, -1.0),
        'rwkv_w2': nrm((L, LORA_W, RWKV_WIDTH), 0.5 * LORA_W ** -0.5),
        'rwkv_a0': nrm((L, RWKV_WIDTH), 0.1),
        'rwkv_a2': nrm((L, LORA_A, RWKV_WIDTH), 0.5 * LORA_A ** -0.5),
        'rwkv_g2': nrm((L, LORA_G, RWKV_WIDTH), LORA_G ** -0.5),
        'rwkv_k_k': 0.85 + nrm((L, RWKV_WIDTH), 0.05),
        'rwkv_k_a': 1.0 + nrm((L, RWKV_WIDTH), 0.05),
        'rwkv_r_k': nrm((L, RWKV_HEADS, HEAD_DIM), 0.1),
        'rwkv_ln_g': 1.0 + nrm((L, RWKV_WIDTH), 0.1),
        'rwkv_ln_b': nrm((L, RWKV_WIDTH), 0.01),
        'w_proj_a': nrm((L, NSA_WIDTH, D), NSA_WIDTH ** -0.5),
        'w_proj_b': nrm((L, RWKV_WIDTH, D), RWKV_WIDTH ** -0.5),
        'w_out': nrm((L, D, D), D ** -0.5),
        'ffn_norm_g': 1.0 + nrm((L, D), 0.1),
        'w_up': nrm((L, D, 2 * D_FF), D ** -0.5),
        'conv_w': nrm((L, CONV_WIDTH, 2 * D_FF), CONV_WIDTH ** -0.5),
        'conv_b': nrm((L, 2 * D_FF), 0.01),
        'w_down': nrm((L, D_FF, D), D_FF ** -0.5),
    }

def first_block(x, attn_norm_g, w_in, rel_bias, q_norm_g, k_norm_g, cmp_pe_k, cmp_w1_k, cmp_w2_k,
              cmp_pe_v, cmp_w1_v, cmp_w2_v, rwkv_mu, rwkv_w0, rwkv_w2, rwkv_a0, rwkv_a2, rwkv_g2,
              rwkv_k_k, rwkv_k_a, rwkv_r_k, rwkv_ln_g, rwkv_ln_b, w_proj_a, w_proj_b, w_out,
              ffn_norm_g, w_up, conv_w, conv_b, w_down):
    for l in range(DEPTH):
        h = rmsnorm(x, attn_norm_g[l])
        proj = h @ w_in[l]
        q, k_c, v_c, k_s, v_s, k_w, v_w, nsa_gate, rwkv_in, gate_a, gate_b = jnp.split(proj, IN_SPLITS, axis=-1)
        o_a = nsa_mixer(q, k_c, v_c, k_s, v_s, k_w, v_w, nsa_gate, rel_bias, q_norm_g[l], k_norm_g[l],
                        cmp_pe_k[l], cmp_w1_k[l], cmp_w2_k[l], cmp_pe_v[l], cmp_w1_v[l], cmp_w2_v[l])
        o_b = rwkv7_mixer(rwkv_in, rwkv_mu[l], rwkv_w0[l], rwkv_w2[l], rwkv_a0[l], rwkv_a2[l], rwkv_g2[l],
                          rwkv_k_k[l], rwkv_k_a[l], rwkv_r_k[l], rwkv_ln_g[l], rwkv_ln_b[l])
        merged = jax.nn.sigmoid(gate_a) * (o_a @ w_proj_a[l]) + jax.nn.sigmoid(gate_b) * (o_b @ w_proj_b[l])
        x = x + (merged @ w_out[l]).astype(x.dtype)
        h2 = rmsnorm(x, ffn_norm_g[l])
        x = x + conv_ffn(h2, w_up[l], conv_w[l], conv_b[l], w_down[l]).astype(x.dtype)
    return x


A_HEADS = 8
A_HEAD_DIM = 64
A_WIDTH = A_HEADS * A_HEAD_DIM
IDX_HEADS = 8
IDX_DIM = 32
INDEX_TOPK = 256
SPARSE_Q_BLOCK = 64
N_BUCKETS = 32
MAX_DISTANCE = 128

B_HEADS = 4
B_KEY_DIM = 64
B_VAL_DIM = 128
B_KEY_WIDTH = B_HEADS * B_KEY_DIM
B_WIDTH = B_HEADS * B_VAL_DIM
GATE_RANK = 16
GATE_TEMP = 16.0
GLA_CHUNK = 64

MIX_WIDTH = A_WIDTH + B_WIDTH

PROJ_SPLITS = (A_WIDTH, A_WIDTH, A_WIDTH,
               IDX_HEADS * IDX_DIM, IDX_DIM, IDX_HEADS,
               B_KEY_WIDTH, B_KEY_WIDTH, B_WIDTH,
               GATE_RANK, B_WIDTH)
PROJ_WIDTH = 3 * A_WIDTH + IDX_HEADS * IDX_DIM + IDX_DIM + IDX_HEADS + 2 * B_KEY_WIDTH + B_WIDTH + GATE_RANK + B_WIDTH

N_GROUPS = 4
EXPERTS_PER_GROUP = 8
N_EXPERTS = N_GROUPS * EXPERTS_PER_GROUP
EXPERT_TOPK = 2
D_EXPERT = 256

EPS = 1e-6


def rmsnorm_2(x, g):
    xf = x.astype(jnp.float32)
    y = xf * lax.rsqrt(jnp.mean(xf * xf, axis=-1, keepdims=True) + EPS)
    return (y * g.astype(jnp.float32)).astype(x.dtype)

def t5_bucket_2(dist):
    max_exact = N_BUCKETS // 2
    d_f = jnp.maximum(dist, 1).astype(jnp.float32)
    large = max_exact + (jnp.log(d_f / max_exact) / math.log(MAX_DISTANCE / max_exact)
                         * (N_BUCKETS - max_exact)).astype(jnp.int32)
    large = jnp.minimum(large, N_BUCKETS - 1)
    return jnp.where(dist < max_exact, dist, large)

def dsa_attention(q, k, v, iq, ik, iw, rel_bias):
    bsz, s_len = q.shape[0], q.shape[1]
    topk = min(INDEX_TOPK, s_len // 4)
    nb = s_len // SPARSE_Q_BLOCK

    def blocks(a):
        return a.reshape(bsz, nb, SPARSE_Q_BLOCK, *a.shape[2:]).swapaxes(0, 1)

    q_pos = jnp.arange(s_len, dtype=jnp.int32).reshape(nb, SPARSE_Q_BLOCK)
    key_pos = jnp.arange(s_len, dtype=jnp.int32)
    ik_f = ik.astype(jnp.float32)
    gather = jax.vmap(lambda a, i: a[i])

    def one_block(args):
        qb, iqb, iwb, tb = args
        idx_logits = jnp.einsum('bqhd,bsd->bqhs', iqb.astype(jnp.float32), ik_f) * IDX_DIM ** -0.5
        score = jnp.einsum('bqhs,bqh->bqs', jax.nn.relu(idx_logits),
                           iwb.astype(jnp.float32) * IDX_HEADS ** -0.5)
        causal = key_pos[None, :] <= tb[:, None]
        score = jnp.where(causal[None], score, -jnp.inf)
        _, idx = lax.top_k(score, topk)
        valid = idx <= tb[None, :, None]
        k_sel = gather(k, idx)
        v_sel = gather(v, idx)
        logits = jnp.einsum('bqhd,bqkhd->bhqk', qb, k_sel).astype(jnp.float32) * A_HEAD_DIM ** -0.5
        dist = jnp.maximum(tb[None, :, None] - idx, 0)
        bias = rel_bias[t5_bucket_2(dist)]
        logits = logits + jnp.transpose(bias, (0, 3, 1, 2)).astype(jnp.float32)
        logits = jnp.where(valid[:, None], logits, -jnp.inf)
        p = jax.nn.softmax(logits, axis=-1).astype(v.dtype)
        return jnp.einsum('bhqk,bqkhd->bqhd', p, v_sel)

    out = lax.map(one_block, (blocks(q), blocks(iq), blocks(iw), q_pos))
    return out.swapaxes(0, 1).reshape(bsz, s_len, A_HEADS * A_HEAD_DIM)

def gla_chunked(q, k, v, log_a):
    bsz, s_len, h, dk = q.shape
    dv = v.shape[-1]
    nc = s_len // GLA_CHUNK

    def chunks(a):
        return a.reshape(bsz, nc, GLA_CHUNK, h, a.shape[-1]).transpose(1, 0, 3, 2, 4)

    tri = jnp.tril(jnp.ones((GLA_CHUNK, GLA_CHUNK), dtype=bool))

    def step(state, inp):
        qc, kc, vc, gc = inp
        b = jnp.cumsum(gc, axis=2)
        o_inter = jnp.einsum('bhcd,bhdv->bhcv', qc * jnp.exp(b), state)
        diff = b[:, :, :, None, :] - b[:, :, None, :, :]
        decay = jnp.exp(jnp.where(tri[None, None, :, :, None], diff, -jnp.inf))
        attn = jnp.einsum('bhtd,bhsd,bhtsd->bhts', qc, kc, decay)
        o_intra = jnp.einsum('bhts,bhsv->bhtv', attn, vc)
        b_last = b[:, :, -1:, :]
        state = (jnp.exp(b_last[:, :, 0, :])[..., None] * state
                 + jnp.einsum('bhsd,bhsv->bhdv', kc * jnp.exp(b_last - b), vc))
        return state, o_inter + o_intra

    init = jnp.zeros((bsz, h, dk, dv), jnp.float32)
    _, o = lax.scan(step, init, (chunks(q * dk ** -0.5), chunks(k), chunks(v), chunks(log_a)))
    return o.transpose(1, 0, 3, 2, 4).reshape(bsz, s_len, h, dv)

def hier_moe(h, w_rg, b_rg, w_re, b_re, w_g, w_u, w_d):
    bsz, s_len, d = h.shape
    hf = h.reshape(-1, d)
    g_logits = (hf @ w_rg).astype(jnp.float32) + b_rg.astype(jnp.float32)
    g_prob = jax.nn.softmax(g_logits, axis=-1)
    _, g_sel = lax.top_k(g_logits, 1)
    g_onehot = jax.nn.one_hot(g_sel[:, 0], N_GROUPS, dtype=jnp.float32)
    g_weight = jnp.sum(g_prob * g_onehot, axis=-1, keepdims=True)
    e_logits = ((hf @ w_re).astype(jnp.float32) + b_re.astype(jnp.float32)).reshape(-1, N_GROUPS, EXPERTS_PER_GROUP)
    e_logits_sel = jnp.einsum('nge,ng->ne', e_logits, g_onehot)
    top_val, top_idx = lax.top_k(e_logits_sel, EXPERT_TOPK)
    e_weight = jax.nn.softmax(top_val, axis=-1) * g_weight
    e_idx = g_sel * EXPERTS_PER_GROUP + top_idx
    gates = jnp.sum(jax.nn.one_hot(e_idx, N_EXPERTS, dtype=jnp.float32) * e_weight[..., None], axis=1)
    out = jnp.zeros(hf.shape, jnp.float32)
    for g in range(N_GROUPS):
        sl = slice(g * EXPERTS_PER_GROUP, (g + 1) * EXPERTS_PER_GROUP)
        a = jnp.einsum('nd,edf->nef', hf, w_g[sl])
        u = jnp.einsum('nd,edf->nef', hf, w_u[sl])
        hid = jax.nn.silu(a) * u * gates[:, sl, None].astype(hf.dtype)
        out = out + jnp.einsum('nef,efd->nd', hid, w_d[sl]).astype(jnp.float32)
    return out.astype(h.dtype).reshape(bsz, s_len, d)

def second_inputs(seed: int = 0) -> dict:
    key = jax.random.key(seed)
    ks = jax.random.split(key, 20)
    f32 = jnp.float32
    nrm = lambda k, shape, scale: jax.random.normal(k, shape, f32) * scale
    return {
        "x": nrm(ks[0], (BATCH, SEQ, D_MODEL), 1.0),
        "norm1_g": 1.0 + nrm(ks[1], (DEPTH, D_MODEL), 0.01),
        "w_in": nrm(ks[2], (DEPTH, D_MODEL, PROJ_WIDTH), D_MODEL ** -0.5),
        "q_norm_g": 1.0 + nrm(ks[3], (DEPTH, A_HEAD_DIM), 0.01),
        "k_norm_g": 1.0 + nrm(ks[4], (DEPTH, A_HEAD_DIM), 0.01),
        "rel_bias": nrm(ks[5], (N_BUCKETS, A_HEADS), 0.5),
        "gla_gate_w2": nrm(ks[6], (DEPTH, GATE_RANK, B_KEY_WIDTH), GATE_RANK ** -0.5),
        "gla_gate_b": nrm(ks[7], (DEPTH, B_KEY_WIDTH), 0.1),
        "gla_out_norm_g": 1.0 + nrm(ks[8], (DEPTH, B_VAL_DIM), 0.01),
        "w_out": nrm(ks[9], (DEPTH, MIX_WIDTH, D_MODEL), MIX_WIDTH ** -0.5),
        "norm2_g": 1.0 + nrm(ks[10], (DEPTH, D_MODEL), 0.01),
        "w_router_group": nrm(ks[11], (DEPTH, D_MODEL, N_GROUPS), D_MODEL ** -0.5),
        "b_router_group": nrm(ks[12], (DEPTH, N_GROUPS), 0.01),
        "w_router_expert": nrm(ks[13], (DEPTH, D_MODEL, N_EXPERTS), D_MODEL ** -0.5),
        "b_router_expert": nrm(ks[14], (DEPTH, N_EXPERTS), 0.01),
        "w_exp_gate": nrm(ks[15], (DEPTH, N_EXPERTS, D_MODEL, D_EXPERT), D_MODEL ** -0.5),
        "w_exp_up": nrm(ks[16], (DEPTH, N_EXPERTS, D_MODEL, D_EXPERT), D_MODEL ** -0.5),
        "w_exp_down": nrm(ks[17], (DEPTH, N_EXPERTS, D_EXPERT, D_MODEL), D_EXPERT ** -0.5),
    }

def second_block(x, norm1_g, w_in, q_norm_g, k_norm_g, rel_bias, gla_gate_w2, gla_gate_b,
              gla_out_norm_g, w_out, norm2_g, w_router_group, b_router_group,
              w_router_expert, b_router_expert, w_exp_gate, w_exp_up, w_exp_down):
    bsz, s_len, _ = x.shape
    split_points = np.cumsum(PROJ_SPLITS)[:-1].tolist()
    for l in range(DEPTH):
        h = rmsnorm_2(x, norm1_g[l])
        proj = h @ w_in[l]
        qa, ka, va, iq, ik, iw, qb, kb, vb, g_lr, r_gate = jnp.split(proj, split_points, axis=-1)

        qa = rmsnorm_2(qa.reshape(bsz, s_len, A_HEADS, A_HEAD_DIM), q_norm_g[l])
        ka = rmsnorm_2(ka.reshape(bsz, s_len, A_HEADS, A_HEAD_DIM), k_norm_g[l])
        va = va.reshape(bsz, s_len, A_HEADS, A_HEAD_DIM)
        o_a = dsa_attention(qa, ka, va, iq.reshape(bsz, s_len, IDX_HEADS, IDX_DIM), ik, iw, rel_bias)

        log_a = jax.nn.log_sigmoid((g_lr @ gla_gate_w2[l]).astype(jnp.float32)
                                   + gla_gate_b[l].astype(jnp.float32)) / GATE_TEMP
        o_b = gla_chunked(qb.reshape(bsz, s_len, B_HEADS, B_KEY_DIM).astype(jnp.float32),
                          kb.reshape(bsz, s_len, B_HEADS, B_KEY_DIM).astype(jnp.float32),
                          vb.reshape(bsz, s_len, B_HEADS, B_VAL_DIM).astype(jnp.float32),
                          log_a.reshape(bsz, s_len, B_HEADS, B_KEY_DIM))
        o_b = rmsnorm_2(o_b, gla_out_norm_g[l]).reshape(bsz, s_len, B_WIDTH).astype(x.dtype) * jax.nn.silu(r_gate)

        x = x + jnp.concatenate([o_a, o_b], axis=-1) @ w_out[l]

        x = x + hier_moe(rmsnorm_2(x, norm2_g[l]), w_router_group[l], b_router_group[l],
                         w_router_expert[l], b_router_expert[l],
                         w_exp_gate[l], w_exp_up[l], w_exp_down[l])
    return x


def setup_inputs(seed=0):
    out = dict(first_inputs(seed))
    for name, value in second_inputs(seed + 1).items():
        if name != "x":
            out[name + "_2"] = value
    return out


def reference(
    x, attn_norm_g, w_in, rel_bias, q_norm_g, k_norm_g, cmp_pe_k, cmp_w1_k, cmp_w2_k, cmp_pe_v,
    cmp_w1_v, cmp_w2_v, rwkv_mu, rwkv_w0, rwkv_w2, rwkv_a0, rwkv_a2, rwkv_g2, rwkv_k_k,
    rwkv_k_a, rwkv_r_k, rwkv_ln_g, rwkv_ln_b, w_proj_a, w_proj_b, w_out, ffn_norm_g, w_up,
    conv_w, conv_b, w_down, norm1_g_2, w_in_2, q_norm_g_2, k_norm_g_2, rel_bias_2,
    gla_gate_w2_2, gla_gate_b_2, gla_out_norm_g_2, w_out_2, norm2_g_2, w_router_group_2,
    b_router_group_2, w_router_expert_2, b_router_expert_2, w_exp_gate_2, w_exp_up_2,
    w_exp_down_2,
):
    x = first_block(
        x, attn_norm_g, w_in, rel_bias, q_norm_g, k_norm_g, cmp_pe_k, cmp_w1_k, cmp_w2_k,
        cmp_pe_v, cmp_w1_v, cmp_w2_v, rwkv_mu, rwkv_w0, rwkv_w2, rwkv_a0, rwkv_a2, rwkv_g2,
        rwkv_k_k, rwkv_k_a, rwkv_r_k, rwkv_ln_g, rwkv_ln_b, w_proj_a, w_proj_b, w_out,
        ffn_norm_g, w_up, conv_w, conv_b, w_down,
    )
    return second_block(
        x, norm1_g_2, w_in_2, q_norm_g_2, k_norm_g_2, rel_bias_2, gla_gate_w2_2, gla_gate_b_2,
        gla_out_norm_g_2, w_out_2, norm2_g_2, w_router_group_2, b_router_group_2,
        w_router_expert_2, b_router_expert_2, w_exp_gate_2, w_exp_up_2, w_exp_down_2,
    )


_drawn_inputs = setup_inputs


def setup_inputs(seed=0):
    import zlib

    import numpy as np

    out = dict(_drawn_inputs(seed))
    spreads = {}
    factors = {'q_norm_g': 2.877,
     'cmp_pe_k': 3.638,
     'rwkv_w2': 3.032,
     'rwkv_ln_b': 5.189,
     'norm1_g_2': 3.024,
     'q_norm_g_2': 8.0,
     'k_norm_g_2': 8.0,
     'gla_out_norm_g_2': 6.266,
     'norm2_g_2': 3.37,
     'b_router_group_2': 8.0,
     'b_router_expert_2': 12.098}
    for name, (base, spread) in spreads.items():
        noise = np.random.default_rng([zlib.crc32(name.encode()), seed]).standard_normal(out[name].shape)
        drawn = base * np.exp(spread * noise) if base else spread * noise
        out[name] = jnp.asarray(drawn.astype(out[name].dtype))
    for name, factor in factors.items():
        out[name] = (out[name] * factor).astype(out[name].dtype)
    return out
```

```python
import math
from contextlib import ExitStack

import numpy as np

import concourse.bass as bass
from concourse import mybir

F32 = mybir.dt.float32
BF16 = mybir.dt.bfloat16
I32 = mybir.dt.int32
U32 = mybir.dt.uint32
ALU = mybir.AluOpType
ACT = mybir.ActivationFunctionType
AX = mybir.AxisListType.X

P = 128
S, D = 512, 1024
TT = S // P
KD = D // P
NEG = -1e30
TAKEN = -3e38
RMS_EPS = 1e-6

DH, NH, NG, NR = 64, 8, 2, 4
KVW = NG * DH
CB, CS, CHID = 32, 16, 256
NC = S // CS - CB // CS + 1
NW = NH * DH
COL_Q, COL_KC = 0, NW
COL_VC, COL_KS, COL_VS, COL_KW, COL_VW = (COL_KC + i * KVW for i in range(1, 6))
COL_GATE = COL_KC + 6 * KVW
COL_R = COL_GATE + 3 * NH
RW = 512
COL_K, COL_V, COL_LORA = COL_R + RW, COL_R + 2 * RW, COL_R + 3 * RW
COL_GA = COL_LORA + 256
COL_GB = COL_GA + D
DFF = 2816
FT = DFF // P
GN_EPS = 64e-5
DECAY = math.exp(-0.5)
NORM_FLOOR = 1e-24
LN_SHIFT = 20
IH, ID, TOPK = 8, 32, 128
COL2_Q, COL2_K, COL2_V, COL2_IQ = 0, 512, 1024, 1536
COL2_IK = COL2_IQ + IH * ID
COL2_IW = COL2_IK + ID
COL2_QB = COL2_IW + IH
COL2_KB = COL2_QB + 256
COL2_VB = COL2_KB + 256
COL2_LR = COL2_VB + 512
COL2_RG = COL2_LR + 16
BH, BK, BV, RANK, TEMP, GC = 4, 64, 128, 16, 16.0, 64
XG, XE, NE, DE = 4, 8, 32, 256
NTILE = 2 * S // P + NE - 1


def t5_bucket(n):
    large = 16 + (np.log(np.maximum(n, 1).astype(np.float32) / np.float32(16)) / np.float32(math.log(8))
                  * np.float32(16)).astype(np.int32)
    return np.where(n < 16, n, np.minimum(large, 31))


def level_mask(m):
    i = np.arange(P)
    return ((i[:, None] // (2 * m) == i[None, :] // (2 * m))
            & (i[:, None] // m % 2 == 1) & (i[None, :] // m % 2 == 0)).astype(np.float32)


def constants():
    i = np.arange(P)
    parts = {}
    parts["ident"] = np.eye(P)
    parts["ones64"] = (i[:, None] // 64 == i[None, :] // 64) * 1.0
    parts["allones"] = np.ones((P, P))
    parts["before"] = (i[:, None] < i[None, :]) * 1.0
    strict, upto = (i[:, None] < i[None, :]) * 1.0, (i[:, None] <= i[None, :]) * 1.0
    parts["mask_rw"] = np.concatenate([strict, upto, strict, upto], 1)
    parts["mask_low4"] = np.tile(strict.T, (1, 4))
    same = i[:, None] // GC == i[None, :] // GC
    parts["mask_gla"] = np.tile(upto * same, (1, 4))
    parts["lev0u"] = level_mask(1).T
    for lv in range(7):
        parts[f"lev{lv}"] = level_mask(1 << lv)
    parts["valid_c"] = np.stack([(i + P * t >= CB - 1) * 1.0 for t in range(TT)], 1)
    parts["iota"] = np.tile(np.arange(XE * 1.0), (P, 1))
    parts["tile_no"] = np.tile(np.arange(NTILE * 1.0), (P, 1))
    parts["token_no"] = i[:, None] + P * np.arange(TT)[None, :] * 1.0
    parts["eps"] = np.full((P, 1), RMS_EPS)
    parts["gn_eps"] = np.full((P, 1), GN_EPS)
    parts["ln_back"] = np.full((P, 1), 0.5 * LN_SHIFT * math.log(2.0))
    where, at = {}, 0
    for k, v in parts.items():
        where[k] = (at, at + v.shape[1])
        at += v.shape[1]
    return np.concatenate(list(parts.values()), 1).astype(np.float32), where


def distance_tables():
    def one_hot(n):
        t = np.zeros((33, n.size), np.float32)
        t[t5_bucket(np.maximum(n, 0)), np.arange(n.size)] = n >= 0
        t[32] = np.where(n < 0, np.float32(NEG), 0)
        return t
    return np.concatenate([one_hot(np.arange(1024) - 511), one_hot(np.arange(640) - 127)], 1)


class Lane:

    def __init__(self, sem, one_at_a_time=False):
        self.sem, self.count, self.queue, self.seen = sem, 0, [], {}
        self.one_at_a_time = one_at_a_time

    def wait(self, *tokens):
        for t in tokens:
            if t is None:
                continue
            if isinstance(t, list):
                self.wait(*t)
                continue
            sem, value = t
            if self.seen.get(id(sem), 0) < value:
                self.seen[id(sem)] = value
                self.queue.append(lambda eng, s=sem, v=value: eng.wait_ge(s, v))

    def do(self, make, *after, signal=True):
        self.wait(*after)
        if self.one_at_a_time:
            self.wait(self.last())
        if not signal:
            self.queue.append(make)
            return None
        self.count += 1
        self.queue.append(lambda eng, m=make, s=self.sem: m(eng).then_inc(s, 1))
        return (self.sem, self.count)

    def last(self):
        return (self.sem, self.count) if self.count else None

    def run(self, eng):
        for f in self.queue:
            f(eng)


class Channel:

    def __init__(self, sem):
        self.sem, self.count = sem, 0

    def dma(self, lane, out, in_, *after, slow=False):
        lane.wait(*after)
        self.count += 16
        lane.queue.append(lambda eng, s=self.sem: eng.dma_start(
            out, in_, allow_slow_non_contiguous=slow).then_inc(s, 16))
        return (self.sem, self.count)


class Slot:
    def __init__(self, t, channel=None):
        self.t, self.channel, self.free = t, channel, []


class Ring:

    def __init__(self, slots):
        self.slots, self.n = slots, 0

    def take(self):
        s = self.slots[self.n % len(self.slots)]
        self.n += 1
        return s


class Core:

    def __init__(self, nc, ctx, w):
        self.nc, self.ctx, self.w = nc, ctx, w
        self.names = {}
        self.pe, self.act, self.dve, self.pool, self.sp = (
            Lane(self.sem(f"done_{n}"), one_at_a_time=(n == "pool")) for n in ("pe", "act", "dve", "pool", "sp"))
        self.stores = []
        self.more_channel = self.channel("in_w_more")

    def fresh(self, name):
        self.names[name] = self.names.get(name, 0) + 1
        return name if self.names[name] == 1 else f"{name}_{self.names[name]}"

    def sem(self, name):
        name = self.fresh("sem " + name).replace("sem ", "")
        return self.ctx.enter_context(self.nc.semaphore(name))

    def channel(self, name):
        return Channel(self.sem(name))

    def sb(self, ctx, name, shape, dt=F32):
        name = self.fresh(name)
        return ctx.enter_context(self.nc.sbuf_tensor(name, shape, dt))

    def ring(self, ctx, name, n, shape, dt=F32, channels=False):
        return Ring([Slot(self.sb(ctx, f"{name}{i}", shape, dt),
                          self.channel(f"in_{name}{i}") if channels else None) for i in range(n)])

    def mm(self, out, lhsT, rhs, *after, start=True, stop=True, signal=True, loose=False):
        return self.pe.do(lambda e: e.matmul(out, lhsT, rhs, start=start, stop=stop, skip_group_check=loose),
                          *after, signal=signal)

    def tr(self, out, in_, *after, signal=True):
        n = in_.shape[0]
        return self.pe.do(lambda e: e.transpose(out, in_, self.c("ident")[0:n, 0:n]), *after, signal=signal)

    def a(self, out, in_, func, *after, bias=None, scale=None, accum=None):
        kw = {k: v for k, v in (("bias", bias), ("scale", scale), ("accum_out", accum)) if v is not None}
        return self.act.do(lambda e: e.activation(out, in_, func, **kw), *after)

    def tt(self, out, x, y, op, *after, lane=None):
        return (lane or self.dve).do(lambda e: e.tensor_tensor(out, x, y, op), *after)

    def ts(self, out, x, s1, op0, *after, s2=None, op1=None, lane=None):
        if op1 is None:
            return (lane or self.dve).do(lambda e: e.tensor_scalar(out, x, s1, None, op0), *after)
        return (lane or self.dve).do(lambda e: e.tensor_scalar(out, x, s1, s2, op0, op1), *after)

    def stt(self, out, x, s, y, op0, op1, *after):
        return self.dve.do(lambda e: e.scalar_tensor_tensor(out=out, in0=x, scalar=s, in1=y, op0=op0, op1=op1),
                           *after)

    def cp(self, out, x, *after, lane=None):
        return (lane or self.dve).do(lambda e: e.tensor_copy(out, x), *after)

    def red(self, out, x, op, *after):
        return self.dve.do(lambda e: e.tensor_reduce(out, x, AX, op), *after)

    def recip(self, out, x, *after):
        return self.dve.do(lambda e: e.reciprocal(out, x), *after)

    def zero(self, out, *after, lane=None, value=0.0):
        return (lane or self.pool).do(lambda e: e.memset(out, value), *after)

    def c(self, name):
        lo, hi = self.where[name]
        return self.consts[:, lo:hi]

    def store(self, out, in_, *after, lane=None, channel=None):
        ch = channel or self.channel(f"store{len(self.stores)}")
        t = ch.dma(lane or self.sp, out, in_, *after)
        self.stores.append(t)
        return t

    def meet(self):
        tokens = [x.last() for x in (self.pe, self.act, self.dve, self.pool)]
        for lane in (self.pe, self.act, self.dve, self.pool):
            lane.wait([t for t in tokens if t])
        self.met = tokens

    def load_distances(self, ctx):
        self.dist = self.sb(ctx, "dist", list(self.dist_dram.shape))
        self.dist_ready = self.channel("dist_in").dma(self.act, self.dist[:, :], self.dist_dram, self.dve.last())

    def more_weights(self, ctx):
        s = Slot(self.sb(ctx, "w_more", [P, 8 * 512]), self.more_channel)
        s.free = [t for t in self.met if t]
        ring, base = self.wring, list(self.wring.slots)
        at = ring.n % len(base)
        self.wring = Ring(base[at:] + base[:at] + [s])
        ctx.callback(self.fewer_weights)

    def fewer_weights(self):
        ring = self.wring
        at = ring.n % 4
        order = ring.slots[at:] + ring.slots[:at]
        self.wring = Ring([s for s in order if s.channel is not self.more_channel])

    def load(self, slot, parts, *after):
        for out, in_ in parts:
            t = slot.channel.dma(self.sp, out, in_, slot.free, *after)
        slot.free = []
        return t

    def weights(self, src, at, n, ktiles=KD):
        s = self.wring.take()
        v = s.t[:, 0:ktiles * n].rearrange("p (k n) -> p k n", k=ktiles)
        return s, v, self.load(s, [(v, src.rearrange("(k p) n -> p k n", p=P)[:, :, at:at + n])])

    def project(self, bank, out, lhs, rhs, n, *after):
        for k in range(n):
            t = self.mm(out, lhs(k), rhs(k), *((bank.free,) + after if k == 0 else ()),
                        start=(k == 0), stop=(k == n - 1), signal=(k == n - 1))
        bank.free = []
        return t

    def norm_to_fm(self, ctx, name, x, gain, gain_ready, ready, hT, hT_free, keep=None):
        junk = self.ring(ctx, f"{name}_h", 2, [P, D])
        st = self.sb(ctx, f"{name}_st", [P, 4 * TT])
        done = []
        for t in range(TT):
            s = junk.take()
            ss, ms, rc, rs = (st[:, 4 * t + j:4 * t + j + 1] for j in range(4))
            k = self.a(s.t[:, :], x[:, t, :], ACT.Square, ready[t], s.free, accum=ss)
            k = self.ts(ms, ss, 1.0 / D, ALU.mult, k, s2=RMS_EPS, op1=ALU.add)
            k = self.recip(rc, ms, k)
            k = self.a(rs, rc, ACT.Sqrt, k)
            k = self.stt(s.t[:, :], x[:, t, :], rs, gain, ALU.mult, ALU.mult, k, gain_ready)
            s.free = []
            if keep:
                s.free.append(self.store(keep[t * P:(t + 1) * P, :], s.t[:, :], k))
            for half in range(2):
                b = self.banks.take()
                for j in range(4):
                    f = half * 4 + j
                    m = self.tr(b.t[:, j * P:(j + 1) * P], s.t[:, f * P:(f + 1) * P], k,
                                b.free if j == 0 else None, signal=(j == 3))
                e = self.cp(hT[:, half * 4:half * 4 + 4, t * P:(t + 1) * P],
                            b.t[:, :].rearrange("p (k n) -> p k n", k=4), m, hT_free)
                b.free = [e]
                done.append(e)
            s.free.append(m)
        return done

    def to_fm(self, o, o_ready, oT):
        for f in range(4):
            b = self.banks.take()
            for t in range(TT):
                m = self.tr(b.t[:, t * P:(t + 1) * P], o[:, t, f * P:(f + 1) * P], o_ready[t], b.free,
                            signal=(t == TT - 1))
            k = self.a(oT[:, f, :], b.t[:, :], ACT.Copy, m)
            b.free = [k]
        return k

    def head_norm(self, tmp, bank, got, out, gain, n=S):
        raw, sq, e = tmp.take(), tmp.take(), tmp.take()
        k0 = self.cp(raw.t[:, 0:n], bank.t[:, 0:n], got, raw.free)
        k1 = self.a(sq.t[:, 0:n], raw.t[:, 0:n], ACT.Square, k0, sq.free)
        bank.free = [k0]
        b = self.banks.take()
        m = self.mm(b.t[:, 0:n], self.c("ones64"), sq.t[:, 0:n], k1, b.free)
        sq.free = [m]
        k = self.a(e.t[:, 0:n], b.t[:, 0:n], ACT.Ln, m, e.free, scale=1.0 / DH, bias=self.c("eps"))
        b.free = [k]
        k = self.a(e.t[:, 0:n], e.t[:, 0:n], ACT.Exp, k, scale=-0.5)
        k = self.stt(out, raw.t[:, 0:n], gain, e.t[:, 0:n], ALU.mult, ALU.mult, k, k0)
        raw.free = e.free = [k]
        return k

    def bias_table(self, ctx, name, rel_bias, big, relb_tile):
        ch = self.channel(f"{name}_relb")
        z = self.zero(relb_tile[32:33, :], value=1.0)
        r = ch.dma(self.act, relb_tile[0:32, :], rel_bias)
        row = self.sb(ctx, f"{name}_row", [NH, 640])
        for lo, hi in ((0, 512), (512, 640)):
            b = self.banks.take()
            m = self.mm(b.t[0:NH, 0:hi - lo], relb_tile[:, :], self.dist[:, 1024 + lo:1024 + hi],
                        b.free, r, z, self.dist_ready)
            k = self.cp(row[:, lo:hi], b.t[0:NH, 0:hi - lo], m)
            b.free = [k]
        dram = self.nc.dram_tensor(f"{name}_dram", (NH, 640), F32, kind="Internal").ap()
        k = self.store(dram, row[:, :], k)
        skew = bass.AP(tensor=dram.tensor, offset=0, ap=[[1, P], [640, NH], [1, 512]])
        return self.channel(f"{name}_skew").dma(self.sp, big[:, :, :], skew, k), [r, z]

    def attention(self, ctx, name, q, kk, v, width, big, ready, finish, extra=None):
        sc, pr, pt = (self.ring(ctx, f"{name}_{x}", 3, [P, S]) for x in ("s", "p", "t"))
        st = self.sb(ctx, f"{name}_stat", [P, TT, 2, NH])
        ring_s, ring_t, ring_o = (Ring([self.banks.slots[j] for j in js]) for js in ((0, 1, 2), (3, 4, 5), (6, 7)))
        units = [(i, h) for i in range(TT) for h in range(NH)]
        probs, turned, outs, sums = {}, {}, {}, {}

        def score(i, h):
            n = (i + 1) * P
            b, s, p = ring_s.take(), sc.take(), pr.take()
            got = self.mm(b.t[:, 0:n], q(h)[:, i * P:(i + 1) * P], kk(h)[:, 0:n], b.free, ready,
                          start=True, stop=not extra or i == 0)
            if extra and i:
                got = extra(i, b.t[:, 0:n])
            low = st[:, i, 0, h:h + 1]
            k = self.dve.do(lambda e: e.tensor_tensor_reduce(
                out=s.t[:, 0:n], in0=b.t[:, 0:n], in1=reversed_(big[:, h, 0:n]), scale=-1.0, scalar=3e38,
                op0=ALU.add, op1=ALU.min, accum_out=low), got, s.free)
            b.free = [k]
            k = self.a(p.t[:, 0:n], s.t[:, 0:n], ACT.Exp, k, p.free, scale=-1.0, bias=low,
                       accum=st[:, i, 1, h:h + 1])
            s.free = [k]
            sums[i] = k
            probs[i, h] = (p, k)

        def turn(i, h):
            n = (i + 1) * P
            p, k = probs.pop((i, h))
            b, w = ring_t.take(), pt.take()
            for j in range(i + 1):
                m = self.tr(b.t[:, j * P:(j + 1) * P], p.t[:, j * P:(j + 1) * P], k, b.free, signal=(j == i))
            p.free = [m]
            if h % 2:
                k = self.a(w.t[:, 0:n], b.t[:, 0:n], ACT.Copy, m, w.free)
            else:
                k = self.cp(w.t[:, 0:n], b.t[:, 0:n], m, w.free)
            b.free = [k]
            turned[i, h] = (w, k)

        def combine(i, h):
            w, k = turned.pop((i, h))
            if h == 0:
                outs[i] = ring_o.take()
            b = outs[i]
            for j in range(i + 1):
                m = self.mm(b.t[:, h * DH:(h + 1) * DH], w.t[:, j * P:(j + 1) * P], v(h, j), k, b.free,
                            start=(j == 0), stop=(j == i), signal=(j == i))
            b.free = []
            w.free = [m]
            if h == NH - 1:
                b.free = [finish(i, b, m, st[:, i, 1, :], sums[i])]

        for n in range(len(units) + 3):
            if n < len(units):
                score(*units[n])
            if 0 <= n - 2 < len(units):
                turn(*units[n - 2])
            if 0 <= n - 3 < len(units):
                combine(*units[n - 3])
        return sums


def spread(ap, m, axis=2):
    shape = list(ap.shape)
    return ap.unsqueeze(axis).broadcast_to(shape[:axis] + [m] + shape[axis:])


def reversed_(ap):
    (pstep, p), (step, n) = ap.ap
    return bass.AP(tensor=ap.tensor, offset=ap.offset + step * (n - 1), ap=[[pstep, p], [-step, n]])


def nsa(K, outer, hT, ready, oT, spare):
    w, c = K.w, K.c
    w_in = w["w_in"]
    sm = K.channel("nsa_small")
    ctx = ExitStack()
    qT = K.sb(outer, "qT", [P, NR, S])
    ksT, kwT = K.sb(outer, "ksT", [P, S]), K.sb(outer, "kwT", [P, S])
    vs, vw = K.sb(outer, "vs", [P, TT, KVW]), K.sb(outer, "vw", [P, TT, KVW])
    x2 = oT[:, :, :].rearrange("p (j g) t -> p j g t", j=2)
    gate = K.sb(outer, "nsa_gate", [P, TT, 3 * NH])
    big = K.sb(outer, "nsa_bias", [P, NH, 512])
    relb = K.sb(outer, "nsa_relb", [33, NH])
    raw = K.sb(ctx, "cmp_raw", [P, 2, S])
    o = spare
    tmp = K.ring(ctx, "nsa_tmp", 4, [P, S])
    gains = K.sb(ctx, "nsa_gains", [P, 2])
    pe_in = K.sb(ctx, "pe_in", [16, 2, P])
    peT = K.sb(ctx, "peT", [P, 2, 16])
    w2k, w2v = K.sb(ctx, "w2k", [P, 2, 2, DH]), K.sb(ctx, "w2v", [P, 2, DH])

    for half in range(2):
        for j, name in enumerate(("q_norm_g", "k_norm_g")):
            small = sm.dma(K.act, gains[half * DH:(half + 1) * DH, j:j + 1], w[name].rearrange("o d -> d o"), slow=True)
        small = sm.dma(K.act, w2k[:, :, half, :], w["cmp_w2_k"].rearrange("(k p) d -> p k d", p=P))
    small = sm.dma(K.act, w2v[:, :, :], w["cmp_w2_v"].rearrange("(k p) d -> p k d", p=P))
    for j, name in enumerate(("cmp_pe_k", "cmp_pe_v")):
        small = sm.dma(K.act, pe_in[:, j, :], w[name].rearrange("(m two) d -> m (two d)", two=2))
    K.load_distances(ctx)
    gq = K.ts(gains[:, 0:1], gains[:, 0:1], DH ** -0.5, ALU.mult, small)
    big_ready, relb_ready = K.bias_table(ctx, "nsa", w["rel_bias"], big, relb)

    s = K.wring.take()
    v = s.t[:, :].rearrange("p (k r g d) -> p k r g d", k=KD, r=NR, g=NG)
    src = w_in.rearrange("(k p) n -> p k n", p=P)
    got = K.load(s, [(v[:, :, r, g, :], src[:, :, COL_Q + (g * NR + r) * DH:COL_Q + (g * NR + r + 1) * DH])
                     for r in range(NR) for g in range(NG)])
    q_ready = []
    for r in range(NR):
        b = K.banks.take()
        m = K.project(b, b.t[:, :], lambda k: v[:, k, r, :, :].rearrange("p g d -> p (g d)"),
                      lambda k: hT[:, k, :], KD, got, ready)
        q_ready.append(K.head_norm(tmp, b, m, qT[:, r, :], gains[:, 0:1]))
    s.free = [m]

    s, v, got = K.weights(w_in, COL_KC, 512)
    raw_ready = []
    for j in range(2):
        b = K.banks.take()
        m = K.project(b, b.t[:, :], lambda k: v[:, k, j * P:(j + 1) * P], lambda k: hT[:, k, :], KD, got)
        e = K.a(raw[:, j, :], b.t[:, :], ACT.Copy, m)
        b.free = [e]
        raw_ready.append(e)
    b = K.banks.take()
    m = K.project(b, b.t[:, :], lambda k: v[:, k, 2 * P:3 * P], lambda k: hT[:, k, :], KD, got)
    ks_ready = K.head_norm(tmp, b, m, ksT[:, :], gains[:, 1:2])

    def values(dst, v, at):
        b = K.banks.take()
        for t in range(TT):
            m = K.project(b, b.t[:, t * P:(t + 1) * P], lambda k: hT[:, k, t * P:(t + 1) * P],
                          lambda k: v[:, k, at:at + P], KD)
        e = K.a(dst[:, :, :], b.t[:, :].rearrange("p (t n) -> p t n", t=TT), ACT.Copy, m)
        b.free = [e]
        return m, e

    m, vs_ready = values(vs, v, 3 * P)
    s.free = [m]

    sh = K.channel("cmp_shift")
    for j in range(2):
        for g in range(NG):
            src = raw[g * DH:(g + 1) * DH, j, :]
            shifted = sh.dma(K.sp, x2[0:DH, j, g, :], src, raw_ready[j])
            shifted = sh.dma(K.sp, x2[DH:P, j, g, 0:S - 1], src[:, 1:S])

    s, v, got = K.weights(w_in, COL_KW, 2 * KVW + 3 * NH)
    b = K.banks.take()
    m = K.project(b, b.t[:, :], lambda k: v[:, k, 0:P], lambda k: hT[:, k, :], KD, got)
    kw_ready = K.head_norm(tmp, b, m, kwT[:, :], gains[:, 1:2])
    m, vw_ready = values(vw, v, P)
    b = K.banks.take()
    for t in range(TT):
        m = K.project(b, b.t[:, t * 24:(t + 1) * 24], lambda k: hT[:, k, t * P:(t + 1) * P],
                      lambda k: v[:, k, 2 * P:2 * P + 24], KD)
    s.free = [m]
    gate_ready = K.a(gate[:, :, :], b.t[:, 0:96].rearrange("p (t n) -> p t n", t=TT), ACT.Sigmoid, m)
    b.free = [gate_ready]

    NB = NG * NC
    hid = K.sb(ctx, "cmp_hid", [P, 5, 4, NB])
    peh = K.sb(ctx, "cmp_peh", [P, 4])
    b = K.banks.take()
    for j in range(2):
        m = K.tr(b.t[:, j * 16:(j + 1) * 16], pe_in[:, j, :], small, b.free, K.consts_ready)
    b.free = []
    pe_ready = K.cp(peT[:, :, :], b.t[:, 0:32].rearrange("p (j m) -> p j m", j=2), m)
    b.free = [pe_ready]
    for j, name in enumerate(("cmp_w1_k", "cmp_w1_v")):
        s = K.wring.take()
        v1 = s.t[:, :].rearrange("p (m n) -> p m n", m=16)
        got = K.load(s, [(v1, w[name].rearrange("(m p) n -> p m n", p=P))])
        for half in range(2):
            b = K.banks.take()
            cols = slice(half * P, (half + 1) * P)
            K.project(b, b.t[:, 0:NB].rearrange("p (g n) -> p g n", g=NG), lambda k: v1[:, k, cols],
                      lambda k: x2[:, j, :, 2 * k:2 * k + CS * (NC - 1) + 1:CS], 16, got, shifted)
            m = K.project(b, b.t[:, NB:NB + 1], lambda k: v1[:, k, cols], lambda k: peT[:, j, k:k + 1], 16, pe_ready)
            u = j * 2 + half
            k = K.cp(peh[:, u:u + 1], b.t[:, NB:NB + 1], m)
            k = K.ts(hid[:, 0, u, :], b.t[:, 0:NB], peh[:, u:u + 1], ALU.add, k)
            b.free = [k]
        s.free = [m]
    x, x3, inner, th, act = (hid[:, i, :, :] for i in range(5))
    k = K.tt(x3, x, x, ALU.mult, k)
    k = K.tt(x3, x3, x, ALU.mult, k)
    k = K.stt(inner, x3, 0.044715, x, ALU.mult, ALU.add, k)
    k = K.a(th, inner, ACT.Tanh, k, scale=math.sqrt(2 / math.pi))
    k = K.stt(act, th, 1.0, x, ALU.add, ALU.mult, k)
    act_ready = K.ts(act, act, 0.5, ALU.mult, k)
    kcT = K.sb(ctx, "kcT", [P, NB])
    vc = K.sb(ctx, "vc", [P, NG, DH])
    b = K.banks.take()
    m = K.project(b, b.t[:, 0:NB], lambda k: w2k[:, k, :, :], lambda k: act[:, k, :], 2, act_ready)
    kc_ready = K.head_norm(tmp, b, m, kcT[:, :], gains[:, 1:2], n=NB)
    z = K.zero(vc[:, :, :])
    b = K.banks.take()
    for r in range(NR):
        for g in range(NG):
            m = K.project(b, b.t[32 * r:32 * r + NC, g * DH:(g + 1) * DH], lambda k: act[:, 2 + k, g * NC:(g + 1) * NC],
                          lambda k: w2v[:, k, :], 2)
    for r in range(NR):
        vc_ready = K.cp(vc[32 * r:32 * r + NC, :, :],
                        b.t[32 * r:32 * r + NC, 0:P].rearrange("p (g d) -> p g d", g=NG), m, z)
    b.free = [vc_ready]

    bias_c = K.sb(ctx, "bias_c", [P, TT, NH, 32])
    z = K.zero(bias_c[:, :, :, :], value=NEG)
    for i in range(TT):
        b = K.banks.take()
        for n in range(NC):
            at = P * i - CS * n - (CB - 1) + 511
            m = K.mm(b.t[:, n:n + 7 * 32 + 1:32], K.dist[:, at:at + P], relb[:, :], relb_ready, b.free,
                     K.dist_ready, signal=(n == NC - 1))
        k = K.cp(bias_c[:, i, :, 0:NC], b.t[:, 0:256].rearrange("p (h n) -> p h n", h=NH)[:, :, 0:NC], m, z)
        b.free = [k]
    bias_ready = k

    pc = K.ring(ctx, "cmp_p", 2, [P, NH, 32])
    pcT = K.ring(ctx, "cmp_pT", 2, [P, 2, P])
    st = K.sb(ctx, "cmp_stat", [P, TT, 3, NH])
    coef = K.sb(ctx, "cmp_coef", [P, TT, NH])
    o_ready = {}
    for i in range(TT):
        s, t2 = pc.take(), pcT.take()
        z = K.cp(s.t[:, :, NC:32], bias_c[:, i, :, NC:32], s.free, bias_ready)
        for g in range(NG):
            b = K.banks.take()
            half = slice(g * DH, (g + 1) * DH)
            for r in range(NR):
                m = K.mm(b.t[:, r * 32:r * 32 + NC], qT[half, r, i * P:(i + 1) * P],
                         kcT[half, g * NC:(g + 1) * NC], b.free, q_ready, kc_ready, signal=(r == NR - 1))
            v3 = b.t[:, 0:P].rearrange("p (h n) -> p h n", h=NR)[:, :, 0:NC]
            hs = slice(g * NR, (g + 1) * NR)
            k = K.tt(s.t[:, hs, 0:NC], v3, bias_c[:, i, hs, 0:NC], ALU.add, m, s.free, bias_ready)
            b.free = [k]
        mx, sm_, rc = (st[:, i, j, :] for j in range(3))
        k = K.red(mx, s.t[:, :, :], ALU.max, k, z)
        k = K.tt(s.t[:, :, :], s.t[:, :, :], spread(mx, 32), ALU.subtract, k)
        k = K.a(s.t[:, :, :], s.t[:, :, :], ACT.Exp, k)
        p_ready = k
        k = K.red(sm_, s.t[:, :, :], ALU.add, k)
        k = K.ts(sm_, sm_, 1e-30, ALU.max, k)
        k = K.recip(rc, sm_, k)
        k = K.stt(coef[:, i, :], rc, c("valid_c")[:, i:i + 1], gate[:, i, 0:3 * NH:3], ALU.mult, ALU.mult, k, gate_ready)
        b = K.banks.take()
        for g in range(NG):
            m = K.tr(b.t[:, g * P:(g + 1) * P], s.t[:, g * NR:(g + 1) * NR, :].rearrange("p h n -> p (h n)"),
                     p_ready, b.free)
        e = K.cp(t2.t[:, :, :], b.t[:, 0:2 * P].rearrange("p (g n) -> p g n", g=2), m, t2.free)
        s.free, b.free = [m, k], [e]
        for r in range(NR):
            b = K.banks.take()
            rows = slice(32 * r, 32 * r + NC)
            for g in range(NG):
                m = K.mm(b.t[:, g * DH:(g + 1) * DH], t2.t[rows, g, :], vc[rows, g, :], e, b.free, vc_ready)
            k = K.tt(o[:, i, :].rearrange("p (g r d) -> p g r d", g=NG, r=NR)[:, :, r, :],
                     b.t[:, 0:P].rearrange("p (g d) -> p g d", g=NG),
                     spread(coef[:, i, r:NH:NR], DH), ALU.mult, m, k)
            b.free = [k]
        t2.free = [m]
        o_ready[i] = k

    K.meet()
    ctx.close()
    scratch = K.ring(outer, "att_o", 2, [P, NW])
    for j, (name, kT, vv, k_ready, v_ready) in enumerate(
            (("slc", ksT, vs, ks_ready, vs_ready), ("win", kwT, vw, kw_ready, vw_ready))):
        cf = K.sb(outer, f"{name}_coef", [P, TT, 2, NH])

        def finish(i, b, got, sums, sums_ready):
            k = K.recip(cf[:, i, 0, :], sums, sums_ready)
            k = K.tt(cf[:, i, 1, :], cf[:, i, 0, :], gate[:, i, 1 + j:3 * NH:3], ALU.mult, k, gate_ready)
            s = scratch.take()
            e = K.tt(s.t[:, :].rearrange("p (h d) -> p h d", h=NH), b.t[:, :].rearrange("p (h d) -> p h d", h=NH),
                     spread(cf[:, i, 1, :], DH), ALU.mult, k, got, s.free)
            k = K.tt(o[:, i, :], o[:, i, :], s.t[:, :], ALU.add, e, o_ready[i])
            s.free = [k]
            o_ready[i] = k
            return e

        with ExitStack() as inner_ctx:
            K.attention(inner_ctx, name,
                        lambda h: qT[(h // NR) * DH:(h // NR + 1) * DH, h % NR, :],
                        lambda h: kT[(h // NR) * DH:(h // NR + 1) * DH, :],
                        lambda h, j2: vv[:, j2, (h // NR) * DH:(h // NR + 1) * DH],
                        NW, big, [q_ready, k_ready, v_ready, big_ready], finish)
            K.meet()

    return K.to_fm(o, o_ready, oT)


def mix(K, p1, d, mu, out, ready, out_free):
    k = K.tt(d, p1[:, 0:S], p1[:, 1:S + 1], ALU.subtract, ready)
    return K.stt(out, d, mu, p1[:, 1:S + 1], ALU.mult, ALU.add, k, out_free)


def rwkv(K, ctx, hT, ready, oT):
    w, c = K.w, K.c
    w_in = w["w_in"]
    sm = K.channel("rwkv_small")
    mu = K.sb(ctx, "mu", [P, 14])
    vec = K.sb(ctx, "rwkv_vec", [P, 8, 4])
    w2a2, g2 = K.sb(ctx, "w2a2", [P, RW]), K.sb(ctx, "g2", [P, RW])
    rows = K.sb(ctx, "rwkv_rows", [46, P])
    small = sm.dma(K.act, rows[0:14, :], w["rwkv_mu"].rearrange("o (k p) -> (o k) p", p=P))
    names = ("rwkv_w0", "rwkv_a0", "rwkv_k_k", "rwkv_k_a", "rwkv_r_k", "rwkv_ln_g", "rwkv_ln_b")
    for j, name in enumerate(names):
        src = w[name].rearrange("(k two) d -> k (two d)", two=2) if name == "rwkv_r_k" else \
            w[name].rearrange("o (k p) -> (o k) p", p=P)
        small = sm.dma(K.act, rows[14 + 4 * j:18 + 4 * j, :], src)
    small = sm.dma(K.act, w2a2[0:64, :], w["rwkv_w2"])
    small = sm.dma(K.act, w2a2[64:P, :], w["rwkv_a2"])
    small = sm.dma(K.act, g2[:, :], w["rwkv_g2"])
    b = K.banks.take()
    m = K.tr(b.t[:, 0:42], rows[0:42, :], small, b.free, K.consts_ready)
    k = K.cp(mu[:, :], b.t[:, 0:14], m)
    vec_ready = K.cp(vec[:, 0:7, :], b.t[:, 14:42].rearrange("p (j k) -> p j k", j=7), m)
    b.free = [vec_ready]
    w0, a0, kkg, kag, rkg, lng, lnb = (vec[:, j, :] for j in range(7))

    p1 = K.ring(ctx, "p1", 3, [P, S + 1])
    for s in p1.slots:
        s.free = [K.zero(s.t[:, 0:1])]
    tmp = K.ring(ctx, "rw_tmp", 3, [P, S])
    lor, xg = K.sb(ctx, "lor", [P, S]), K.sb(ctx, "xg", [P, S])
    thw = K.sb(ctx, "thw", [DH, S])

    def mixed(v, at, got, muc, out, out_free=None):
        b, s, d = K.banks.take(), p1.take(), tmp.take()
        m = K.project(b, b.t[:, :], lambda k: v[:, k, at:at + P], lambda k: hT[:, k, :], KD, got, ready)
        e = K.a(s.t[:, 1:S + 1], b.t[:, :], ACT.Copy, m, s.free)
        b.free = [e]
        k = mix(K, s.t, d.t[:, :], mu[:, muc:muc + 1], out, [e, d.free, vec_ready], out_free)
        s.free = d.free = [k]
        return m, k

    s, v, got = K.weights(w_in, COL_LORA, 256)
    m, lor_ready = mixed(v, 0, got, 12, lor[:, :])
    m, k = mixed(v, P, got, 13, xg[:, :])
    s.free = [m]
    thw_ready = K.a(thw[:, :], lor[0:DH, :], ACT.Tanh, lor_ready)
    sg_ready = K.a(xg[:, :], xg[:, :], ACT.Sigmoid, k)

    names = ("rT", "kT", "vT", "lw", "aT", "gT", "bv")
    buf = {n: K.sb(ctx, f"rw_{n}", [P, S]) for n in names}
    rT, kT, vT, lw, aT, gT, bv = (buf[n][:, :] for n in names)
    kk, kp, y = lw, kT, aT.rearrange("p (h d) -> p h d", h=8)
    L, E1, E2 = (K.sb(ctx, f"rw_{n}", [P, TT, P + 1]) for n in ("L", "E1", "E2"))
    ra = K.sb(ctx, "rw_ra", [P, TT, 2, P])
    kt, bt = K.sb(ctx, "rw_kt", [P, TT, P]), K.sb(ctx, "rw_bt", [P, TT, P])
    Kt, Bt, Vt = (K.sb(ctx, f"rw_{n}_tm", [P, TT, P]) for n in "KBV")
    AM = K.sb(ctx, "rw_AM", [P, 8, 4, P])
    ready0 = [K.zero(AM[:, :, :, :]), K.zero(L[:, :, 0:1])]
    Alow = [K.sb(ctx, f"rw_low{g}", [P, 4, P]) for g in range(2)]
    ready0 += [K.zero(x[:, :, :]) for x in Alow]
    level = K.ring(ctx, "rw_lev", 2, [P, 4, P])
    WU = [[K.sb(ctx, f"rw_{n}{g}", [P, 4, P]) for n in "WUY"] for g in range(2)]
    Z = K.sb(ctx, "rw_Z", [P, P])
    zs = K.sb(ctx, "rw_zs", [P, TT])
    step = K.ring(ctx, "rw_step", 4, [P, P])
    yst = K.sb(ctx, "rw_yst", [P, 4, 8])
    ones = K.sb(ctx, "rw_ones", [P, P])
    ones_ready = K.zero(ones[:, :], value=1.0)
    pair_done = []

    for f in range(4):
        cols = slice(f * P, (f + 1) * P)
        s = K.wring.take()
        v = s.t[:, 0:8 * 384].rearrange("p (k n) -> p k n", k=KD)
        got = K.load(s, [(v[:, :, j * P:(j + 1) * P], w_in.rearrange("(k p) n -> p k n", p=P)[:, :, at + f * P:at + (f + 1) * P])
                         for j, at in enumerate((COL_R, COL_K, COL_V))])
        free = pair_done
        m, r_ready = mixed(v, 0, got, f, rT, free)
        m, k_ready = mixed(v, P, got, 4 + f, kT, free)
        m, v_ready = mixed(v, 2 * P, got, 8 + f, vT, free)
        s.free = [m]
        b = K.banks.take()
        m = K.mm(b.t[:, :], w2a2[0:DH, cols], thw[:, :], b.free, thw_ready)
        k = K.a(lw, b.t[:, :], ACT.Sigmoid, m, free, bias=w0[:, f:f + 1])
        b.free = [k]
        k = K.ts(lw, lw, -DECAY, ALU.mult, k)
        lw_ready = k
        b = K.banks.take()
        m = K.mm(b.t[:, :], w2a2[DH:P, cols], lor[DH:P, :], b.free, lor_ready)
        a_ready = K.a(aT, b.t[:, :], ACT.Sigmoid, m, free, bias=a0[:, f:f + 1])
        b.free = [a_ready]
        b = K.banks.take()
        m = K.mm(b.t[:, :], g2[:, cols], xg[:, :], b.free, sg_ready)
        g_ready = K.a(gT, b.t[:, :], ACT.Copy, m, free)
        b.free = [g_ready]
        for n in range(TT):
            k = K.dve.do(lambda e, n=n: e.tensor_tensor_scan(
                L[:, n, 1:P + 1], ones[:, :], buf["lw"][:, n * P:(n + 1) * P], 0.0, ALU.mult, ALU.add),
                lw_ready, ones_ready, ready0, free)
        scanned = k
        k = K.tt(E1[:, :, :], L[:, :, :], L[:, :, 64:65].broadcast_to([P, TT, P + 1]), ALU.subtract, k)
        e2 = K.a(E2[:, :, :], E1[:, :, :], ACT.Exp, k, scale=-1.0)
        e1 = K.a(E1[:, :, :], E1[:, :, :], ACT.Exp, e2)
        k0 = K.ts(kk, kT, kkg[:, f:f + 1], ALU.mult, k_ready, vec_ready, scanned)
        t1, t2 = tmp.take(), tmp.take()
        k = K.a(t1.t[:, :], kk, ACT.Square, k0, t1.free)
        b = K.banks.take()
        m = K.mm(b.t[:, :], c("ones64"), t1.t[:, :], k, b.free)
        k = K.ts(t2.t[:, :], b.t[:, :], NORM_FLOOR, ALU.max, m, t2.free)
        b.free, t1.free = [k], [m]
        k = K.a(t2.t[:, :], t2.t[:, :], ACT.Ln, k, scale=2.0 ** LN_SHIFT)
        k = K.a(t2.t[:, :], t2.t[:, :], ACT.Exp, k, scale=-0.5, bias=c("ln_back"))
        kk_ready = K.tt(kk, kk, t2.t[:, :], ALU.mult, k)
        t2.free = [kk_ready]
        t1 = tmp.take()
        k = K.ts(t1.t[:, :], aT, -1.0, ALU.add, a_ready, t1.free, s2=kag[:, f:f + 1], op1=ALU.mult)
        kp_ready = K.stt(kp, t1.t[:, :], 1.0, kT, ALU.add, ALU.mult, k, k0)
        t1.free = [kp_ready]
        v4 = lambda x: x.rearrange("p (n t) -> p n t", n=TT)
        k = K.stt(ra[:, :, 0, :], v4(kk), -1.0, E1[:, :, 0:P], ALU.mult, ALU.mult, kk_ready, e1)
        ra_ready = K.tt(ra[:, :, 1, :], v4(rT), E1[:, :, 1:P + 1], ALU.mult, e1, r_ready)
        kt_ready = K.tt(kt[:, :, :], v4(kp), E2[:, :, 1:P + 1], ALU.mult, kp_ready, e2)
        t1 = tmp.take()
        k = K.tt(t1.t[:, :], kk, aT, ALU.mult, kk_ready, a_ready, t1.free)
        bt_ready = K.tt(bt[:, :, :], v4(t1.t[:, :]), E2[:, :, 1:P + 1], ALU.mult, k)
        t1.free = [bt_ready]
        t1 = tmp.take()
        k = K.stt(t1.t[:, :], rT, rkg[:, f:f + 1], kp, ALU.mult, ALU.mult, kp_ready, r_ready, t1.free)
        b = K.banks.take()
        m = K.mm(b.t[:, :], c("ones64"), t1.t[:, :], k, b.free)
        t1.free = [m]
        bv_ready = K.tt(bv, b.t[:, :], vT, ALU.mult, m, v_ready)
        b.free = [bv_ready]
        zs_ready = K.tt(zs[:, 0:TT - 1], E1[:, 0:TT - 1, P:P + 1].rearrange("p n o -> p (n o)"),
                        E2[:, 1:TT, 0:1].rearrange("p n o -> p (n o)"), ALU.mult, e1, e2, bv_ready)
        tm_ready = []
        for dst, src, r0 in ((Kt, kt[:, :, :], kt_ready), (Bt, bt[:, :, :], bt_ready), (Vt, v4(vT), v_ready)):
            b = K.banks.take()
            for n in range(TT):
                m = K.tr(b.t[:, n * P:(n + 1) * P], src[:, n, :], r0, b.free, signal=(n == TT - 1))
            k = K.a(dst[:, :, :], b.t[:, :].rearrange("p (n t) -> p n t", n=TT), ACT.Copy, m, free)
            b.free = [k]
            tm_ready.append(k)
        am_ready = {}
        for u in range(8):
            hh, n = divmod(u, TT)
            hp = slice(hh * DH, (hh + 1) * DH)
            b = K.banks.take()
            K.mm(b.t[:, 0:256].rearrange("p (x t) -> p x t", x=2), kt[hp, n, :], ra[hp, n, :, :], b.free, kt_ready, ra_ready, signal=False)
            m = K.mm(b.t[:, 256:512].rearrange("p (x t) -> p x t", x=2), bt[hp, n, :], ra[hp, n, :, :], bt_ready)
            k = K.dve.do(lambda e, u=u, b=b: e.copy_predicated(
                AM[:, u, :, :], c("mask_rw").bitcast(I32).rearrange("p (x t) -> p x t", x=4),
                b.t[:, :].rearrange("p (x t) -> p x t", x=4)), m, ready0, free)
            b.free = [k]
            am_ready[u] = k
        inv_ready = []
        state = []
        for g in range(2):
            b = K.banks.take()
            for i in range(4):
                n, hh = i, g
                hp = slice(hh * DH, (hh + 1) * DH)
                m = K.mm(b.t[:, i * P:(i + 1) * P], ra[hp, n, 0, :], bt[hp, n, :], b.free, ra_ready, bt_ready,
                         signal=(i == 3))
            A = Alow[g]
            a_low = K.dve.do(lambda e, A=A, b=b: e.copy_predicated(
                A[:, :, :], c("mask_low4").bitcast(I32).rearrange("p (x t) -> p x t", x=4),
                b.t[:, :].rearrange("p (x t) -> p x t", x=4)), m, ready0, free)
            b.free = [a_low]
            W, U, Y = WU[g]
            eye = spread(c("ident"), 4, 1)
            k = K.tt(W[:, :, :], AM[:, 4 * g:4 * g + 4, 2, :], spread(c("lev0u"), 4, 1), ALU.mult, am_ready[4 * g + 3], free)
            w_r = K.tt(W[:, :, :], W[:, :, :], eye, ALU.add, k)
            k = K.tt(U[:, :, :], A[:, :, :], spread(c("lev0"), 4, 1), ALU.mult, a_low, free)
            u_r = K.tt(U[:, :, :], U[:, :, :], eye, ALU.add, k)
            state.append((A, W, U, Y, a_low, w_r, u_r))
        for lv in range(1, 7):
            for g in range(2):
                A, W, U, Y, a_low, w_r, u_r = state[g]
                s = level.take()
                am = K.tt(s.t[:, :, :], A[:, :, :], spread(c(f"lev{lv}"), 4, 1), ALU.mult, a_low, s.free, lane=K.pool)
                b = K.banks.take()
                for i in range(4):
                    m = K.mm(b.t[:, i * P:(i + 1) * P], s.t[:, i, :], W[:, i, :], am, w_r, b.free, signal=(i == 3))
                s.free = [m]
                y_r = K.a(Y[:, :, :], b.t[:, :].rearrange("p (x t) -> p x t", x=4), ACT.Copy, m, free)
                b.free = [y_r]
                b1 = K.banks.take()
                for i in range(4):
                    m1 = K.mm(b1.t[:, i * P:(i + 1) * P], U[:, i, :], Y[:, i, :], y_r, u_r, b1.free, signal=(i == 3))
                m2 = None
                if lv < 6:
                    b2 = K.banks.take()
                    for i in range(4):
                        m2 = K.mm(b2.t[:, i * P:(i + 1) * P], Y[:, i, :], U[:, i, :], b2.free, signal=(i == 3))
                w_r = K.tt(W[:, :, :], W[:, :, :], b1.t[:, :].rearrange("p (x t) -> p x t", x=4), ALU.add, m1)
                b1.free = [w_r]
                if lv < 6:
                    u_r = K.tt(U[:, :, :], U[:, :, :], b2.t[:, :].rearrange("p (x t) -> p x t", x=4), ALU.add, m2)
                    b2.free = [u_r]
                state[g] = (A, W, U, Y, a_low, w_r, u_r)
        z_r = K.zero(Z[:, :], free)
        for n in range(TT):
            units = [n, TT + n]
            b, sa, rhs = K.banks.take(), step.take(), step.take()
            K.mm(b.t[:, 0:P], ra[:, n, 0, :], Z[:, :], z_r, b.free, ra_ready, signal=False, stop=False, loose=True)
            for hh, u in enumerate(units):
                m = K.mm(b.t[:, hh * DH:(hh + 1) * DH], AM[:, u, 0, :], Vt[:, n, hh * DH:(hh + 1) * DH],
                         am_ready[u], tm_ready, start=False, loose=True)
            k = K.a(rhs.t[:, :], b.t[:, 0:P], ACT.Copy, m, rhs.free)
            b.free = [k]
            b = K.banks.take()
            for hh, u in enumerate(units):
                m = K.mm(b.t[:, hh * DH:(hh + 1) * DH], state[hh][1][:, n, :], rhs.t[:, hh * DH:(hh + 1) * DH],
                         k, state[hh][5], b.free)
            rhs.free = [m]
            sa_r = K.cp(sa.t[:, :], b.t[:, 0:P], m, sa.free)
            b.free = [sa_r]
            if n < TT - 1:
                b = K.banks.take()
                K.mm(b.t[:, 0:P], Kt[:, n, :], Vt[:, n, :], b.free, signal=False, stop=False)
                mz = K.mm(b.t[:, 0:P], Bt[:, n, :], sa.t[:, :], sa_r, start=False)
                bz = b
            b = K.banks.take()
            K.mm(b.t[:, 0:P], ra[:, n, 1, :], Z[:, :], b.free, signal=False, stop=False, loose=True)
            for hh, u in enumerate(units):
                cs = slice(hh * DH, (hh + 1) * DH)
                K.mm(b.t[:, cs], AM[:, u, 1, :], Vt[:, n, cs], start=False, stop=False, signal=False, loose=True)
                m = K.mm(b.t[:, cs], AM[:, u, 3, :], sa.t[:, cs], sa_r, start=False, loose=True)
            y_ready = K.a(y[:, 2 * n:2 * n + 2, :], b.t[:, 0:P].rearrange("p (h d) -> p h d", h=2), ACT.Copy, m, free, bt_ready)
            b.free = [y_ready]
            sa.free = [m]
            if n < TT - 1:
                for hh in range(2):
                    hp = slice(hh * DH, (hh + 1) * DH)
                    k = K.tt(Z[hp, hp], Z[hp, hp], bz.t[hp, hp], ALU.add, mz, m)
                bz.free = [k]
                z_r = K.ts(Z[:, :], Z[:, :], zs[:, n:n + 1], ALU.mult, k, zs_ready)
        t1 = tmp.take()
        sq = t1.t[:, :].rearrange("p (h d) -> p h d", h=8)
        s1, s2, s3, s4 = (yst[:, j, :] for j in range(4))
        k = K.red(s1, y[:, :, :], ALU.add, y_ready)
        k = K.ts(s2, s1, 1.0 / DH, ALU.mult, k)
        k = K.tt(y[:, :, :], y[:, :, :], spread(s2, DH), ALU.subtract, k)
        k1 = K.a(sq, y[:, :, :], ACT.Square, k, t1.free)
        k = K.red(s3, sq, ALU.add, k1)
        t1.free = [k]
        k = K.ts(s3, s3, 1.0 / DH, ALU.mult, k, s2=GN_EPS, op1=ALU.add)
        k = K.recip(s4, s3, k)
        k = K.a(s4, s4, ACT.Sqrt, k)
        k = K.tt(y[:, :, :], y[:, :, :], spread(s4, DH), ALU.mult, k)
        b = K.banks.take()
        for n in range(TT):
            m = K.tr(b.t[:, n * P:(n + 1) * P], y[:, 2 * n:2 * n + 2, :].rearrange("p h d -> p (h d)"), k, b.free,
                     signal=(n == TT - 1))
        t1 = tmp.take()
        k = K.ts(t1.t[:, :], b.t[:, :], lng[:, f:f + 1], ALU.mult, m, t1.free, s2=lnb[:, f:f + 1], op1=ALU.add)
        b.free = [k]
        k = K.tt(t1.t[:, :], t1.t[:, :], bv, ALU.add, k, bv_ready)
        k = K.tt(oT[:, f, :], t1.t[:, :], gT, ALU.mult, k, g_ready)
        t1.free = [k]
        pair_done = [k, K.pe.last(), K.act.last()]
        out = k
    return out


def merge(K, ctx, hT, oaT, obT, oa_ready, ob_ready, x):
    w = K.w
    mT = K.sb(ctx, "mergedT", [P, KD, S])
    sg = K.ring(ctx, "sg", 4, [P, S])
    acc = K.ring(ctx, "mg", 2, [P, S])
    branches = []
    sp_, vp = [None, None], [None, None]
    gp = [None, None]
    for half in range(2):
        gs = [K.weights(w["w_in"], at + half * 512, 512) for at in (COL_GA, COL_GB)]
        if half == 0:
            ps = [K.weights(w[n], 0, D, ktiles=4) for n in ("w_proj_a", "w_proj_b")]
        for mm_ in range(4):
            f = half * 4 + mm_
            part = []
            for j, (oT, o_ready) in enumerate(((oaT, oa_ready), (obT, ob_ready))):
                gslot, gv, ggot = gs[j]
                pslot, pv, pgot = ps[j]
                b, s = K.banks.take(), sg.take()
                m = K.project(b, b.t[:, :], lambda k: gv[:, k, mm_ * P:(mm_ + 1) * P], lambda k: hT[:, k, :], KD, ggot)
                e = K.a(s.t[:, :], b.t[:, :], ACT.Sigmoid, m, s.free)
                b.free = [e]
                if mm_ == 3:
                    gslot.free = [m]
                b = K.banks.take()
                m = K.project(b, b.t[:, :], lambda k: pv[:, k, f * P:(f + 1) * P], lambda k: oT[:, k, :], 4, pgot, o_ready)
                k = K.tt(s.t[:, :], s.t[:, :], b.t[:, :], ALU.mult, m, e)
                b.free = [k]
                if f == KD - 1:
                    pslot.free = [m]
                part.append((s, k))
            (s0, k0), (s1, k1) = part
            k = K.tt(mT[:, f, :], s0.t[:, :], s1.t[:, :], ALU.add, k0, k1)
            s0.free = s1.free = [k]
    return add_product(K, "w_out", mT, KD, k, x)


def add_product(K, name, aT, n, ready, x):
    done = [[] for _ in range(TT)]
    for half in range(2):
        s, v, got = K.weights(K.w[name], half * 512, 512, ktiles=n)
        for t in range(TT):
            b = K.banks.take()
            m = K.project(b, b.t[:, :], lambda k: aT[:, k, t * P:(t + 1) * P], lambda k: v[:, k, :], n, got, ready)
            xs = x[:, t, half * 512:(half + 1) * 512]
            k = K.tt(xs, xs, b.t[:, :], ALU.add, m)
            b.free = [k]
            done[t].append(k)
        s.free = [m]
    return done


def ffn(K, ctx, h2T, ready, x):
    w = K.w
    conv_rows = K.sb(ctx, "conv_rows", [4 * 2 * FT // 2, 2, P])
    cv = K.sb(ctx, "conv_cols", [P, 4, 2 * FT])
    sm = K.channel("ffn_small")
    for j in range(4):
        src = w["conv_b"] if j == 3 else w["conv_w"][j:j + 1, :]
        small = sm.dma(K.act, conv_rows[FT * j:FT * (j + 1), :, :],
                       src.rearrange("o (two k p) -> (o k) two p", two=2, p=P))
    for two in range(2):
        b = K.banks.take()
        m = K.tr(b.t[:, 0:4 * FT], conv_rows[:, two, :], small, b.free)
        cv_ready = K.cp(cv[:, :, two * FT:(two + 1) * FT], b.t[:, 0:4 * FT].rearrange("p (j k) -> p j k", j=4), m)
        b.free = [cv_ready]
    fT = K.sb(ctx, "fT", [P, FT, S])
    ub = K.ring(ctx, "ffn_u", 4, [P, S + 2])
    cb = K.ring(ctx, "ffn_c", 4, [P, S])
    for s in ub.slots:
        s.free = [K.zero(s.t[:, 0:2])]
    w_up = w["w_up"].rearrange("(k p) n -> p k n", p=P)
    for j in range(FT // 2):
        s = K.wring.take()
        v = s.t[:, :].rearrange("p (k two n) -> p k two n", k=KD, two=2)
        got = K.load(s, [(v[:, :, two, :], w_up[:, :, two * DFF + j * 256:two * DFF + (j + 1) * 256]) for two in range(2)])
        for i in range(2):
            f = 2 * j + i
            conv = []
            for two in range(2):
                b, u, cbuf = K.banks.take(), ub.take(), cb.take()
                col = two * FT + f
                m = K.project(b, b.t[:, :], lambda k: v[:, k, two, i * P:(i + 1) * P], lambda k: h2T[:, k, :], KD, got, ready)
                e = K.a(u.t[:, 2:S + 2], b.t[:, :], ACT.Copy, m, u.free)
                k = K.a(cbuf.t[:, :], b.t[:, :], ACT.Identity, m, cbuf.free, cv_ready,
                        scale=cv[:, 2, col:col + 1], bias=cv[:, 3, col:col + 1])
                b.free = [k]
                for tap in (1, 0):
                    k = K.stt(cbuf.t[:, :], u.t[:, tap:tap + S], cv[:, tap, col:col + 1], cbuf.t[:, :],
                              ALU.mult, ALU.add, k, e)
                u.free = [k]
                conv.append((cbuf, k))
            (val, kv), (gt, kg) = conv
            sgm = ub.take()
            k = K.a(sgm.t[:, 2:S + 2], gt.t[:, :], ACT.Sigmoid, kg, sgm.free)
            k2 = K.tt(gt.t[:, :], gt.t[:, :], val.t[:, :], ALU.mult, kv, k, lane=K.pool)
            k = K.tt(fT[:, f, :], gt.t[:, :], sgm.t[:, 2:S + 2], ALU.mult, k, k2)
            sgm.free = gt.free = [k]
            val.free = [k2]
        s.free = [m]
    f_ready = k
    done = [[] for _ in range(TT)]
    w_down = w["w_down"].rearrange("(k p) n -> p k n", p=P)
    for half in range(2):
        acc = [K.banks.take() for _ in range(TT)]
        for k0 in range(0, FT, 8):
            n = min(8, FT - k0)
            s = K.wring.take()
            v = s.t[:, 0:n * 512].rearrange("p (k n) -> p k n", k=n)
            got = K.load(s, [(v, w_down[:, k0:k0 + n, half * 512:(half + 1) * 512])])
            for t in range(TT):
                for k in range(n):
                    m = K.mm(acc[t].t[:, :], fT[:, k0 + k, t * P:(t + 1) * P], v[:, k, :], got, acc[t].free, f_ready,
                             start=(k0 + k == 0), stop=(k0 + k == FT - 1), signal=(k == n - 1))
                if k0 + n == FT:
                    xs = x[:, t, half * 512:(half + 1) * 512]
                    e = K.tt(xs, xs, acc[t].t[:, :], ALU.add, m)
                    acc[t].free = [e]
                    done[t].append(e)
            s.free = [m]
    return done


def selected_attention(K, ctx, hT, ready, oT, spare):
    w, c = K.w, K.c
    w_in = w["w_in_2"]
    sm = K.channel("dsa_small")
    qT, kT = K.sb(ctx, "q2T", [P, 4, S]), K.sb(ctx, "k2T", [P, 4, S])
    va = K.sb(ctx, "va", [P, TT, NW])
    iqT, ikT = K.sb(ctx, "iqT", [P, 2, S]), K.sb(ctx, "ikT", [P, S])
    iw = K.sb(ctx, "iw", [P, TT, IH])
    big = K.sb(ctx, "dsa_bias", [P, NH, 512])
    gains = K.sb(ctx, "dsa_gains", [P, 2])
    score = K.sb(ctx, "score", [P, TT, S])
    masks = K.sb(ctx, "selmask", [P, TT, S], BF16)
    top = K.sb(ctx, "top8", [P, TT, 8])
    eye = K.sb(ctx, "eye_bf", [P, P], BF16)
    outer, ctx = ctx, ExitStack()
    relb = K.sb(ctx, "dsa_relb", [33, NH])
    tmp = K.ring(ctx, "dsa_tmp", 4, [P, S])
    eye_ready = K.cp(eye[:, :], c("ident"))
    for half in range(2):
        for j, name in enumerate(("q_norm_g_2", "k_norm_g_2")):
            small = sm.dma(K.act, gains[half * DH:(half + 1) * DH, j:j + 1], w[name].rearrange("o d -> d o"), slow=True)
    K.ts(gains[:, 0:1], gains[:, 0:1], DH ** -0.5, ALU.mult, small)
    K.load_distances(ctx)
    big_ready, _ = K.bias_table(ctx, "dsa", w["rel_bias_2"], big, relb)

    s = K.wring.take()
    width = IH * ID + 4 * ID + IH
    v = s.t[:, 0:KD * width].rearrange("p (k n) -> p k n", k=KD)
    src = w_in.rearrange("(k p) n -> p k n", p=P)
    got = K.load(s, [(v[:, :, 0:IH * ID + ID], src[:, :, COL2_IQ:COL2_IW])]
                 + [(v[:, :, 256 + q * ID:256 + (q + 1) * ID], src[:, :, COL2_IK:COL2_IW]) for q in range(1, 4)]
                 + [(v[:, :, 256 + 4 * ID:width], src[:, :, COL2_IW:COL2_QB])])
    for j in range(2):
        b = K.banks.take()
        m = K.project(b, b.t[:, :], lambda k: v[:, k, j * P:(j + 1) * P], lambda k: hT[:, k, :], KD, got, ready)
        iq_ready = K.a(iqT[:, j, :], b.t[:, :], ACT.Copy, m)
        b.free = [iq_ready]
    b = K.banks.take()
    m = K.project(b, b.t[:, :], lambda k: v[:, k, 256:256 + 4 * ID], lambda k: hT[:, k, :], KD)
    ik_ready = K.a(ikT[:, :], b.t[:, :], ACT.Copy, m)
    b.free = [ik_ready]
    b = K.banks.take()
    for t in range(TT):
        m = K.project(b, b.t[:, t * IH:(t + 1) * IH], lambda k: hT[:, k, t * P:(t + 1) * P],
                      lambda k: v[:, k, 256 + 4 * ID:width], KD)
    s.free = [m]
    iw_ready = K.ts(iw[:, :, :], b.t[:, 0:TT * IH].rearrange("p (t h) -> p t h", t=TT), IH ** -0.5, ALU.mult, m)
    b.free = [iw_ready]

    rel = K.ring(ctx, "idx_r", 3, [P, S])
    score_ready = {}
    for i in range(1, TT):
        n = (i + 1) * P
        for h in range(IH):
            rows = slice((h % 4) * ID, (h % 4 + 1) * ID)
            b, r = K.banks.take(), rel.take()
            m = K.mm(b.t[:, 0:n], iqT[rows, h // 4, i * P:(i + 1) * P], ikT[rows, 0:n], b.free, iq_ready, ik_ready)
            e = K.a(r.t[:, 0:n], b.t[:, 0:n], ACT.Relu, m, r.free, scale=ID ** -0.5)
            b.free = [e]
            if h == 0:
                k = K.ts(score[:, i, 0:n], r.t[:, 0:n], iw[:, i, h:h + 1], ALU.mult, e, iw_ready)
            else:
                k = K.stt(score[:, i, 0:n], r.t[:, 0:n], iw[:, i, h:h + 1], score[:, i, 0:n], ALU.mult, ALU.add, e, k)
            r.free = [k]
        diag = score[:, i, i * P:n]
        score_ready[i] = K.pool.do(lambda e, d=diag: e.affine_select(
            out=d, in_=d, compare_op=ALU.is_ge, fill=NEG, base=0, pattern=[[-1, P]], channel_multiplier=1), k)

    def feature_major(dst, at, gain):
        s, v, got = K.weights(w_in, at, 512)
        for f in range(4):
            b = K.banks.take()
            m = K.project(b, b.t[:, :], lambda k: v[:, k, f * P:(f + 1) * P], lambda k: hT[:, k, :], KD, got)
            r = K.head_norm(tmp, b, m, dst[:, f, :], gain)
        s.free = [m]
        return r

    q_ready = feature_major(qT, COL2_Q, gains[:, 0:1])
    k_ready = feature_major(kT, COL2_K, gains[:, 1:2])
    s, v, got = K.weights(w_in, COL2_V, 512)
    for t in range(TT):
        b = K.banks.take()
        m = K.project(b, b.t[:, :], lambda k: hT[:, k, t * P:(t + 1) * P], lambda k: v[:, k, :], KD, got)
        v_ready = K.a(va[:, t, :], b.t[:, :], ACT.Copy, m)
        b.free = [v_ready]
    s.free = [m]

    K.meet()
    ctx.close()
    ctx = outer
    mask_ready = {}
    chain = dict(score_ready)
    for i in range(1, TT):
        n = (i + 1) * P
        sc, t8 = score[:, i, 0:n], top[:, i, :]
        for _ in range(TOPK // 8):
            k = K.dve.do(lambda e, sc=sc, t8=t8: e.max(t8, sc), chain[i])
            chain[i] = K.dve.do(lambda e, sc=sc, t8=t8: e.match_replace(sc, t8, sc, TAKEN), k)
        mask_ready[i] = K.ts(masks[:, i, 0:n], sc, 0.5 * TAKEN, ALU.is_gt, chain[i], s2=NEG, op1=ALU.mult)

    def extra(i, out):
        return K.mm(out, eye[:, :], masks[:, i, 0:(i + 1) * P], mask_ready[i], eye_ready, start=False)

    o = spare
    rc = K.sb(ctx, "dsa_rc", [P, TT, NH])
    o_ready = {}

    def finish(i, b, got, sums, sums_ready):
        k = K.recip(rc[:, i, :], sums, sums_ready)
        k = K.tt(o[:, i, :].rearrange("p (h d) -> p h d", h=NH), b.t[:, :].rearrange("p (h d) -> p h d", h=NH),
                 spread(rc[:, i, :], DH), ALU.mult, k, got)
        o_ready[i] = k
        return k

    K.attention(ctx, "dsa", lambda h: qT[(h % 2) * DH:(h % 2 + 1) * DH, h // 2, :],
                lambda h: kT[(h % 2) * DH:(h % 2 + 1) * DH, h // 2, :],
                lambda h, j: va[:, j, h * DH:(h + 1) * DH], NW, big, [q_ready, k_ready, v_ready, big_ready],
                finish, extra)
    return K.to_fm(o, o_ready, oT)


def gla(K, ctx, hT, ready, oT):
    w, c = K.w, K.c
    w_in = w["w_in_2"]
    sm = K.channel("gla_small")
    w2 = K.sb(ctx, "gla_w2", [RANK, 2 * P])
    cols = K.sb(ctx, "gla_cols", [P, 3])
    small = sm.dma(K.act, w2[:, :], w["gla_gate_w2_2"])
    small = sm.dma(K.act, cols[:, 0:2], w["gla_gate_b_2"].rearrange("o (k p) -> p (o k)", p=P), slow=True)
    small = sm.dma(K.act, cols[:, 2:3], w["gla_out_norm_g_2"].rearrange("o d -> d o"), slow=True)
    NCH = S // GC
    ones = K.sb(ctx, "gla_ones", [P, P])
    ones_ready = K.zero(ones[:, :], value=1.0)
    tmp = K.ring(ctx, "gla_tmp", 4, [P, S])
    rg = K.sb(ctx, "rgT", [P, 4, S])
    vb = K.sb(ctx, "vb", [P, TT, RW])
    qT, kT = K.sb(ctx, "gla_qT", [P, 2, S]), K.sb(ctx, "gla_kT", [P, 2, S])
    glr = K.sb(ctx, "glr", [RANK, S])

    s, v, got = K.weights(w_in, COL2_QB, 512)
    for j in range(4):
        b = K.banks.take()
        m = K.project(b, b.t[:, :], lambda k: v[:, k, j * P:(j + 1) * P], lambda k: hT[:, k, :], KD, got, ready)
        if j < 2:
            qk_ready = K.a(qT[:, j, :], b.t[:, :], ACT.Copy, m, scale=BK ** -0.5)
        else:
            qk_ready = K.a(kT[:, j - 2, :], b.t[:, :], ACT.Copy, m)
        b.free = [qk_ready]
    s.free = [m]
    s, v, got = K.weights(w_in, COL2_LR, RANK)
    b = K.banks.take()
    m = K.project(b, b.t[0:RANK, :], lambda k: v[:, k, :], lambda k: hT[:, k, :], KD, got)
    s.free = [m]
    glr_ready = K.a(glr[:, :], b.t[0:RANK, :], ACT.Copy, m)
    b.free = [glr_ready]
    L, Lc, E1, E2 = (K.sb(ctx, f"gla_{n}", [P, 2, NCH, GC + 1]) for n in ("L", "Lc", "E1", "E2"))
    ready0 = K.zero(L[:, :, :, 0:1])
    qt, kt = K.sb(ctx, "gla_qt", [P, 2, S]), K.sb(ctx, "gla_kt", [P, 2, S])
    ktm = K.sb(ctx, "gla_ktm", [P, 2, TT, P])
    A = K.sb(ctx, "gla_A", [P, 2, 2, TT, P])
    ready0 = [ready0, K.zero(A[:, :, :, :, :])]
    zs = K.sb(ctx, "gla_zs", [P, 2, NCH])
    pair = []
    for j in range(2):
        b = K.banks.take()
        m = K.mm(b.t[:, :], w2[:, j * P:(j + 1) * P], glr[:, :], glr_ready, small, b.free)
        x, t = tmp.take(), tmp.take()
        kx = K.ts(x.t[:, :], b.t[:, :], cols[:, j:j + 1], ALU.add, m, x.free)
        b.free = [kx]
        k = K.a(t.t[:, :], x.t[:, :], ACT.Abs, kx, t.free)
        k = K.a(t.t[:, :], t.t[:, :], ACT.Exp, k, scale=-1.0)
        k = K.a(t.t[:, :], t.t[:, :], ACT.Ln, k, bias=1.0)
        k = K.stt(x.t[:, :], x.t[:, :], 0.0, t.t[:, :], ALU.min, ALU.subtract, k)
        t.free = [k]
        k = K.ts(x.t[:, :], x.t[:, :], 1.0 / TEMP, ALU.mult, k)
        for n in range(NCH):
            ks = K.dve.do(lambda e, n=n, x=x, j=j: e.tensor_tensor_scan(
                L[:, j, n, 1:GC + 1], ones[:, 0:GC], x.t[:, n * GC:(n + 1) * GC], 0.0, ALU.mult, ALU.add),
                k, ones_ready, ready0)
        x.free = [ks]
        k = K.tt(Lc[:, j, :, :], L[:, j, :, :], L[:, j, :, 32:33].broadcast_to([P, NCH, GC + 1]), ALU.subtract, ks)
        e1 = K.a(E1[:, j, :, :], Lc[:, j, :, :], ACT.Exp, k)
        e2 = K.a(E2[:, j, :, :], Lc[:, j, :, :], ACT.Exp, k, scale=-1.0)
        v8 = lambda y: y.rearrange("p (n t) -> p n t", n=NCH)
        qt_r = K.tt(v8(qt[:, j, :]), v8(qT[:, j, :]), E1[:, j, :, 1:GC + 1], ALU.mult, e1, qk_ready)
        kt_r = K.tt(v8(kt[:, j, :]), v8(kT[:, j, :]), E2[:, j, :, 1:GC + 1], ALU.mult, e2, qk_ready)
        zs_r = K.tt(zs[:, j, 0:NCH - 1], E1[:, j, 0:NCH - 1, GC:GC + 1].rearrange("p n o -> p (n o)"),
                    E2[:, j, 1:NCH, 0:1].rearrange("p n o -> p (n o)"), ALU.mult, e1, e2)
        b = K.banks.take()
        for n in range(TT):
            m = K.tr(b.t[:, n * P:(n + 1) * P], kt[:, j, n * P:(n + 1) * P], kt_r, b.free, signal=(n == TT - 1))
        ktm_r = K.a(ktm[:, j, :, :], b.t[:, :].rearrange("p (n t) -> p n t", n=TT), ACT.Copy, m)
        b.free = [ktm_r]
        for hh in range(2):
            hp = slice(hh * BK, (hh + 1) * BK)
            b = K.banks.take()
            for n in range(TT):
                ts_ = slice(n * P, (n + 1) * P)
                m = K.mm(b.t[:, ts_], kt[hp, j, ts_], qt[hp, j, ts_], kt_r, qt_r, b.free, signal=(n == TT - 1))
            a_r = K.dve.do(lambda e, b=b, j=j, hh=hh: e.copy_predicated(
                A[:, j, hh, :, :], c("mask_gla").bitcast(I32).rearrange("p (x t) -> p x t", x=4),
                b.t[:, :].rearrange("p (x t) -> p x t", x=4)), m, ready0)
            b.free = [a_r]
        pair.append((qt_r, zs_r, ktm_r, a_r))
    s, v, got = K.weights(w_in, COL2_VB, 512)
    for t in range(TT):
        b = K.banks.take()
        m = K.project(b, b.t[:, :], lambda k: hT[:, k, t * P:(t + 1) * P], lambda k: v[:, k, :], KD, got)
        vb_ready = K.a(vb[:, t, :], b.t[:, :], ACT.Copy, m)
        b.free = [vb_ready]
    s.free = [m]
    s, v, got = K.weights(w_in, COL2_RG, 512)
    for f in range(4):
        b, t = K.banks.take(), tmp.take()
        m = K.project(b, b.t[:, :], lambda k: v[:, k, f * P:(f + 1) * P], lambda k: hT[:, k, :], KD, got)
        e = K.a(t.t[:, :], b.t[:, :], ACT.Sigmoid, m, t.free)
        rg_ready = K.tt(rg[:, f, :], b.t[:, :], t.t[:, :], ALU.mult, m, e)
        b.free = t.free = [rg_ready]
    s.free = [m]
    Z = K.sb(ctx, "gla_Z", [P, 2, 2 * BV])
    z_r = [K.zero(Z[:, j, :]) for j in range(2)]
    o = K.sb(ctx, "gla_o", [P, TT, RW])
    o_r = {}
    for n in range(TT):
        for j in range(2):
            qt_r, zs_r, ktm_r, a_r = pair[j]
            b = K.banks.take()
            for hh in range(2):
                h = 2 * j + hh
                K.mm(b.t[:, hh * BV:(hh + 1) * BV], A[:, j, hh, n, :], vb[:, n, h * BV:(h + 1) * BV],
                     a_r, vb_ready, b.free, start=(hh == 0), stop=False, signal=False, loose=True)
            for half in range(2):
                ch = 2 * n + half
                rows = slice(half * GC, (half + 1) * GC)
                m = K.mm(b.t[rows, 0:2 * BV], qt[:, j, n * P + half * GC:n * P + (half + 1) * GC], Z[:, j, :],
                         z_r[j], qt_r, start=False, stop=(half == 1), loose=True)
                if ch < NCH - 1:
                    b2 = K.banks.take()
                    m2 = K.mm(b2.t[:, 0:2 * BV], ktm[rows, j, n, :], vb[rows, n, 2 * j * BV:(2 * j + 2) * BV],
                              ktm_r, b2.free)
                    for hh in range(2):
                        hp, cs = slice(hh * BK, (hh + 1) * BK), slice(hh * BV, (hh + 1) * BV)
                        k = K.tt(Z[hp, j, cs], Z[hp, j, cs], b2.t[hp, cs], ALU.add, m, m2)
                    b2.free = [k]
                    z_r[j] = K.ts(Z[:, j, :], Z[:, j, :], zs[:, j, ch:ch + 1], ALU.mult, k, zs_r)
            e = K.a(o[:, n, j * 2 * BV:(j + 1) * 2 * BV], b.t[:, 0:2 * BV], ACT.Copy, m)
            b.free = [e]
            o_r[n] = e
    st = K.sb(ctx, "gla_st", [P, TT, 3, BH])
    for n in range(TT):
        t = tmp.take()
        sq = t.t[:, :].rearrange("p (h d) -> p h d", h=BH)
        o3 = o[:, n, :].rearrange("p (h d) -> p h d", h=BH)
        ms, rc, rs = (st[:, n, q, :] for q in range(3))
        k = K.a(sq, o3, ACT.Square, o_r[n], t.free)
        k = K.red(ms, sq, ALU.add, k)
        t.free = [k]
        k = K.ts(ms, ms, 1.0 / BV, ALU.mult, k, s2=RMS_EPS, op1=ALU.add)
        k = K.recip(rc, ms, k)
        k = K.a(rs, rc, ACT.Sqrt, k)
        o_r[n] = K.tt(o3, o3, spread(rs, BV), ALU.mult, k)
    for f in range(4):
        b = K.banks.take()
        for n in range(TT):
            m = K.tr(b.t[:, n * P:(n + 1) * P], o[:, n, f * P:(f + 1) * P], o_r[n], b.free, signal=(n == TT - 1))
        k = K.stt(oT[:, f, :], b.t[:, :], cols[:, 2:3], rg[:, f, :], ALU.mult, ALU.mult, m, rg_ready)
        b.free = [k]
    return k


def add_mixed(K, o1T, o2T, ready, x):
    done = [[] for _ in range(TT)]
    for half in range(2):
        s, v, got = K.weights(K.w["w_out_2"], half * 512, 512)
        for t in range(TT):
            b = K.banks.take()
            m = K.project(b, b.t[:, :], lambda k: (o1T if k < 4 else o2T)[:, k % 4, t * P:(t + 1) * P],
                          lambda k: v[:, k, :], KD, got, ready)
            xs = x[:, t, half * 512:(half + 1) * 512]
            k = K.tt(xs, xs, b.t[:, :], ALU.add, m)
            b.free = [k]
            done[t].append(k)
        s.free = [m]
    return done


def moe(K, ctx, hT, ready, h_dram, h_stored, x, x_ready, out):
    nc, w, c = K.nc, K.w, K.c
    sm = K.channel("moe_small")
    wr = K.sb(ctx, "w_router", [P, KD, XG + NE])
    br = K.sb(ctx, "b_router", [P, XG + NE])
    small = sm.dma(K.act, wr[:, :, 0:XG], w["w_router_group_2"].rearrange("(k p) n -> p k n", p=P))
    small = sm.dma(K.act, wr[:, :, XG:], w["w_router_expert_2"].rearrange("(k p) n -> p k n", p=P))
    small = sm.dma(K.act, br[:, 0:XG], w["b_router_group_2"].rearrange("o n -> (o n)").partition_broadcast(P))
    small = sm.dma(K.act, br[:, XG:], w["b_router_expert_2"].rearrange("o n -> (o n)").partition_broadcast(P))
    lg = K.sb(ctx, "logits", [P, TT, XG + NE])
    pad = K.sb(ctx, "group_pad", [P, TT, XE])
    z = K.zero(pad[:, :, :], value=NEG)
    b = K.banks.take()
    for t in range(TT):
        m = K.project(b, b.t[:, t * 36:(t + 1) * 36], lambda k: hT[:, k, t * P:(t + 1) * P], lambda k: wr[:, k, :],
                      KD, small, ready)
    k = K.tt(lg[:, :, :], b.t[:, 0:TT * 36].rearrange("p (t n) -> p t n", t=TT), spread(br[:, :], TT, 1), ALU.add, m)
    b.free = [k]
    lg_r = k
    k = K.cp(pad[:, :, 0:XG], lg[:, :, 0:XG], k, z)
    top = K.sb(ctx, "mx", [P, 2, TT, 8])
    idx = K.sb(ctx, "mi", [P, 2, TT, 8], U32)
    idf = K.sb(ctx, "mif", [P, 2, TT, 8])
    esel = K.sb(ctx, "esel", [P, TT, XE])
    t8 = K.sb(ctx, "moe_t8", [P, TT, XE])
    g1h = K.sb(ctx, "g1h", [P, TT, XE])
    e1h = K.sb(ctx, "e1h", [P, 2, TT, XE])
    s4 = K.sb(ctx, "moe_s4", [P, 8, TT])

    def best(j, src, k):
        for t in range(TT):
            k1 = K.dve.do(lambda e, t=t: e.max(top[:, j, t, :], src[:, t, :]), k)
            k1 = K.dve.do(lambda e, t=t: e.max_index(idx[:, j, t, :], top[:, j, t, :], src[:, t, :]), k1)
        return K.cp(idf[:, j, :, :], idx[:, j, :, :], k1)

    iota = spread(c("iota"), TT, 1)
    k = best(0, pad, k)
    k = K.tt(g1h[:, :, :], iota, idf[:, 0, :, 0:1].broadcast_to([P, TT, XE]), ALU.is_equal, k)
    g_r = k
    k = K.tt(t8[:, :, :], pad[:, :, :], top[:, 0, :, 0:1].broadcast_to([P, TT, XE]), ALU.subtract, k)
    k = K.a(t8[:, :, :], t8[:, :, :], ACT.Exp, k)
    k = K.red(s4[:, 0, :], t8[:, :, :], ALU.add, k)
    gw_r = K.recip(s4[:, 1, :], s4[:, 0, :], k)
    for g in range(XG):
        src = lg[:, :, XG + g * XE:XG + (g + 1) * XE]
        on = g1h[:, :, g:g + 1].broadcast_to([P, TT, XE])
        if g == 0:
            k = K.tt(esel[:, :, :], src, on, ALU.mult, g_r)
        else:
            k1 = K.tt(t8[:, :, :], src, on, ALU.mult, k, gw_r)
            k = K.tt(esel[:, :, :], esel[:, :, :], t8[:, :, :], ALU.add, k1)
    k = best(1, esel, k)
    for j in range(2):
        e_r = K.tt(e1h[:, j, :, :], iota, idf[:, 1, :, j:j + 1].broadcast_to([P, TT, XE]), ALU.is_equal, k)
    d = s4[:, 2, :]
    k = K.tt(d, top[:, 1, :, 1], top[:, 1, :, 0], ALU.subtract, k)
    k = K.a(d, d, ACT.Exp, k)
    k = K.ts(s4[:, 3, :], d, 1.0, ALU.add, k)
    k = K.recip(s4[:, 4, :], s4[:, 3, :], k)
    k = K.tt(s4[:, 5, :], s4[:, 4, :], s4[:, 1, :], ALU.mult, k)
    wt_r = K.tt(s4[:, 6, :], s4[:, 5, :], d, ALU.mult, k)
    weight = (s4[:, 5, :], s4[:, 6, :])
    mem = K.sb(ctx, "member", [P, 2, TT, NE])
    both = K.sb(ctx, "member2", [P, TT, NE])
    for j in range(2):
        for g in range(XG):
            k = K.tt(mem[:, j, :, g * XE:(g + 1) * XE], e1h[:, j, :, :], g1h[:, :, g:g + 1].broadcast_to([P, TT, XE]),
                     ALU.mult, e_r)
    k = K.tt(both[:, :, :], mem[:, 0, :, :], mem[:, 1, :, :], ALU.add, k)
    b = K.banks.take()
    for t in range(TT):
        m = K.mm(b.t[:, t * NE:(t + 1) * NE], c("before"), both[:, t, :], k, b.free, start=True, stop=(t == 0))
        for u in range(t):
            m = K.mm(b.t[:, t * NE:(t + 1) * NE], c("allones"), both[:, u, :], start=False, stop=(u == t - 1))
    for t in range(TT):
        m = K.mm(b.t[:, TT * NE:(TT + 1) * NE], c("allones"), both[:, t, :], start=(t == 0), stop=(t == TT - 1))
    cnt = K.sb(ctx, "counts", [P, 4, NE])
    n_e, tl, end, base = (cnt[:, q, :] for q in range(4))
    rank = K.sb(ctx, "rank", [P, TT, NE])
    kr = K.cp(rank[:, :, :], b.t[:, 0:TT * NE].rearrange("p (t n) -> p t n", t=TT), m)
    k = K.cp(n_e, b.t[:, TT * NE:(TT + 1) * NE], m)
    b.free = [k]
    k = K.ts(tl, n_e, 0.5, ALU.is_gt, k)
    for q in range(1, TT):
        k = K.stt(tl, n_e, P * q + 0.5, tl, ALU.is_gt, ALU.add, k)
    onesr = K.sb(ctx, "moe_ones", [P, NE])
    z = K.zero(onesr[:, :], value=1.0)
    k = K.dve.do(lambda e: e.tensor_tensor_scan(end, onesr[:, :], tl, 0.0, ALU.mult, ALU.add), k, z)
    end_r = k
    k = K.tt(base, end, tl, ALU.subtract, k)
    tile_ = K.sb(ctx, "tile_of", [P, TT, NE])
    where_ = K.sb(ctx, "slot_where", [P, 2, TT, NE])
    prod = K.sb(ctx, "pos_prod", [P, TT, NE])
    posf = K.sb(ctx, "posf", [P, 2, 2, TT])
    posi = K.sb(ctx, "posi", [P, 2, 2, TT], U32)
    kb = k
    k = K.ts(tile_[:, :, :], rank[:, :, :], P - 0.5, ALU.is_gt, kr)
    for q in range(2, TT):
        k = K.stt(tile_[:, :, :], rank[:, :, :], P * q - 0.5, tile_[:, :, :], ALU.is_gt, ALU.add, k)
    k = K.stt(rank[:, :, :], tile_[:, :, :], -float(P), rank[:, :, :], ALU.mult, ALU.add, k)
    k = K.tt(tile_[:, :, :], tile_[:, :, :], spread(base, TT, 1), ALU.add, k, kb)
    k = K.stt(where_[:, 0, :, :], tile_[:, :, :], float(P), rank[:, :, :], ALU.mult, ALU.add, k)
    k = K.stt(where_[:, 1, :, :], rank[:, :, :], float(NTILE), tile_[:, :, :], ALU.mult, ALU.add, k)
    for q in range(2):
        for j in range(2):
            k = K.tt(prod[:, :, :], mem[:, j, :, :], where_[:, q, :, :], ALU.mult, k)
            k = K.red(posf[:, q, j, :], prod[:, :, :], ALU.add, k)
    pos_r = K.cp(posi[:, :, :, :], posf[:, :, :, :], k)
    cmp_ = K.sb(ctx, "tile_cmp", [P, NTILE, NE])
    tef = K.sb(ctx, "tile_ef", [P, NTILE])
    tei = K.sb(ctx, "tile_ei", [P, NTILE], I32)
    k = K.tt(cmp_[:, :, :], spread(end, NTILE, 1), spread(c("tile_no"), NE, 2), ALU.is_le, end_r)
    k = K.red(tef[:, :], cmp_[:, :, :], ALU.add, k)
    k = K.ts(tef[:, :], tef[:, :], float(NE - 1), ALU.min, k)
    te_r = K.cp(tei[:, :], tef[:, :], k)

    tab = nc.dram_tensor("slot_token", (NTILE * P, 1), U32, kind="Internal").ap()
    zt = K.sb(ctx, "zero_tab", [P, NTILE], U32)
    tok = K.sb(ctx, "tokens", [P, TT], U32)
    slot_tok = K.sb(ctx, "slot_tok", [P, NTILE], U32)
    k = K.zero(zt[:, :], lane=K.dve, value=0)
    z_s = K.store(tab.rearrange("(p t) o -> p (t o)", p=P), zt[:, :], k)
    k = K.cp(tok[:, :], c("token_no"))
    sc = K.channel("scatter")
    K.pool.wait(z_s, k, pos_r)
    for j in range(2):
        for t in range(TT):
            sc.count += 16
            K.pool.queue.append(lambda e, j=j, t=t: e.indirect_dma_start(
                out=tab[:, :], out_offset=bass.IndirectOffsetOnAxis(ap=posi[:, 1, j, t:t + 1], axis=0),
                in_=tok[:, t:t + 1], in_offset=None).then_inc(sc.sem, 16))
    sc_r = (sc.sem, sc.count)
    K.stores.append(sc_r)
    st_r = K.channel("slot_tok_in").dma(K.pool, slot_tok[:, :], tab.rearrange("(p t) o -> p (t o)", p=P), sc_r)

    ys = nc.dram_tensor("slot_out", (NTILE * P, D), F32, kind="Internal").ap()
    wg, wu, wd = w["w_exp_gate_2"], w["w_exp_up_2"], w["w_exp_down_2"]
    gring = K.ring(ctx, "gath", 3, [P, D], channels=True)
    dring = K.ring(ctx, "wd", 2, [P, 2, D], channels=True)
    hgT = K.ring(ctx, "hgT", 2, [P, KD, P])
    hd = K.ring(ctx, "hid", 2, [P, 2, DE])
    hdT = K.ring(ctx, "hidT", 2, [P, 2, P])
    yr = K.ring(ctx, "yout", 2, [P, D], channels=True)
    gathered, wts = {}, {}
    y_stored = []

    def gather(n):
        g = gring.take()
        K.pool.wait(st_r, g.free, h_stored)
        g.channel.count += 16
        K.pool.queue.append(lambda e, g=g, n=n: e.indirect_dma_start(
            out=g.t[:, :], out_offset=None, in_=h_dram[:, :],
            in_offset=bass.IndirectOffsetOnAxis(ap=slot_tok[:, n:n + 1], axis=0)).then_inc(g.channel.sem, 16))
        gathered[n] = (g, (g.channel.sem, g.channel.count))

    def fetch(n):
        s, s2 = K.wring.take(), dring.take()
        K.sp.wait(te_r, s.free, s2.free)
        v = s.t[:, :].rearrange("p (two k n) -> p two k n", two=2, k=KD)
        s.channel.count += 32
        s2.channel.count += 16

        def issue(e, n=n, s=s, s2=s2, v=v):
            r = e.value_load(tei[0:1, n:n + 1], min_val=0, max_val=NE - 1)
            for two, src in ((0, wg), (1, wu)):
                e.dma_start(v[:, two, :, :], src[bass.ds(r, 1), :, :].rearrange("o (p k) n -> p (o k) n", k=KD)
                            ).then_inc(s.channel.sem, 16)
            e.dma_start(s2.t[:, :, :], wd[bass.ds(r, 1), :, :].rearrange("o (p k) n -> p (o k) n", k=2)
                        ).then_inc(s2.channel.sem, 16)
        K.sp.queue.append(issue)
        wts[n] = (s, v, (s.channel.sem, s.channel.count), s2, (s2.channel.sem, s2.channel.count))

    hidden = {}

    def up(n):
        g, g_r = gathered.pop(n)
        s, v, w_r, s2, d_r = wts[n]
        t = hgT.take()
        for half in range(2):
            b = K.banks.take()
            for j in range(4):
                q = half * 4 + j
                m = K.tr(b.t[:, j * P:(j + 1) * P], g.t[:, q:D:KD], g_r, b.free, signal=(j == 3))
            src = b.t[:, :].rearrange("p (k n) -> p k n", k=4)
            e = K.a(t.t[:, half * 4:half * 4 + 4, :], src, ACT.Copy, m, t.free) if half else \
                K.cp(t.t[:, 0:4, :], src, m, t.free)
            b.free = [e]
            if half == 0:
                e0 = e
        g.free = [m]
        b = K.banks.take()
        m = K.project(b, b.t[:, :].rearrange("p (two n) -> p two n", two=2), lambda k: t.t[:, k, :],
                      lambda k: v[:, :, k, :], KD, w_r, e, e0)
        s.free = [m]
        t.free = [m]
        hb = hd.take()
        k = K.a(hb.t[:, 0, :], b.t[:, 0:DE], ACT.Sigmoid, m, hb.free)
        k = K.tt(hb.t[:, 0, :], hb.t[:, 0, :], b.t[:, 0:DE], ALU.mult, k)
        k = K.tt(hb.t[:, 1, :], hb.t[:, 0, :], b.t[:, DE:2 * DE], ALU.mult, k)
        b.free = [k]
        hidden[n] = (hb, k)

    def down(n):
        hb, k = hidden.pop(n)
        s, v, w_r, s2, d_r = wts.pop(n)
        ht, yb = hdT.take(), yr.take()
        b = K.banks.take()
        for j in range(2):
            m = K.tr(b.t[:, j * P:(j + 1) * P], hb.t[:, 1, j:DE:2], k, b.free, signal=(j == 1))
        hb.free = [m]
        e = K.cp(ht.t[:, :, :], b.t[:, 0:2 * P].rearrange("p (k n) -> p k n", k=2), m, ht.free)
        b.free = [e]
        for half in range(2):
            b = K.banks.take()
            m = K.project(b, b.t[:, :], lambda k: ht.t[:, k, :], lambda k: s2.t[:, k, half * 512:(half + 1) * 512],
                          2, d_r, e)
            dst = yb.t[:, half * 512:(half + 1) * 512]
            q = K.a(dst, b.t[:, :], ACT.Copy, m, yb.free) if half else K.cp(dst, b.t[:, :], m, yb.free)
            b.free = [q]
            if half == 0:
                q0 = q
        ht.free = s2.free = [m]
        t = K.store(ys[n * P:(n + 1) * P, :], yb.t[:, :], q, q0, lane=K.act, channel=yb.channel)
        yb.free = [t]
        y_stored.append(t)

    for n in range(NTILE + 1):
        if n < NTILE:
            fetch(n)
            gather(n)
            up(n)
        if n >= 1:
            down(n - 1)

    fin = K.ring(ctx, "fin", 2, [P, 2, D], channels=True)
    for t in range(TT):
        s = fin.take()
        K.pool.wait(y_stored[-2:], s.free)
        for j in range(2):
            s.channel.count += 16
            K.pool.queue.append(lambda e, s=s, j=j, t=t: e.indirect_dma_start(
                out=s.t[:, j, :], out_offset=None, in_=ys[:, :],
                in_offset=bass.IndirectOffsetOnAxis(ap=posi[:, 0, j, t:t + 1], axis=0)).then_inc(s.channel.sem, 16))
        k = (s.channel.sem, s.channel.count)
        for j in range(2):
            k = K.stt(x[:, t, :], s.t[:, j, :], weight[j][:, t:t + 1], x[:, t, :], ALU.mult, ALU.add, k, wt_r, x_ready[t])
        s.free = [k]
        K.store(out[t * P:(t + 1) * P, :], x[:, t, :], k)


def build(nc, w, consts, dist, where, out, probes=()):
    with ExitStack() as ctx:
        K = Core(nc, ctx, w)
        K.where = where
        K.probe = dict(probes)
        K.banks = Ring([Slot(ctx.enter_context(nc.psum_tensor(f"bank{i}", [P, 512], F32))) for i in range(8)])
        K.consts = K.sb(ctx, "consts", [P, consts.shape[1]])
        K.dist_dram = dist
        x = K.sb(ctx, "x_res", [P, TT, D])
        hT = K.sb(ctx, "hT", [P, KD, S])
        oaT, obT = K.sb(ctx, "oaT", [P, 4, S]), K.sb(ctx, "obT", [P, 4, S])
        K.wring = K.ring(ctx, "w", 3, [P, 8 * 512], channels=True)
        xin = [K.channel(f"x_in{t}").dma(K.sp, x[:, t, :], w["x"][t * P:(t + 1) * P, :]) for t in range(TT)]
        K.consts_ready = K.channel("const_in").dma(K.act, K.consts[:, :], consts)
        for lane in (K.pe, K.act, K.dve, K.pool):
            lane.wait(K.consts_ready)

        gch = K.channel("gain_in")

        def normed(name, gname, ready, keep=None):
            with ExitStack() as c2:
                gain = K.sb(c2, "norm_gain", [P, D])
                g = gch.dma(K.act, gain[:, :], w[gname].rearrange("o n -> (o n)").partition_broadcast(P))
                done = K.norm_to_fm(c2, name, x, gain[:, :], g, ready, hT, K.pe.last(), keep)
                K.meet()
            return done

        def probe(name, ap):
            if name in K.probe:
                K.meet()
                K.sp.wait([t for t in K.met if t])
                K.store(K.probe[name], ap)

        ready = normed("n1", "attn_norm_g", xin)
        probe("hT", hT[:, :, :])
        with ExitStack() as c2:
            oa = nsa(K, c2, hT, ready, oaT, obT)
            K.meet()
        probe("oaT", oaT[:, :, :])
        with ExitStack() as c2:
            ob = rwkv(K, c2, hT, ready, obT)
            K.meet()
        probe("obT", obT[:, :, :])
        with ExitStack() as c2:
            K.more_weights(c2)
            done = merge(K, c2, hT, oaT, obT, oa, ob, x)
            K.meet()
        probe("x1", x[:, :, :])
        ready = normed("n2", "ffn_norm_g", done)
        with ExitStack() as c2:
            K.more_weights(c2)
            done = ffn(K, c2, hT, ready, x)
            K.meet()
        probe("x2", x[:, :, :])
        ready = normed("n3", "norm1_g_2", done)
        with ExitStack() as c2:
            K.more_weights(c2)
            oa = selected_attention(K, c2, hT, ready, oaT, obT)
            K.meet()
        probe("o2aT", oaT[:, :, :])
        with ExitStack() as c2:
            K.more_weights(c2)
            ob = gla(K, c2, hT, ready, obT)
            K.meet()
        probe("o2bT", obT[:, :, :])
        done = add_mixed(K, oaT, obT, [oa, ob], x)
        probe("x3", x[:, :, :])
        h_dram = nc.dram_tensor("h_rows", (S, D), F32, kind="Internal").ap()
        n_stores = len(K.stores)
        ready = normed("n4", "norm2_g_2", done, keep=h_dram)
        h_stored = K.stores[n_stores:]
        with ExitStack() as c2:
            K.more_weights(c2)
            moe(K, c2, hT, ready, h_dram, h_stored, x, done, out)
            K.meet()
        K.sp.wait(K.stores)

        block = ctx.enter_context(nc.Block())
        block.sync(K.sp.run)
        block.scalar(K.act.run)
        block.gpsimd(K.pool.run)
        block.vector(K.dve.run)
        block.tensor(K.pe.run)


_INS = [
    "x", "attn_norm_g", "w_in", "rel_bias", "q_norm_g", "k_norm_g", "cmp_pe_k", "cmp_w1_k", "cmp_w2_k",
    "cmp_pe_v", "cmp_w1_v", "cmp_w2_v", "rwkv_mu", "rwkv_w0", "rwkv_w2", "rwkv_a0", "rwkv_a2", "rwkv_g2",
    "rwkv_k_k", "rwkv_k_a", "rwkv_r_k", "rwkv_ln_g", "rwkv_ln_b", "w_proj_a", "w_proj_b", "w_out",
    "ffn_norm_g", "w_up", "conv_w", "conv_b", "w_down", "norm1_g_2", "w_in_2", "q_norm_g_2", "k_norm_g_2",
    "rel_bias_2", "gla_gate_w2_2", "gla_gate_b_2", "gla_out_norm_g_2", "w_out_2", "norm2_g_2",
    "w_router_group_2", "b_router_group_2", "w_router_expert_2", "b_router_expert_2", "w_exp_gate_2",
    "w_exp_up_2", "w_exp_down_2",
]


def kernel(**inputs):
    import concourse.bacc as _bacc
    from concourse.bass_utils import run_bass_kernel_spmd as _run

    nc = _bacc.Bacc("TRN2", target_bir_lowering=False, num_devices=1)
    arrays, w = {}, {}
    for name in _INS:
        a = np.ascontiguousarray(inputs[name])
        if a.shape[0] == 1 and a.ndim > 2:
            a = a.reshape(a.shape[1:])
        arrays[f"in_{name}"] = a
        w[name] = nc.dram_tensor(f"in_{name}", a.shape, mybir.dt.from_np(a.dtype), kind="ExternalInput").ap()
    table, where = constants()
    for name, a in (("consts", table), ("dist", distance_tables())):
        arrays[f"in_{name}"] = a
        w[name] = nc.dram_tensor(f"in_{name}", a.shape, F32, kind="ExternalInput").ap()
    out = nc.dram_tensor("out_x", (S, D), F32, kind="ExternalOutput").ap()
    build(nc, w, w.pop("consts"), w.pop("dist"), where, out)
    r = _run(nc, [arrays], core_ids=[0])
    return r.results[0]["out_x"].reshape(1, S, D)
```

```python
import math
from contextlib import ExitStack

import numpy as np

import concourse.bass as bass
from concourse import mybir

F32 = mybir.dt.float32
F32R = mybir.dt.float32r
BF16 = mybir.dt.bfloat16
I32 = mybir.dt.int32
U32 = mybir.dt.uint32
ALU = mybir.AluOpType
ACT = mybir.ActivationFunctionType
AX = mybir.AxisListType.X

P = 128
S, D = 512, 1024
TT = S // P
KD = D // P
NEG = -1e30
TAKEN = -3e38
RMS_EPS = 1e-6

DH, NH, NG, NR = 64, 8, 2, 4
KVW = NG * DH
CB, CS, CHID = 32, 16, 256
NC = S // CS - CB // CS + 1
NW = NH * DH
COL_Q, COL_KC = 0, NW
COL_VC, COL_KS, COL_VS, COL_KW, COL_VW = (COL_KC + i * KVW for i in range(1, 6))
COL_GATE = COL_KC + 6 * KVW
COL_R = COL_GATE + 3 * NH
RW = 512
COL_K, COL_V, COL_LORA = COL_R + RW, COL_R + 2 * RW, COL_R + 3 * RW
COL_GA = COL_LORA + 256
COL_GB = COL_GA + D
DFF = 2816
FT = DFF // P
GN_EPS = 64e-5
DECAY = math.exp(-0.5)
NORM_FLOOR = 1e-24
LN_SHIFT = 20
IH, ID, TOPK = 8, 32, 128
COL2_Q, COL2_K, COL2_V, COL2_IQ = 0, 512, 1024, 1536
COL2_IK = COL2_IQ + IH * ID
COL2_IW = COL2_IK + ID
COL2_QB = COL2_IW + IH
COL2_KB = COL2_QB + 256
COL2_VB = COL2_KB + 256
COL2_LR = COL2_VB + 512
COL2_RG = COL2_LR + 16
BH, BK, BV, RANK, TEMP, GC = 4, 64, 128, 16, 16.0, 64
XG, XE, NE, DE = 4, 8, 32, 256
NTILE = 2 * S // P + NE - 1


def t5_bucket(n):
    large = 16 + (np.log(np.maximum(n, 1).astype(np.float32) / np.float32(16)) / np.float32(math.log(8))
                  * np.float32(16)).astype(np.int32)
    return np.where(n < 16, n, np.minimum(large, 31))


def level_mask(m):
    i = np.arange(P)
    return ((i[:, None] // (2 * m) == i[None, :] // (2 * m))
            & (i[:, None] // m % 2 == 1) & (i[None, :] // m % 2 == 0)).astype(np.float32)


def constants():
    i = np.arange(P)
    parts = {}
    parts["ident"] = np.eye(P)
    parts["ones64"] = (i[:, None] // 64 == i[None, :] // 64) * 1.0
    parts["allones"] = np.ones((P, P))
    parts["before"] = (i[:, None] < i[None, :]) * 1.0
    strict, upto = (i[:, None] < i[None, :]) * 1.0, (i[:, None] <= i[None, :]) * 1.0
    parts["mask_rw"] = np.concatenate([strict, upto, strict, upto], 1)
    parts["mask_low4"] = np.tile(strict.T, (1, 4))
    same = i[:, None] // GC == i[None, :] // GC
    parts["mask_gla"] = np.tile(upto * same, (1, 4))
    parts["lev0u"] = level_mask(1).T
    for lv in range(7):
        parts[f"lev{lv}"] = level_mask(1 << lv)
    parts["valid_c"] = np.stack([(i + P * t >= CB - 1) * 1.0 for t in range(TT)], 1)
    parts["iota"] = np.tile(np.arange(XE * 1.0), (P, 1))
    parts["tile_no"] = np.tile(np.arange(NTILE * 1.0), (P, 1))
    parts["token_no"] = i[:, None] + P * np.arange(TT)[None, :] * 1.0
    parts["eps"] = np.full((P, 1), RMS_EPS)
    parts["gn_eps"] = np.full((P, 1), GN_EPS)
    parts["ln_back"] = np.full((P, 1), 0.5 * LN_SHIFT * math.log(2.0))
    where, at = {}, 0
    for k, v in parts.items():
        where[k] = (at, at + v.shape[1])
        at += v.shape[1]
    return np.concatenate(list(parts.values()), 1).astype(np.float32), where


def distance_tables():
    def one_hot(n):
        t = np.zeros((33, n.size), np.float32)
        t[t5_bucket(np.maximum(n, 0)), np.arange(n.size)] = n >= 0
        t[32] = np.where(n < 0, np.float32(NEG), 0)
        return t
    return np.concatenate([one_hot(np.arange(1024) - 511), one_hot(np.arange(640) - 127)], 1)


class Lane:

    def __init__(self, sem, one_at_a_time=False):
        self.sem, self.count, self.queue, self.seen = sem, 0, [], {}
        self.one_at_a_time = one_at_a_time

    def wait(self, *tokens):
        for t in tokens:
            if t is None:
                continue
            if isinstance(t, list):
                self.wait(*t)
                continue
            sem, value = t
            if self.seen.get(id(sem), 0) < value:
                self.seen[id(sem)] = value
                self.queue.append(lambda eng, s=sem, v=value: eng.wait_ge(s, v))

    def do(self, make, *after, signal=True):
        self.wait(*after)
        if self.one_at_a_time:
            self.wait(self.last())
        if not signal:
            self.queue.append(make)
            return None
        self.count += 1
        self.queue.append(lambda eng, m=make, s=self.sem: m(eng).then_inc(s, 1))
        return (self.sem, self.count)

    def last(self):
        return (self.sem, self.count) if self.count else None

    def run(self, eng):
        for f in self.queue:
            f(eng)


class Channel:

    def __init__(self, sem):
        self.sem, self.count = sem, 0

    def dma(self, lane, out, in_, *after, slow=False):
        lane.wait(*after)
        self.count += 16
        lane.queue.append(lambda eng, s=self.sem: eng.dma_start(
            out, in_, allow_slow_non_contiguous=slow).then_inc(s, 16))
        return (self.sem, self.count)


class Slot:
    def __init__(self, t, channel=None):
        self.t, self.channel, self.free = t, channel, []


class Ring:

    def __init__(self, slots):
        self.slots, self.n = slots, 0

    def take(self):
        s = self.slots[self.n % len(self.slots)]
        self.n += 1
        return s


class Core:

    def __init__(self, nc, ctx, w):
        self.nc, self.ctx, self.w = nc, ctx, w
        self.names = {}
        self.pe, self.act, self.dve, self.pool, self.sp = (
            Lane(self.sem(f"done_{n}"), one_at_a_time=(n == "pool")) for n in ("pe", "act", "dve", "pool", "sp"))
        self.stores, self.deferred, self.side = [], [], []
        self.more_channel = self.channel("in_w_more")

    def fresh(self, name):
        self.names[name] = self.names.get(name, 0) + 1
        return name if self.names[name] == 1 else f"{name}_{self.names[name]}"

    def sem(self, name):
        name = self.fresh("sem " + name).replace("sem ", "")
        return self.ctx.enter_context(self.nc.semaphore(name))

    def channel(self, name):
        return Channel(self.sem(name))

    def sb(self, ctx, name, shape, dt=F32):
        name = self.fresh(name)
        return ctx.enter_context(self.nc.sbuf_tensor(name, shape, dt))

    def ring(self, ctx, name, n, shape, dt=F32, channels=False):
        return Ring([Slot(self.sb(ctx, f"{name}{i}", shape, dt),
                          self.channel(f"in_{name}{i}") if channels else None) for i in range(n)])

    def mm(self, out, lhsT, rhs, *after, start=True, stop=True, signal=True, loose=False):
        return self.pe.do(lambda e: e.matmul(out, lhsT, rhs, start=start, stop=stop, skip_group_check=loose),
                          *after, signal=signal)

    def tr(self, out, in_, *after, signal=True):
        n = in_.shape[0]
        return self.pe.do(lambda e: e.transpose(out, in_, self.c("ident")[0:n, 0:n]), *after, signal=signal)

    def a(self, out, in_, func, *after, bias=None, scale=None, accum=None):
        kw = {k: v for k, v in (("bias", bias), ("scale", scale), ("accum_out", accum)) if v is not None}
        return self.act.do(lambda e: e.activation(out, in_, func, **kw), *after)

    def tt(self, out, x, y, op, *after, lane=None):
        return (lane or self.dve).do(lambda e: e.tensor_tensor(out, x, y, op), *after)

    def ts(self, out, x, s1, op0, *after, s2=None, op1=None, lane=None):
        if op1 is None:
            return (lane or self.dve).do(lambda e: e.tensor_scalar(out, x, s1, None, op0), *after)
        return (lane or self.dve).do(lambda e: e.tensor_scalar(out, x, s1, s2, op0, op1), *after)

    def stt(self, out, x, s, y, op0, op1, *after):
        return self.dve.do(lambda e: e.scalar_tensor_tensor(out=out, in0=x, scalar=s, in1=y, op0=op0, op1=op1),
                           *after)

    def cp(self, out, x, *after, lane=None):
        return (lane or self.dve).do(lambda e: e.tensor_copy(out, x), *after)

    def red(self, out, x, op, *after):
        return self.dve.do(lambda e: e.tensor_reduce(out, x, AX, op), *after)

    def recip(self, out, x, *after):
        return self.dve.do(lambda e: e.reciprocal(out, x), *after)

    def zero(self, out, *after, lane=None, value=0.0):
        return (lane or self.pool).do(lambda e: e.memset(out, value), *after)

    def c(self, name):
        lo, hi = self.where[name]
        return self.consts[:, lo:hi]

    def store(self, out, in_, *after, lane=None, channel=None):
        ch = channel or self.channel(f"store{len(self.stores)}")
        t = ch.dma(lane or self.sp, out, in_, *after)
        self.stores.append(t)
        return t

    def meet(self):
        self.flush()
        tokens = [x.last() for x in (self.pe, self.act, self.dve, self.pool)]
        for lane in (self.pe, self.act, self.dve, self.pool):
            lane.wait([t for t in tokens if t])
        self.met = tokens

    def load_distances(self, ctx):
        self.dist = self.sb(ctx, "dist", list(self.dist_dram.shape))
        self.dist_ready = self.channel("dist_in").dma(self.act, self.dist[:, :], self.dist_dram, self.dve.last())

    def more_weights(self, ctx):
        s = Slot(self.sb(ctx, "w_more", [P, 8 * 512]), self.more_channel)
        s.free = [t for t in self.met if t]
        ring, base = self.wring, list(self.wring.slots)
        at = ring.n % len(base)
        self.wring = Ring(base[at:] + base[:at] + [s])
        ctx.callback(self.fewer_weights)

    def fewer_weights(self):
        ring = self.wring
        at = ring.n % 4
        order = ring.slots[at:] + ring.slots[:at]
        self.wring = Ring([s for s in order if s.channel is not self.more_channel])

    def load(self, slot, parts, *after):
        for out, in_ in parts:
            t = slot.channel.dma(self.sp, out, in_, slot.free, *after)
        slot.free = []
        return t

    def weights(self, src, at, n, ktiles=KD):
        s = self.wring.take()
        v = s.t[:, 0:ktiles * n].rearrange("p (k n) -> p k n", k=ktiles)
        return s, v, self.load(s, [(v, src.rearrange("(k p) n -> p k n", p=P)[:, :, at:at + n])])

    def later(self, make):
        out = []
        self.deferred.append((make, out))
        return out

    def flush(self):
        jobs, self.deferred = self.deferred, []
        for make, out in jobs:
            out.append(make())

    def fill(self, steps):
        while steps and self.side:
            try:
                next(self.side[0])
                steps -= 1
            except StopIteration:
                self.side.pop(0)

    def drain_side(self):
        while self.side:
            self.fill(1)

    def project(self, bank, out, lhs, rhs, n, *after):
        for k in range(n):
            t = self.mm(out, lhs(k), rhs(k), *((bank.free,) + after if k == 0 else ()),
                        start=(k == 0), stop=(k == n - 1), signal=(k == n - 1))
        bank.free = []
        self.flush()
        return t

    def halves(self, hi, lo, src, *after):
        k = self.a(hi, src, ACT.Copy, *after)
        return self.tt(lo, src, hi, ALU.subtract, k)

    def cut_ring(self, ctx, n):
        self.cuts = self.ring(ctx, "cut", n, [P, 2, 1024], F32R)

    def cut(self, src, *after):
        s = self.cuts.take()
        a, b = src.shape[1:]
        hi, lo = (s.t[:, j, 0:a * b].rearrange("p (a b) -> p a b", a=a) for j in range(2))
        return s, (hi, lo), self.halves(hi, lo, src, s.free, *after)

    def mm3(self, out, lhsT, rhs, *after, start, stop, signal):
        self.mm(out, lhsT[0], rhs[0], *after, start=start, stop=False, signal=False)
        self.mm(out, lhsT[0], rhs[1], start=False, stop=False, signal=False)
        return self.mm(out, lhsT[1], rhs[0], start=False, stop=stop, signal=signal)

    def project3(self, bank, out, lhs, rhs, n, *after):
        for k in range(n):
            t = self.mm3(out, lhs(k), rhs(k), *((bank.free,) + after if k == 0 else ()),
                         start=(k == 0), stop=(k == n - 1), signal=(k == n - 1))
        bank.free = []
        self.flush()
        return t

    def norm_to_fm(self, ctx, name, x, gain, gain_ready, ready, hT, hT_free, keep=None):
        junk = self.ring(ctx, f"{name}_h", 2, [P, D])
        st = self.sb(ctx, f"{name}_st", [P, 4 * TT])
        done = []
        for t in range(TT):
            s = junk.take()
            ss, ms, rc, rs = (st[:, 4 * t + j:4 * t + j + 1] for j in range(4))
            k = self.a(s.t[:, :], x[:, t, :], ACT.Square, ready[t], s.free, accum=ss)
            k = self.ts(ms, ss, 1.0 / D, ALU.mult, k, s2=RMS_EPS, op1=ALU.add)
            k = self.recip(rc, ms, k)
            k = self.a(rs, rc, ACT.Sqrt, k)
            k = self.stt(s.t[:, :], x[:, t, :], rs, gain, ALU.mult, ALU.mult, k, gain_ready)
            s.free = []
            if keep:
                s.free.append(self.store(keep[t * P:(t + 1) * P, :], s.t[:, :], k))
            for half in range(2):
                b = self.banks.take()
                for j in range(4):
                    f = half * 4 + j
                    m = self.tr(b.t[:, j * P:(j + 1) * P], s.t[:, f * P:(f + 1) * P], k,
                                b.free if j == 0 else None, signal=(j == 3))
                src = b.t[:, :].rearrange("p (k n) -> p k n", k=4)
                at = (slice(None), slice(half * 4, half * 4 + 4), slice(t * P, (t + 1) * P))
                e = self.halves(hT[0][at], hT[1][at], src, m, hT_free) if isinstance(hT, tuple) else \
                    self.cp(hT[at], src, m, hT_free)
                b.free = [e]
                done.append(e)
            s.free.append(m)
        return done

    def to_fm(self, o, o_ready, oT):
        for f in range(4):
            b = self.banks.take()
            for t in range(TT):
                m = self.tr(b.t[:, t * P:(t + 1) * P], o[:, t, f * P:(f + 1) * P], o_ready[t], b.free,
                            signal=(t == TT - 1))
            k = self.a(oT[:, f, :], b.t[:, :], ACT.Copy, m)
            b.free = [k]
        return k

    def head_norm(self, tmp, bank, got, out, gain, n=S):
        raw, sq, e = tmp.take(), tmp.take(), tmp.take()
        k0 = self.cp(raw.t[:, 0:n], bank.t[:, 0:n], got, raw.free)
        k1 = self.a(sq.t[:, 0:n], raw.t[:, 0:n], ACT.Square, k0, sq.free)
        bank.free = [k0]

        def rest():
            b = self.banks.take()
            m = self.mm(b.t[:, 0:n], self.c("ones64"), sq.t[:, 0:n], k1, b.free)
            sq.free = [m]
            k = self.a(e.t[:, 0:n], b.t[:, 0:n], ACT.Ln, m, e.free, scale=1.0 / DH, bias=self.c("eps"))
            b.free = [k]
            k = self.a(e.t[:, 0:n], e.t[:, 0:n], ACT.Exp, k, scale=-0.5)
            k = self.stt(out, raw.t[:, 0:n], gain, e.t[:, 0:n], ALU.mult, ALU.mult, k, k0)
            raw.free = e.free = [k]
            return k
        return self.later(rest)

    def bias_table(self, ctx, name, rel_bias, big, relb_tile):
        ch = self.channel(f"{name}_relb")
        z = self.zero(relb_tile[32:33, :], value=1.0)
        r = ch.dma(self.act, relb_tile[0:32, :], rel_bias)
        row = self.sb(ctx, f"{name}_row", [NH, 640])
        for lo, hi in ((0, 512), (512, 640)):
            b = self.banks.take()
            m = self.mm(b.t[0:NH, 0:hi - lo], relb_tile[:, :], self.dist[:, 1024 + lo:1024 + hi],
                        b.free, r, z, self.dist_ready)
            k = self.cp(row[:, lo:hi], b.t[0:NH, 0:hi - lo], m)
            b.free = [k]
        dram = self.nc.dram_tensor(f"{name}_dram", (NH, 640), F32, kind="Internal").ap()
        k = self.store(dram, row[:, :], k)
        skew = bass.AP(tensor=dram.tensor, offset=0, ap=[[1, P], [640, NH], [1, 512]])
        return self.channel(f"{name}_skew").dma(self.sp, big[:, :, :], skew, k), [r, z]

    def attention(self, ctx, name, branches, big):
        sc, pr, pt = (self.ring(ctx, f"{name}_{x}", 3, [P, S]) for x in ("s", "p", "t"))
        st = self.sb(ctx, f"{name}_stat", [P, len(branches), TT, 2, NH])
        ring_s, ring_t, ring_o = (Ring([self.banks.slots[j] for j in js]) for js in ((0, 1, 2), (3, 4, 5), (6, 7)))
        units = [(b, i, h) for b in range(len(branches)) for pair in ((3, 0), (2, 1)) for h in range(NH) for i in pair]
        probs, turned, outs, sums = {}, {}, {}, {}

        def score(br, i, h):
            q, kk, v, ready, finish, extra = branches[br]
            n = (i + 1) * P
            b, s, p = ring_s.take(), sc.take(), pr.take()
            got = self.mm(b.t[:, 0:n], q(h)[:, i * P:(i + 1) * P], kk(h)[:, 0:n], b.free, ready,
                          start=True, stop=not extra or i == 0)
            if extra and i:
                got = extra(i, b.t[:, 0:n])
            low = st[:, br, i, 0, h:h + 1]
            k = self.dve.do(lambda e: e.tensor_tensor_reduce(
                out=s.t[:, 0:n], in0=b.t[:, 0:n], in1=reversed_(big[:, h, 0:n]), scale=-1.0, scalar=3e38,
                op0=ALU.add, op1=ALU.min, accum_out=low), got, s.free)
            b.free = [k]
            k = self.a(p.t[:, 0:n], s.t[:, 0:n], ACT.Exp, k, p.free, scale=-1.0, bias=low,
                       accum=st[:, br, i, 1, h:h + 1])
            s.free = [k]
            sums[br, i] = k
            probs[br, i, h] = (p, k)

        def turn(br, i, h):
            n = (i + 1) * P
            p, k = probs.pop((br, i, h))
            b, w = ring_t.take(), pt.take()
            for j in range(i + 1):
                m = self.tr(b.t[:, j * P:(j + 1) * P], p.t[:, j * P:(j + 1) * P], k, b.free, signal=(j == i))
            p.free = [m]
            if h % 2:
                k = self.a(w.t[:, 0:n], b.t[:, 0:n], ACT.Copy, m, w.free)
            else:
                k = self.cp(w.t[:, 0:n], b.t[:, 0:n], m, w.free)
            b.free = [k]
            turned[br, i, h] = (w, k)

        def combine(br, i, h):
            v, finish = branches[br][2], branches[br][4]
            w, k = turned.pop((br, i, h))
            if h == 0:
                outs[br, i] = ring_o.take()
            b = outs[br, i]
            for j in range(i + 1):
                m = self.mm(b.t[:, h * DH:(h + 1) * DH], w.t[:, j * P:(j + 1) * P], v(h, j), k, b.free,
                            start=(j == 0), stop=(j == i), signal=(j == i))
            b.free = []
            w.free = [m]
            if h == NH - 1:
                b.free = [finish(i, b, m, st[:, br, i, 1, :], sums[br, i])]

        for n in range(len(units) + 3):
            if n < len(units):
                score(*units[n])
            if 0 <= n - 2 < len(units):
                turn(*units[n - 2])
            if 0 <= n - 3 < len(units):
                combine(*units[n - 3])


def spread(ap, m, axis=2):
    shape = list(ap.shape)
    return ap.unsqueeze(axis).broadcast_to(shape[:axis] + [m] + shape[axis:])


def reversed_(ap):
    (pstep, p), (step, n) = ap.ap
    return bass.AP(tensor=ap.tensor, offset=ap.offset + step * (n - 1), ap=[[pstep, p], [-step, n]])


def nsa(K, outer, hT, ready, oT, spare):
    w, c = K.w, K.c
    w_in = w["w_in"]
    sm = K.channel("nsa_small")
    ctx = ExitStack()
    qT = K.sb(outer, "qT", [P, NR, S])
    ksT, kwT = K.sb(outer, "ksT", [P, S]), K.sb(outer, "kwT", [P, S])
    vs, vw = K.sb(outer, "vs", [P, TT, KVW]), K.sb(outer, "vw", [P, TT, KVW])
    x2 = oT[:, :, :].rearrange("p (j g) t -> p j g t", j=2)
    gate = K.sb(outer, "nsa_gate", [P, TT, 3 * NH])
    big = K.sb(outer, "nsa_bias", [P, NH, 512])
    relb = K.sb(outer, "nsa_relb", [33, NH])
    raw = K.sb(ctx, "cmp_raw", [P, 2, S])
    o = spare
    tmp = K.ring(ctx, "nsa_tmp", 6, [P, S])
    gains = K.sb(ctx, "nsa_gains", [P, 2])
    pe_in = K.sb(ctx, "pe_in", [16, 2, P])
    peT = K.sb(ctx, "peT", [P, 2, 16])
    w2k, w2v = K.sb(ctx, "w2k", [P, 2, 2, DH]), K.sb(ctx, "w2v", [P, 2, DH])

    for half in range(2):
        for j, name in enumerate(("q_norm_g", "k_norm_g")):
            small = sm.dma(K.act, gains[half * DH:(half + 1) * DH, j:j + 1], w[name].rearrange("o d -> d o"), slow=True)
        small = sm.dma(K.act, w2k[:, :, half, :], w["cmp_w2_k"].rearrange("(k p) d -> p k d", p=P))
    small = sm.dma(K.act, w2v[:, :, :], w["cmp_w2_v"].rearrange("(k p) d -> p k d", p=P))
    for j, name in enumerate(("cmp_pe_k", "cmp_pe_v")):
        small = sm.dma(K.act, pe_in[:, j, :], w[name].rearrange("(m two) d -> m (two d)", two=2))
    K.load_distances(ctx)
    gq = K.ts(gains[:, 0:1], gains[:, 0:1], DH ** -0.5, ALU.mult, small)
    big_ready, relb_ready = K.bias_table(ctx, "nsa", w["rel_bias"], big, relb)

    s = K.wring.take()
    v = s.t[:, :].rearrange("p (k r g d) -> p k r g d", k=KD, r=NR, g=NG)
    src = w_in.rearrange("(k p) n -> p k n", p=P)
    got = K.load(s, [(v[:, :, r, g, :], src[:, :, COL_Q + (g * NR + r) * DH:COL_Q + (g * NR + r + 1) * DH])
                     for r in range(NR) for g in range(NG)])
    q_ready = []
    for r in range(NR):
        b = K.banks.take()
        m = K.project(b, b.t[:, :], lambda k: v[:, k, r, :, :].rearrange("p g d -> p (g d)"),
                      lambda k: hT[:, k, :], KD, got, ready)
        q_ready.append(K.head_norm(tmp, b, m, qT[:, r, :], gains[:, 0:1]))
    s.free = [m]

    s, v, got = K.weights(w_in, COL_KC, 512)
    raw_ready = []
    for j in range(2):
        b = K.banks.take()
        m = K.project(b, b.t[:, :], lambda k: v[:, k, j * P:(j + 1) * P], lambda k: hT[:, k, :], KD, got)
        e = K.a(raw[:, j, :], b.t[:, :], ACT.Copy, m)
        b.free = [e]
        raw_ready.append(e)
    b = K.banks.take()
    m = K.project(b, b.t[:, :], lambda k: v[:, k, 2 * P:3 * P], lambda k: hT[:, k, :], KD, got)
    ks_ready = K.head_norm(tmp, b, m, ksT[:, :], gains[:, 1:2])

    def values(dst, v, at):
        b = K.banks.take()
        for t in range(TT):
            m = K.project(b, b.t[:, t * P:(t + 1) * P], lambda k: hT[:, k, t * P:(t + 1) * P],
                          lambda k: v[:, k, at:at + P], KD)
        e = K.a(dst[:, :, :], b.t[:, :].rearrange("p (t n) -> p t n", t=TT), ACT.Copy, m)
        b.free = [e]
        return m, e

    m, vs_ready = values(vs, v, 3 * P)
    s.free = [m]

    sh = K.channel("cmp_shift")
    for j in range(2):
        for g in range(NG):
            src = raw[g * DH:(g + 1) * DH, j, :]
            shifted = sh.dma(K.sp, x2[0:DH, j, g, :], src, raw_ready[j])
            shifted = sh.dma(K.sp, x2[DH:P, j, g, 0:S - 1], src[:, 1:S])

    s, v, got = K.weights(w_in, COL_KW, 2 * KVW + 3 * NH)
    b = K.banks.take()
    m = K.project(b, b.t[:, :], lambda k: v[:, k, 0:P], lambda k: hT[:, k, :], KD, got)
    kw_ready = K.head_norm(tmp, b, m, kwT[:, :], gains[:, 1:2])
    m, vw_ready = values(vw, v, P)
    b = K.banks.take()
    for t in range(TT):
        m = K.project(b, b.t[:, t * 24:(t + 1) * 24], lambda k: hT[:, k, t * P:(t + 1) * P],
                      lambda k: v[:, k, 2 * P:2 * P + 24], KD)
    s.free = [m]
    gate_ready = K.a(gate[:, :, :], b.t[:, 0:96].rearrange("p (t n) -> p t n", t=TT), ACT.Sigmoid, m)
    b.free = [gate_ready]

    NB = NG * NC
    hid = K.sb(ctx, "cmp_hid", [P, 5, 4, NB])
    peh = K.sb(ctx, "cmp_peh", [P, 4])
    b = K.banks.take()
    for j in range(2):
        m = K.tr(b.t[:, j * 16:(j + 1) * 16], pe_in[:, j, :], small, b.free, K.consts_ready)
    b.free = []
    pe_ready = K.cp(peT[:, :, :], b.t[:, 0:32].rearrange("p (j m) -> p j m", j=2), m)
    b.free = [pe_ready]
    for j, name in enumerate(("cmp_w1_k", "cmp_w1_v")):
        s = K.wring.take()
        v1 = s.t[:, :].rearrange("p (m n) -> p m n", m=16)
        got = K.load(s, [(v1, w[name].rearrange("(m p) n -> p m n", p=P))])
        for half in range(2):
            b = K.banks.take()
            cols = slice(half * P, (half + 1) * P)
            K.project(b, b.t[:, 0:NB].rearrange("p (g n) -> p g n", g=NG), lambda k: v1[:, k, cols],
                      lambda k: x2[:, j, :, 2 * k:2 * k + CS * (NC - 1) + 1:CS], 16, got, shifted)
            m = K.project(b, b.t[:, NB:NB + 1], lambda k: v1[:, k, cols], lambda k: peT[:, j, k:k + 1], 16, pe_ready)
            u = j * 2 + half
            k = K.cp(peh[:, u:u + 1], b.t[:, NB:NB + 1], m)
            k = K.ts(hid[:, 0, u, :], b.t[:, 0:NB], peh[:, u:u + 1], ALU.add, k)
            b.free = [k]
        s.free = [m]
    x, x3, inner, th, act = (hid[:, i, :, :] for i in range(5))
    k = K.tt(x3, x, x, ALU.mult, k)
    k = K.tt(x3, x3, x, ALU.mult, k)
    k = K.stt(inner, x3, 0.044715, x, ALU.mult, ALU.add, k)
    k = K.a(th, inner, ACT.Tanh, k, scale=math.sqrt(2 / math.pi))
    k = K.stt(act, th, 1.0, x, ALU.add, ALU.mult, k)
    act_ready = K.ts(act, act, 0.5, ALU.mult, k)
    kcT = K.sb(ctx, "kcT", [P, NB])
    vc = K.sb(ctx, "vc", [P, NG, DH])
    b = K.banks.take()
    m = K.project(b, b.t[:, 0:NB], lambda k: w2k[:, k, :, :], lambda k: act[:, k, :], 2, act_ready)
    kc_ready = K.head_norm(tmp, b, m, kcT[:, :], gains[:, 1:2], n=NB)
    z = K.zero(vc[:, :, :])
    b = K.banks.take()
    for r in range(NR):
        for g in range(NG):
            m = K.project(b, b.t[32 * r:32 * r + NC, g * DH:(g + 1) * DH], lambda k: act[:, 2 + k, g * NC:(g + 1) * NC],
                          lambda k: w2v[:, k, :], 2)
    for r in range(NR):
        vc_ready = K.cp(vc[32 * r:32 * r + NC, :, :],
                        b.t[32 * r:32 * r + NC, 0:P].rearrange("p (g d) -> p g d", g=NG), m, z)
    b.free = [vc_ready]

    bias_c = K.sb(ctx, "bias_c", [P, TT, NH, 32])
    z = K.zero(bias_c[:, :, :, :], value=NEG)
    for i in range(TT):
        b = K.banks.take()
        for n in range(NC):
            at = P * i - CS * n - (CB - 1) + 511
            m = K.mm(b.t[:, n:n + 7 * 32 + 1:32], K.dist[:, at:at + P], relb[:, :], relb_ready, b.free,
                     K.dist_ready, signal=(n == NC - 1))
        k = K.cp(bias_c[:, i, :, 0:NC], b.t[:, 0:256].rearrange("p (h n) -> p h n", h=NH)[:, :, 0:NC], m, z)
        b.free = [k]
    bias_ready = k

    pc = K.ring(ctx, "cmp_p", TT, [P, NH, 32])
    pcT = K.ring(ctx, "cmp_pT", TT, [P, 2, P])
    st = K.sb(ctx, "cmp_stat", [P, TT, 3, NH])
    coef = K.sb(ctx, "cmp_coef", [P, TT, NH])
    o_ready, soft, turned = {}, {}, {}
    for i in range(TT):
        s = pc.take()
        z = K.cp(s.t[:, :, NC:32], bias_c[:, i, :, NC:32], s.free, bias_ready)
        for g in range(NG):
            b = K.banks.take()
            half = slice(g * DH, (g + 1) * DH)
            for r in range(NR):
                m = K.mm(b.t[:, r * 32:r * 32 + NC], qT[half, r, i * P:(i + 1) * P],
                         kcT[half, g * NC:(g + 1) * NC], b.free, q_ready, kc_ready, signal=(r == NR - 1))
            v3 = b.t[:, 0:P].rearrange("p (h n) -> p h n", h=NR)[:, :, 0:NC]
            hs = slice(g * NR, (g + 1) * NR)
            k = K.tt(s.t[:, hs, 0:NC], v3, bias_c[:, i, hs, 0:NC], ALU.add, m, s.free, bias_ready)
            b.free = [k]
        mx, sm_, rc = (st[:, i, j, :] for j in range(3))
        k = K.red(mx, s.t[:, :, :], ALU.max, k, z)
        k = K.tt(s.t[:, :, :], s.t[:, :, :], spread(mx, 32), ALU.subtract, k)
        k = K.a(s.t[:, :, :], s.t[:, :, :], ACT.Exp, k)
        p_ready = k
        k = K.red(sm_, s.t[:, :, :], ALU.add, k)
        k = K.ts(sm_, sm_, 1e-30, ALU.max, k)
        k = K.recip(rc, sm_, k)
        k = K.stt(coef[:, i, :], rc, c("valid_c")[:, i:i + 1], gate[:, i, 0:3 * NH:3], ALU.mult, ALU.mult, k, gate_ready)
        soft[i] = (s, p_ready, k)
    for i in range(TT):
        s, p_ready, k = soft[i]
        t2 = pcT.take()
        b = K.banks.take()
        for g in range(NG):
            m = K.tr(b.t[:, g * P:(g + 1) * P], s.t[:, g * NR:(g + 1) * NR, :].rearrange("p h n -> p (h n)"),
                     p_ready, b.free)
        e = K.cp(t2.t[:, :, :], b.t[:, 0:2 * P].rearrange("p (g n) -> p g n", g=2), m, t2.free)
        s.free, b.free = [m, k], [e]
        turned[i] = (t2, e, k)
    for i in range(TT):
        t2, e, coef_ready = turned[i]
        for r in range(NR):
            b = K.banks.take()
            rows = slice(32 * r, 32 * r + NC)
            for g in range(NG):
                m = K.mm(b.t[:, g * DH:(g + 1) * DH], t2.t[rows, g, :], vc[rows, g, :], e, b.free, vc_ready)
            k = K.tt(o[:, i, :].rearrange("p (g r d) -> p g r d", g=NG, r=NR)[:, :, r, :],
                     b.t[:, 0:P].rearrange("p (g d) -> p g d", g=NG),
                     spread(coef[:, i, r:NH:NR], DH), ALU.mult, m, coef_ready)
            b.free = [k]
        t2.free = [m]
        o_ready[i] = k

    K.meet()
    ctx.close()
    scratch = K.ring(outer, "att_o", 2, [P, NW])
    branches = []
    for j, (kT, vv, k_ready, v_ready) in enumerate(((ksT, vs, ks_ready, vs_ready), (kwT, vw, kw_ready, vw_ready))):
        cf = K.sb(outer, f"coef{j}", [P, TT, 2, NH])

        def finish(i, b, got, sums, sums_ready, j=j, cf=cf):
            k = K.recip(cf[:, i, 0, :], sums, sums_ready)
            k = K.tt(cf[:, i, 1, :], cf[:, i, 0, :], gate[:, i, 1 + j:3 * NH:3], ALU.mult, k, gate_ready)
            s = scratch.take()
            e = K.tt(s.t[:, :].rearrange("p (h d) -> p h d", h=NH), b.t[:, :].rearrange("p (h d) -> p h d", h=NH),
                     spread(cf[:, i, 1, :], DH), ALU.mult, k, got, s.free)
            k = K.tt(o[:, i, :], o[:, i, :], s.t[:, :], ALU.add, e, o_ready[i])
            s.free = [k]
            o_ready[i] = k
            return e

        branches.append((lambda h: qT[(h // NR) * DH:(h // NR + 1) * DH, h % NR, :],
                         lambda h, kT=kT: kT[(h // NR) * DH:(h // NR + 1) * DH, :],
                         lambda h, j2, vv=vv: vv[:, j2, (h // NR) * DH:(h // NR + 1) * DH],
                         [q_ready, k_ready, v_ready, big_ready], finish, None))
    K.attention(outer, "nsa", branches, big)
    return K.to_fm(o, o_ready, oT)


def mix(K, p1, d, mu, out, ready, out_free):
    k = K.tt(d, p1[:, 0:S], p1[:, 1:S + 1], ALU.subtract, ready)
    return K.stt(out, d, mu, p1[:, 1:S + 1], ALU.mult, ALU.add, k, out_free)


def rwkv(K, ctx, hT, ready, oT):
    w, c = K.w, K.c
    w_in = w["w_in"]
    sm = K.channel("rwkv_small")
    mu = K.sb(ctx, "mu", [P, 14])
    vec = K.sb(ctx, "rwkv_vec", [P, 8, 4])
    w2a2, g2 = K.sb(ctx, "w2a2", [P, RW]), K.sb(ctx, "g2", [P, RW])
    rows = K.sb(ctx, "rwkv_rows", [46, P])
    small = sm.dma(K.act, rows[0:14, :], w["rwkv_mu"].rearrange("o (k p) -> (o k) p", p=P))
    names = ("rwkv_w0", "rwkv_a0", "rwkv_k_k", "rwkv_k_a", "rwkv_r_k", "rwkv_ln_g", "rwkv_ln_b")
    for j, name in enumerate(names):
        src = w[name].rearrange("(k two) d -> k (two d)", two=2) if name == "rwkv_r_k" else \
            w[name].rearrange("o (k p) -> (o k) p", p=P)
        small = sm.dma(K.act, rows[14 + 4 * j:18 + 4 * j, :], src)
    small = sm.dma(K.act, w2a2[0:64, :], w["rwkv_w2"])
    small = sm.dma(K.act, w2a2[64:P, :], w["rwkv_a2"])
    small = sm.dma(K.act, g2[:, :], w["rwkv_g2"])
    b = K.banks.take()
    m = K.tr(b.t[:, 0:42], rows[0:42, :], small, b.free, K.consts_ready)
    k = K.cp(mu[:, :], b.t[:, 0:14], m)
    vec_ready = K.cp(vec[:, 0:7, :], b.t[:, 14:42].rearrange("p (j k) -> p j k", j=7), m)
    b.free = [vec_ready]
    w0, a0, kkg, kag, rkg, lng, lnb = (vec[:, j, :] for j in range(7))

    p1 = K.ring(ctx, "p1", 3, [P, S + 1])
    for s in p1.slots:
        s.free = [K.zero(s.t[:, 0:1])]
    tmp = K.ring(ctx, "rw_tmp", 3, [P, S])
    lor, xg = K.sb(ctx, "lor", [P, S]), K.sb(ctx, "xg", [P, S])
    thw = K.sb(ctx, "thw", [DH, S])

    def mixed(v, at, got, muc, out, out_free=None):
        b, s, d = K.banks.take(), p1.take(), tmp.take()
        m = K.project(b, b.t[:, :], lambda k: v[:, k, at:at + P], lambda k: hT[:, k, :], KD, got, ready)
        e = K.a(s.t[:, 1:S + 1], b.t[:, :], ACT.Copy, m, s.free)
        b.free = [e]
        k = mix(K, s.t, d.t[:, :], mu[:, muc:muc + 1], out, [e, d.free, vec_ready], out_free)
        s.free = d.free = [k]
        return m, k

    s, v, got = K.weights(w_in, COL_LORA, 256)
    m, lor_ready = mixed(v, 0, got, 12, lor[:, :])
    m, k = mixed(v, P, got, 13, xg[:, :])
    s.free = [m]
    thw_ready = K.a(thw[:, :], lor[0:DH, :], ACT.Tanh, lor_ready)
    sg_ready = K.a(xg[:, :], xg[:, :], ACT.Sigmoid, k)

    names = ("rT", "kT", "vT", "lw", "aT", "gT", "bv")
    buf = {n: K.sb(ctx, f"rw_{n}", [P, S]) for n in names}
    rT, kT, vT, lw, aT, gT, bv = (buf[n][:, :] for n in names)
    kk, kp, y = lw, kT, aT.rearrange("p (h d) -> p h d", h=8)
    L, E1, E2 = (K.sb(ctx, f"rw_{n}", [P, TT, P + 1]) for n in ("L", "E1", "E2"))
    ra = K.sb(ctx, "rw_ra", [P, TT, 2, P])
    kt, bt = K.sb(ctx, "rw_kt", [P, TT, P]), K.sb(ctx, "rw_bt", [P, TT, P])
    Kt, Bt, Vt = (K.sb(ctx, f"rw_{n}_tm", [P, TT, P]) for n in "KBV")
    AM = K.sb(ctx, "rw_AM", [P, 8, 4, P])
    ready0 = [K.zero(AM[:, :, :, :]), K.zero(L[:, :, 0:1])]
    Alow = [K.sb(ctx, f"rw_low{g}", [P, 4, P]) for g in range(2)]
    ready0 += [K.zero(x[:, :, :]) for x in Alow]
    level = K.ring(ctx, "rw_lev", 2, [P, 4, P])
    WU = [[K.sb(ctx, f"rw_{n}{g}", [P, 4, P]) for n in "WUY"] for g in range(2)]
    Z = K.sb(ctx, "rw_Z", [P, P])
    zs = K.sb(ctx, "rw_zs", [P, TT])
    step = K.ring(ctx, "rw_step", 4, [P, P])
    yst = K.sb(ctx, "rw_yst", [P, 4, 8])
    ones = K.sb(ctx, "rw_ones", [P, P])
    ones_ready = K.zero(ones[:, :], value=1.0)
    pair_done = []

    for f in range(4):
        cols = slice(f * P, (f + 1) * P)
        s = K.wring.take()
        v = s.t[:, 0:8 * 384].rearrange("p (k n) -> p k n", k=KD)
        got = K.load(s, [(v[:, :, j * P:(j + 1) * P], w_in.rearrange("(k p) n -> p k n", p=P)[:, :, at + f * P:at + (f + 1) * P])
                         for j, at in enumerate((COL_R, COL_K, COL_V))])
        free = pair_done
        m, r_ready = mixed(v, 0, got, f, rT, free)
        m, k_ready = mixed(v, P, got, 4 + f, kT, free)
        m, v_ready = mixed(v, 2 * P, got, 8 + f, vT, free)
        s.free = [m]
        b = K.banks.take()
        m = K.mm(b.t[:, :], w2a2[0:DH, cols], thw[:, :], b.free, thw_ready)
        k = K.a(lw, b.t[:, :], ACT.Sigmoid, m, free, bias=w0[:, f:f + 1])
        b.free = [k]
        k = K.ts(lw, lw, -DECAY, ALU.mult, k)
        lw_ready = k
        b = K.banks.take()
        m = K.mm(b.t[:, :], w2a2[DH:P, cols], lor[DH:P, :], b.free, lor_ready)
        a_ready = K.a(aT, b.t[:, :], ACT.Sigmoid, m, free, bias=a0[:, f:f + 1])
        b.free = [a_ready]
        b = K.banks.take()
        m = K.mm(b.t[:, :], g2[:, cols], xg[:, :], b.free, sg_ready)
        g_ready = K.a(gT, b.t[:, :], ACT.Copy, m, free)
        b.free = [g_ready]
        for n in range(TT):
            k = K.dve.do(lambda e, n=n: e.tensor_tensor_scan(
                L[:, n, 1:P + 1], ones[:, :], buf["lw"][:, n * P:(n + 1) * P], 0.0, ALU.mult, ALU.add),
                lw_ready, ones_ready, ready0, free)
        scanned = k
        k = K.tt(E1[:, :, :], L[:, :, :], L[:, :, 64:65].broadcast_to([P, TT, P + 1]), ALU.subtract, k)
        e2 = K.a(E2[:, :, :], E1[:, :, :], ACT.Exp, k, scale=-1.0)
        e1 = K.a(E1[:, :, :], E1[:, :, :], ACT.Exp, e2)
        k0 = K.ts(kk, kT, kkg[:, f:f + 1], ALU.mult, k_ready, vec_ready, scanned)
        t1, t2 = tmp.take(), tmp.take()
        k = K.a(t1.t[:, :], kk, ACT.Square, k0, t1.free)
        b = K.banks.take()
        m = K.mm(b.t[:, :], c("ones64"), t1.t[:, :], k, b.free)
        k = K.ts(t2.t[:, :], b.t[:, :], NORM_FLOOR, ALU.max, m, t2.free)
        b.free, t1.free = [k], [m]
        k = K.a(t2.t[:, :], t2.t[:, :], ACT.Ln, k, scale=2.0 ** LN_SHIFT)
        k = K.a(t2.t[:, :], t2.t[:, :], ACT.Exp, k, scale=-0.5, bias=c("ln_back"))
        kk_ready = K.tt(kk, kk, t2.t[:, :], ALU.mult, k)
        t2.free = [kk_ready]
        t1 = tmp.take()
        k = K.ts(t1.t[:, :], aT, -1.0, ALU.add, a_ready, t1.free, s2=kag[:, f:f + 1], op1=ALU.mult)
        kp_ready = K.stt(kp, t1.t[:, :], 1.0, kT, ALU.add, ALU.mult, k, k0)
        t1.free = [kp_ready]
        v4 = lambda x: x.rearrange("p (n t) -> p n t", n=TT)
        k = K.stt(ra[:, :, 0, :], v4(kk), -1.0, E1[:, :, 0:P], ALU.mult, ALU.mult, kk_ready, e1)
        ra_ready = K.tt(ra[:, :, 1, :], v4(rT), E1[:, :, 1:P + 1], ALU.mult, e1, r_ready)
        kt_ready = K.tt(kt[:, :, :], v4(kp), E2[:, :, 1:P + 1], ALU.mult, kp_ready, e2)
        t1 = tmp.take()
        k = K.tt(t1.t[:, :], kk, aT, ALU.mult, kk_ready, a_ready, t1.free)
        bt_ready = K.tt(bt[:, :, :], v4(t1.t[:, :]), E2[:, :, 1:P + 1], ALU.mult, k)
        t1.free = [bt_ready]
        t1 = tmp.take()
        k = K.stt(t1.t[:, :], rT, rkg[:, f:f + 1], kp, ALU.mult, ALU.mult, kp_ready, r_ready, t1.free)
        b = K.banks.take()
        m = K.mm(b.t[:, :], c("ones64"), t1.t[:, :], k, b.free)
        t1.free = [m]
        bv_ready = K.tt(bv, b.t[:, :], vT, ALU.mult, m, v_ready)
        b.free = [bv_ready]
        zs_ready = K.tt(zs[:, 0:TT - 1], E1[:, 0:TT - 1, P:P + 1].rearrange("p n o -> p (n o)"),
                        E2[:, 1:TT, 0:1].rearrange("p n o -> p (n o)"), ALU.mult, e1, e2, bv_ready)
        tm_ready = []
        for dst, src, r0 in ((Kt, kt[:, :, :], kt_ready), (Bt, bt[:, :, :], bt_ready), (Vt, v4(vT), v_ready)):
            b = K.banks.take()
            for n in range(TT):
                m = K.tr(b.t[:, n * P:(n + 1) * P], src[:, n, :], r0, b.free, signal=(n == TT - 1))
            k = K.a(dst[:, :, :], b.t[:, :].rearrange("p (n t) -> p n t", n=TT), ACT.Copy, m, free)
            b.free = [k]
            tm_ready.append(k)
        am_ready = {}
        for u in range(8):
            hh, n = divmod(u, TT)
            hp = slice(hh * DH, (hh + 1) * DH)
            b = K.banks.take()
            K.mm(b.t[:, 0:256].rearrange("p (x t) -> p x t", x=2), kt[hp, n, :], ra[hp, n, :, :], b.free, kt_ready, ra_ready, signal=False)
            m = K.mm(b.t[:, 256:512].rearrange("p (x t) -> p x t", x=2), bt[hp, n, :], ra[hp, n, :, :], bt_ready)
            k = K.dve.do(lambda e, u=u, b=b: e.copy_predicated(
                AM[:, u, :, :], c("mask_rw").bitcast(I32).rearrange("p (x t) -> p x t", x=4),
                b.t[:, :].rearrange("p (x t) -> p x t", x=4)), m, ready0, free)
            b.free = [k]
            am_ready[u] = k
        inv_ready = []
        state = []
        for g in range(2):
            b = K.banks.take()
            for i in range(4):
                n, hh = i, g
                hp = slice(hh * DH, (hh + 1) * DH)
                m = K.mm(b.t[:, i * P:(i + 1) * P], ra[hp, n, 0, :], bt[hp, n, :], b.free, ra_ready, bt_ready,
                         signal=(i == 3))
            A = Alow[g]
            a_low = K.dve.do(lambda e, A=A, b=b: e.copy_predicated(
                A[:, :, :], c("mask_low4").bitcast(I32).rearrange("p (x t) -> p x t", x=4),
                b.t[:, :].rearrange("p (x t) -> p x t", x=4)), m, ready0, free)
            b.free = [a_low]
            W, U, Y = WU[g]
            eye = spread(c("ident"), 4, 1)
            k = K.tt(W[:, :, :], AM[:, 4 * g:4 * g + 4, 2, :], spread(c("lev0u"), 4, 1), ALU.mult, am_ready[4 * g + 3], free)
            w_r = K.tt(W[:, :, :], W[:, :, :], eye, ALU.add, k)
            k = K.tt(U[:, :, :], A[:, :, :], spread(c("lev0"), 4, 1), ALU.mult, a_low, free)
            u_r = K.tt(U[:, :, :], U[:, :, :], eye, ALU.add, k)
            state.append((A, W, U, Y, a_low, w_r, u_r))
        for lv in range(1, 7):
            for g in range(2):
                A, W, U, Y, a_low, w_r, u_r = state[g]
                s = level.take()
                am = K.tt(s.t[:, :, :], A[:, :, :], spread(c(f"lev{lv}"), 4, 1), ALU.mult, a_low, s.free, lane=K.pool)
                b = K.banks.take()
                for i in range(4):
                    m = K.mm(b.t[:, i * P:(i + 1) * P], s.t[:, i, :], W[:, i, :], am, w_r, b.free, signal=(i == 3))
                s.free = [m]
                y_r = K.a(Y[:, :, :], b.t[:, :].rearrange("p (x t) -> p x t", x=4), ACT.Copy, m, free)
                b.free = [y_r]
                b1 = K.banks.take()
                for i in range(4):
                    m1 = K.mm(b1.t[:, i * P:(i + 1) * P], U[:, i, :], Y[:, i, :], y_r, u_r, b1.free, signal=(i == 3))
                m2 = None
                if lv < 6:
                    b2 = K.banks.take()
                    for i in range(4):
                        m2 = K.mm(b2.t[:, i * P:(i + 1) * P], Y[:, i, :], U[:, i, :], b2.free, signal=(i == 3))
                w_r = K.tt(W[:, :, :], W[:, :, :], b1.t[:, :].rearrange("p (x t) -> p x t", x=4), ALU.add, m1)
                b1.free = [w_r]
                if lv < 6:
                    u_r = K.tt(U[:, :, :], U[:, :, :], b2.t[:, :].rearrange("p (x t) -> p x t", x=4), ALU.add, m2)
                    b2.free = [u_r]
                state[g] = (A, W, U, Y, a_low, w_r, u_r)
        z_r = K.zero(Z[:, :], free)
        for n in range(TT):
            units = [n, TT + n]
            b, sa, rhs = K.banks.take(), step.take(), step.take()
            K.mm(b.t[:, 0:P], ra[:, n, 0, :], Z[:, :], z_r, b.free, ra_ready, signal=False, stop=False, loose=True)
            for hh, u in enumerate(units):
                m = K.mm(b.t[:, hh * DH:(hh + 1) * DH], AM[:, u, 0, :], Vt[:, n, hh * DH:(hh + 1) * DH],
                         am_ready[u], tm_ready, start=False, loose=True)
            k = K.a(rhs.t[:, :], b.t[:, 0:P], ACT.Copy, m, rhs.free)
            b.free = [k]
            b = K.banks.take()
            for hh, u in enumerate(units):
                m = K.mm(b.t[:, hh * DH:(hh + 1) * DH], state[hh][1][:, n, :], rhs.t[:, hh * DH:(hh + 1) * DH],
                         k, state[hh][5], b.free)
            rhs.free = [m]
            sa_r = K.cp(sa.t[:, :], b.t[:, 0:P], m, sa.free)
            b.free = [sa_r]
            if n < TT - 1:
                b = K.banks.take()
                K.mm(b.t[:, 0:P], Kt[:, n, :], Vt[:, n, :], b.free, signal=False, stop=False)
                mz = K.mm(b.t[:, 0:P], Bt[:, n, :], sa.t[:, :], sa_r, start=False)
                bz = b
            b = K.banks.take()
            K.mm(b.t[:, 0:P], ra[:, n, 1, :], Z[:, :], b.free, signal=False, stop=False, loose=True)
            for hh, u in enumerate(units):
                cs = slice(hh * DH, (hh + 1) * DH)
                K.mm(b.t[:, cs], AM[:, u, 1, :], Vt[:, n, cs], start=False, stop=False, signal=False, loose=True)
                m = K.mm(b.t[:, cs], AM[:, u, 3, :], sa.t[:, cs], sa_r, start=False, loose=True)
            y_ready = K.a(y[:, 2 * n:2 * n + 2, :], b.t[:, 0:P].rearrange("p (h d) -> p h d", h=2), ACT.Copy, m, free, bt_ready)
            b.free = [y_ready]
            sa.free = [m]
            if n < TT - 1:
                for hh in range(2):
                    hp = slice(hh * DH, (hh + 1) * DH)
                    k = K.tt(Z[hp, hp], Z[hp, hp], bz.t[hp, hp], ALU.add, mz, m)
                bz.free = [k]
                z_r = K.ts(Z[:, :], Z[:, :], zs[:, n:n + 1], ALU.mult, k, zs_ready)
        t1 = tmp.take()
        sq = t1.t[:, :].rearrange("p (h d) -> p h d", h=8)
        s1, s2, s3, s4 = (yst[:, j, :] for j in range(4))
        k = K.red(s1, y[:, :, :], ALU.add, y_ready)
        k = K.ts(s2, s1, 1.0 / DH, ALU.mult, k)
        k = K.tt(y[:, :, :], y[:, :, :], spread(s2, DH), ALU.subtract, k)
        k1 = K.a(sq, y[:, :, :], ACT.Square, k, t1.free)
        k = K.red(s3, sq, ALU.add, k1)
        t1.free = [k]
        k = K.ts(s3, s3, 1.0 / DH, ALU.mult, k, s2=GN_EPS, op1=ALU.add)
        k = K.recip(s4, s3, k)
        k = K.a(s4, s4, ACT.Sqrt, k)
        k = K.tt(y[:, :, :], y[:, :, :], spread(s4, DH), ALU.mult, k)
        b = K.banks.take()
        for n in range(TT):
            m = K.tr(b.t[:, n * P:(n + 1) * P], y[:, 2 * n:2 * n + 2, :].rearrange("p h d -> p (h d)"), k, b.free,
                     signal=(n == TT - 1))
        t1 = tmp.take()
        k = K.ts(t1.t[:, :], b.t[:, :], lng[:, f:f + 1], ALU.mult, m, t1.free, s2=lnb[:, f:f + 1], op1=ALU.add)
        b.free = [k]
        k = K.tt(t1.t[:, :], t1.t[:, :], bv, ALU.add, k, bv_ready)
        k = K.tt(oT[:, f, :], t1.t[:, :], gT, ALU.mult, k, g_ready)
        t1.free = [k]
        pair_done = [k, K.pe.last(), K.act.last()]
        out = k
    return out


def merge(K, ctx, hT, oaT, obT, oa_ready, ob_ready, x):
    w = K.w
    K.cut_ring(ctx, 4)
    h = tuple(K.sb(ctx, f"h_{n}", [P, KD, S], F32R) for n in ("hi", "lo"))
    mT = tuple(K.sb(ctx, f"merged_{n}", [P, KD, S], F32R) for n in ("hi", "lo"))
    sg = Ring([Slot(hT[:, k, :]) for k in range(KD)])
    m_ready = []
    for quarter in range(4):
        slots = []
        gs = K.wring.take()
        gv = gs.t[:, :].rearrange("p (j k n) -> p j k n", j=2, k=KD)
        ggot = K.load(gs, [(gv[:, j, :, :], w["w_in"].rearrange("(k p) n -> p k n", p=P)[
            :, :, at + quarter * 256:at + (quarter + 1) * 256]) for j, at in enumerate((COL_GA, COL_GB))])
        if quarter % 2 == 0:
            ps = K.wring.take()
            pv = ps.t[:, :].rearrange("p (j k n) -> p j k n", j=2, k=4)
            pgot = K.load(ps, [(pv[:, j, :, :], w[n].rearrange("(k p) n -> p k n", p=P)[
                :, :, quarter * 256:quarter * 256 + 512]) for j, n in enumerate(("w_proj_a", "w_proj_b"))])
        for i in range(2):
            f, part = quarter * 2 + i, []
            cut = [K.cut(gv[:, j, :, i * P:(i + 1) * P], ggot) for j in range(2)]
            if f == 0:
                h_ready = [K.halves(h[0][:, k, :], h[1][:, k, :], hT[:, k, :]) for k in range(KD)]
                for s, k in zip(sg.slots, h_ready):
                    s.free = [k]
            if i == 1:
                gs.free = [cut[1][2]]
            for j, (oT, o_ready) in enumerate(((oaT, oa_ready), (obT, ob_ready))):
                b = K.banks.take()
                m = K.project(b, b.t[:, :], lambda k: pv[:, j, k, (f % 4) * P:(f % 4 + 1) * P],
                              lambda k: oT[:, k, :], 4, pgot, o_ready)
                part.append((b, m))
            if quarter % 2 and i:
                ps.free = [m]
            for j in range(2):
                c, cols, c_ready = cut[j]
                b, s = K.banks.take(), sg.take()
                m = K.project3(b, b.t[:, :], lambda k: (cols[0][:, k, :], cols[1][:, k, :]),
                               lambda k: (h[0][:, k, :], h[1][:, k, :]), KD, c_ready, h_ready)
                c.free = [m]
                e = K.a(s.t[:, :], b.t[:, :], ACT.Sigmoid, m, s.free)
                b.free = [e]
                pb, pm = part[j]
                k = K.tt(s.t[:, :], s.t[:, :], pb.t[:, :], ALU.mult, e, pm)
                pb.free = [k]
                part[j] = (s, k)
            (s0, k0), (s1, k1) = part
            k = K.tt(s0.t[:, :], s0.t[:, :], s1.t[:, :], ALU.add, k0, k1)
            s1.free = [k]
            k = K.halves(mT[0][:, f, :], mT[1][:, f, :], s0.t[:, :], k)
            s0.free = [k]
            m_ready.append(k)
    return add_product(K, w["w_out"], mT, KD, m_ready, x)


def add_product(K, w, aT, n, ready, x, more=None):
    done = [[] for _ in range(TT)]
    jobs = [(half, k0, slot0) for half in range(2) for slot0 in range(0, n, 8) for k0 in range(slot0, min(slot0 + 8, n), 2)]
    src = w.rearrange("(k p) n -> p k n", p=P)
    pieces, held = {}, {}

    def prepare(half, k0, slot0):
        if k0 == slot0:
            m, s = min(8, n - slot0), K.wring.take()
            v = s.t[:, 0:m * 512].rearrange("p (k n) -> p k n", k=m)
            held["w"] = (s, v, K.load(s, [(v, src[:, slot0:slot0 + m, half * 512:(half + 1) * 512])]))
        s, v, got = held["w"]
        two = min(2, n - k0)
        c = K.cut(v[:, k0 - slot0:k0 - slot0 + two, :], got)
        if k0 + two in (slot0 + 8, n):
            s.free = [c[2]]
        pieces[half, k0] = (two, c)

    for job in jobs[0:2]:
        prepare(*job)
    for i, (half, k0, slot0) in enumerate(jobs):
        if i + 2 < len(jobs):
            prepare(*jobs[i + 2])
        two, (c, cols, c_ready) = pieces.pop((half, k0))
        if k0 == 0:
            acc = [K.banks.take() for _ in range(TT)]
        for t in range(TT):
            for q in range(two):
                k, ts_ = k0 + q, slice(t * P, (t + 1) * P)
                m = K.mm3(acc[t].t[:, :], (aT[0][:, k, ts_], aT[1][:, k, ts_]), (cols[0][:, q, :], cols[1][:, q, :]),
                          c_ready, acc[t].free, ready[k], start=(k == 0), stop=(k == n - 1), signal=(q == two - 1))
            acc[t].free = []
            if k0 + two == n:
                xs = x[:, t, half * 512:(half + 1) * 512]
                e = K.tt(xs, xs, acc[t].t[:, :], ALU.add, m)
                acc[t].free = [e]
                done[t].append(e)
        c.free = [m]
    return done


def ffn(K, ctx, h2T, ready, x):
    w = K.w
    conv_rows = K.sb(ctx, "conv_rows", [4 * 2 * FT // 2, 2, P])
    cv = K.sb(ctx, "conv_cols", [P, 4, 2 * FT])
    sm = K.channel("ffn_small")
    for j in range(4):
        src = w["conv_b"] if j == 3 else w["conv_w"][j:j + 1, :]
        small = sm.dma(K.act, conv_rows[FT * j:FT * (j + 1), :, :],
                       src.rearrange("o (two k p) -> (o k) two p", two=2, p=P))
    for two in range(2):
        b = K.banks.take()
        m = K.tr(b.t[:, 0:4 * FT], conv_rows[:, two, :], small, b.free)
        cv_ready = K.cp(cv[:, :, two * FT:(two + 1) * FT], b.t[:, 0:4 * FT].rearrange("p (j k) -> p j k", j=4), m)
        b.free = [cv_ready]
    FH = 8
    fT = tuple(K.sb(ctx, f"ffn_{n}", [P, FH, S], F32R) for n in ("hi", "lo"))
    ub = K.ring(ctx, "ffn_u", 4, [P, S + 2])
    cb = K.ring(ctx, "ffn_c", 4, [P, S])
    K.cut_ring(ctx, 6)
    for s in ub.slots:
        s.free = [K.zero(s.t[:, 0:2])]
    w_up = w["w_up"].rearrange("(k p) n -> p k n", p=P)
    pieces, held = {}, {}

    def prepare(f):
        j, i = divmod(f, 2)
        if i == 0:
            s = K.wring.take()
            v = s.t[:, :].rearrange("p (k two n) -> p k two n", k=KD, two=2)
            held["w"] = (s, v, K.load(s, [(v[:, :, two, :], w_up[:, :, two * DFF + j * 256:two * DFF + (j + 1) * 256])
                                          for two in range(2)]))
        s, v, got = held["w"]
        pieces[f] = [K.cut(v[:, :, two, i * P:(i + 1) * P], got) for two in range(2)]
        if i == 1:
            s.free = [pieces[f][1][2]]

    f_free, f_ready = None, []
    for f in range(FT):
        if f % FH == 0:
            prepare(f)
            prepare(f + 1)
        if f % FH + 2 < FH and f + 2 < FT:
            prepare(f + 2)
        conv = []
        for two in range(2):
            b, u, cbuf = K.banks.take(), ub.take(), cb.take()
            c, wc, c_ready = pieces[f][two]
            col = two * FT + f
            m = K.project3(b, b.t[:, :], lambda k: (wc[0][:, k, :], wc[1][:, k, :]),
                           lambda k: (h2T[0][:, k, :], h2T[1][:, k, :]), KD, c_ready, ready)
            c.free = [m]
            e = K.a(u.t[:, 2:S + 2], b.t[:, :], ACT.Copy, m, u.free)
            k = K.a(cbuf.t[:, :], b.t[:, :], ACT.Identity, m, cbuf.free, cv_ready,
                    scale=cv[:, 2, col:col + 1], bias=cv[:, 3, col:col + 1])
            b.free = [k]
            for tap in (1, 0):
                k = K.stt(cbuf.t[:, :], u.t[:, tap:tap + S], cv[:, tap, col:col + 1], cbuf.t[:, :],
                          ALU.mult, ALU.add, k, e)
            u.free = [k]
            conv.append((cbuf, k))
        (val, kv), (gt, kg) = conv
        sgm = ub.take()
        k = K.a(sgm.t[:, 2:S + 2], gt.t[:, :], ACT.Sigmoid, kg, sgm.free)
        k2 = K.tt(gt.t[:, :], gt.t[:, :], val.t[:, :], ALU.mult, kv, k, lane=K.pool)
        val.free = [k2]
        k = K.tt(gt.t[:, :], gt.t[:, :], sgm.t[:, 2:S + 2], ALU.mult, k, k2)
        sgm.free = [k]
        k = K.halves(fT[0][:, f % FH, :], fT[1][:, f % FH, :], gt.t[:, :], k, f_free)
        gt.free = [k]
        f_ready.append(k)
        n = len(f_ready)
        if n == FH or f + 1 == FT:
            done = add_product(K, w["w_down"][(f + 1 - n) * P:(f + 1) * P, :], fT, n, f_ready, x)
            f_free, f_ready = K.pe.last(), []
    return done


def selected_attention(K, ctx, hT, ready, oT, spare):
    w, c = K.w, K.c
    w_in = w["w_in_2"]
    sm = K.channel("dsa_small")
    qT, kT = K.sb(ctx, "q2T", [P, 4, S]), K.sb(ctx, "k2T", [P, 4, S])
    va = K.sb(ctx, "va", [P, TT, NW])
    iqT, ikT = K.sb(ctx, "iqT", [P, 2, S]), K.sb(ctx, "ikT", [P, S])
    iw = K.sb(ctx, "iw", [P, TT, IH])
    big = K.sb(ctx, "dsa_bias", [P, NH, 512])
    gains = K.sb(ctx, "dsa_gains", [P, 2])
    score = K.sb(ctx, "score", [P, TT, S])
    masks = K.sb(ctx, "selmask", [P, TT, S], BF16)
    top = K.sb(ctx, "top8", [P, TT, 8])
    eye = K.sb(ctx, "eye_bf", [P, P], BF16)
    outer, ctx = ctx, ExitStack()
    relb = K.sb(ctx, "dsa_relb", [33, NH])
    tmp = K.ring(ctx, "dsa_tmp", 5, [P, S])
    eye_ready = K.cp(eye[:, :], c("ident"))
    for half in range(2):
        for j, name in enumerate(("q_norm_g_2", "k_norm_g_2")):
            small = sm.dma(K.act, gains[half * DH:(half + 1) * DH, j:j + 1], w[name].rearrange("o d -> d o"), slow=True)
    K.ts(gains[:, 0:1], gains[:, 0:1], DH ** -0.5, ALU.mult, small)
    K.load_distances(ctx)
    big_ready, _ = K.bias_table(ctx, "dsa", w["rel_bias_2"], big, relb)

    s = K.wring.take()
    width = IH * ID + 4 * ID + IH
    v = s.t[:, 0:KD * width].rearrange("p (k n) -> p k n", k=KD)
    src = w_in.rearrange("(k p) n -> p k n", p=P)
    got = K.load(s, [(v[:, :, 0:IH * ID + ID], src[:, :, COL2_IQ:COL2_IW])]
                 + [(v[:, :, 256 + q * ID:256 + (q + 1) * ID], src[:, :, COL2_IK:COL2_IW]) for q in range(1, 4)]
                 + [(v[:, :, 256 + 4 * ID:width], src[:, :, COL2_IW:COL2_QB])])
    for j in range(2):
        b = K.banks.take()
        m = K.project(b, b.t[:, :], lambda k: v[:, k, j * P:(j + 1) * P], lambda k: hT[:, k, :], KD, got, ready)
        iq_ready = K.a(iqT[:, j, :], b.t[:, :], ACT.Copy, m)
        b.free = [iq_ready]
    b = K.banks.take()
    m = K.project(b, b.t[:, :], lambda k: v[:, k, 256:256 + 4 * ID], lambda k: hT[:, k, :], KD)
    ik_ready = K.a(ikT[:, :], b.t[:, :], ACT.Copy, m)
    b.free = [ik_ready]
    b = K.banks.take()
    for t in range(TT):
        m = K.project(b, b.t[:, t * IH:(t + 1) * IH], lambda k: hT[:, k, t * P:(t + 1) * P],
                      lambda k: v[:, k, 256 + 4 * ID:width], KD)
    s.free = [m]
    iw_ready = K.ts(iw[:, :, :], b.t[:, 0:TT * IH].rearrange("p (t h) -> p t h", t=TT), IH ** -0.5, ALU.mult, m)
    b.free = [iw_ready]

    rel = K.ring(ctx, "idx_r", 3, [P, S])
    score_ready = {}
    for i in range(1, TT):
        n = (i + 1) * P
        for h in range(IH):
            rows = slice((h % 4) * ID, (h % 4 + 1) * ID)
            b, r = K.banks.take(), rel.take()
            m = K.mm(b.t[:, 0:n], iqT[rows, h // 4, i * P:(i + 1) * P], ikT[rows, 0:n], b.free, iq_ready, ik_ready)
            e = K.a(r.t[:, 0:n], b.t[:, 0:n], ACT.Relu, m, r.free, scale=ID ** -0.5)
            b.free = [e]
            if h == 0:
                k = K.ts(score[:, i, 0:n], r.t[:, 0:n], iw[:, i, h:h + 1], ALU.mult, e, iw_ready)
            else:
                k = K.stt(score[:, i, 0:n], r.t[:, 0:n], iw[:, i, h:h + 1], score[:, i, 0:n], ALU.mult, ALU.add, e, k)
            r.free = [k]
        diag = score[:, i, i * P:n]
        score_ready[i] = K.pool.do(lambda e, d=diag: e.affine_select(
            out=d, in_=d, compare_op=ALU.is_ge, fill=NEG, base=0, pattern=[[-1, P]], channel_multiplier=1), k)

    def feature_major(dst, at, gain):
        s, v, got = K.weights(w_in, at, 512)
        for f in range(4):
            b = K.banks.take()
            m = K.project(b, b.t[:, :], lambda k: v[:, k, f * P:(f + 1) * P], lambda k: hT[:, k, :], KD, got)
            r = K.head_norm(tmp, b, m, dst[:, f, :], gain)
        s.free = [m]
        return r

    q_ready = feature_major(qT, COL2_Q, gains[:, 0:1])
    k_ready = feature_major(kT, COL2_K, gains[:, 1:2])
    s, v, got = K.weights(w_in, COL2_V, 512)
    for t in range(TT):
        b = K.banks.take()
        m = K.project(b, b.t[:, :], lambda k: hT[:, k, t * P:(t + 1) * P], lambda k: v[:, k, :], KD, got)
        v_ready = K.a(va[:, t, :], b.t[:, :], ACT.Copy, m)
        b.free = [v_ready]
    s.free = [m]

    K.meet()
    ctx.close()
    ctx = outer
    mask_ready = {}
    chain = dict(score_ready)
    for i in range(1, TT):
        n = (i + 1) * P
        sc, t8 = score[:, i, 0:n], top[:, i, :]
        for _ in range(TOPK // 8):
            k = K.dve.do(lambda e, sc=sc, t8=t8: e.max(t8, sc), chain[i])
            chain[i] = K.dve.do(lambda e, sc=sc, t8=t8: e.match_replace(sc, t8, sc, TAKEN), k)
        mask_ready[i] = K.ts(masks[:, i, 0:n], sc, 0.5 * TAKEN, ALU.is_gt, chain[i], s2=NEG, op1=ALU.mult)

    def extra(i, out):
        return K.mm(out, eye[:, :], masks[:, i, 0:(i + 1) * P], mask_ready[i], eye_ready, start=False)

    o = spare
    rc = K.sb(ctx, "dsa_rc", [P, TT, NH])
    o_ready = {}

    def finish(i, b, got, sums, sums_ready):
        k = K.recip(rc[:, i, :], sums, sums_ready)
        k = K.tt(o[:, i, :].rearrange("p (h d) -> p h d", h=NH), b.t[:, :].rearrange("p (h d) -> p h d", h=NH),
                 spread(rc[:, i, :], DH), ALU.mult, k, got)
        o_ready[i] = k
        return k

    K.attention(ctx, "dsa", [(lambda h: qT[(h % 2) * DH:(h % 2 + 1) * DH, h // 2, :],
                              lambda h: kT[(h % 2) * DH:(h % 2 + 1) * DH, h // 2, :],
                              lambda h, j: va[:, j, h * DH:(h + 1) * DH],
                              [q_ready, k_ready, v_ready, big_ready], finish, extra)], big)
    return K.to_fm(o, o_ready, oT)


def gla(K, ctx, hT, ready, oT):
    w, c = K.w, K.c
    w_in = w["w_in_2"]
    sm = K.channel("gla_small")
    w2 = K.sb(ctx, "gla_w2", [RANK, 2 * P])
    cols = K.sb(ctx, "gla_cols", [P, 3])
    small = sm.dma(K.act, w2[:, :], w["gla_gate_w2_2"])
    small = sm.dma(K.act, cols[:, 0:2], w["gla_gate_b_2"].rearrange("o (k p) -> p (o k)", p=P), slow=True)
    small = sm.dma(K.act, cols[:, 2:3], w["gla_out_norm_g_2"].rearrange("o d -> d o"), slow=True)
    NCH = S // GC
    ones = K.sb(ctx, "gla_ones", [P, P])
    ones_ready = K.zero(ones[:, :], value=1.0)
    tmp = K.ring(ctx, "gla_tmp", 4, [P, S])
    rg = K.sb(ctx, "rgT", [P, 4, S])
    vb = K.sb(ctx, "vb", [P, TT, RW])
    qT, kT = K.sb(ctx, "gla_qT", [P, 2, S]), K.sb(ctx, "gla_kT", [P, 2, S])
    glr = K.sb(ctx, "glr", [RANK, S])

    s, v, got = K.weights(w_in, COL2_QB, 512)
    for j in range(4):
        b = K.banks.take()
        m = K.project(b, b.t[:, :], lambda k: v[:, k, j * P:(j + 1) * P], lambda k: hT[:, k, :], KD, got, ready)
        if j < 2:
            qk_ready = K.a(qT[:, j, :], b.t[:, :], ACT.Copy, m, scale=BK ** -0.5)
        else:
            qk_ready = K.a(kT[:, j - 2, :], b.t[:, :], ACT.Copy, m)
        b.free = [qk_ready]
    s.free = [m]
    s, v, got = K.weights(w_in, COL2_LR, RANK)
    b = K.banks.take()
    m = K.project(b, b.t[0:RANK, :], lambda k: v[:, k, :], lambda k: hT[:, k, :], KD, got)
    s.free = [m]
    glr_ready = K.a(glr[:, :], b.t[0:RANK, :], ACT.Copy, m)
    b.free = [glr_ready]
    L, Lc, E1, E2 = (K.sb(ctx, f"gla_{n}", [P, 2, NCH, GC + 1]) for n in ("L", "Lc", "E1", "E2"))
    ready0 = K.zero(L[:, :, :, 0:1])
    qt, kt = K.sb(ctx, "gla_qt", [P, 2, S]), K.sb(ctx, "gla_kt", [P, 2, S])
    ktm = K.sb(ctx, "gla_ktm", [P, 2, TT, P])
    A = K.sb(ctx, "gla_A", [P, 2, 2, TT, P])
    ready0 = [ready0, K.zero(A[:, :, :, :, :])]
    zs = K.sb(ctx, "gla_zs", [P, 2, NCH])
    pair = []
    for j in range(2):
        b = K.banks.take()
        m = K.mm(b.t[:, :], w2[:, j * P:(j + 1) * P], glr[:, :], glr_ready, small, b.free)
        x, t = tmp.take(), tmp.take()
        kx = K.ts(x.t[:, :], b.t[:, :], cols[:, j:j + 1], ALU.add, m, x.free)
        b.free = [kx]
        k = K.a(t.t[:, :], x.t[:, :], ACT.Abs, kx, t.free)
        k = K.a(t.t[:, :], t.t[:, :], ACT.Exp, k, scale=-1.0)
        k = K.a(t.t[:, :], t.t[:, :], ACT.Ln, k, bias=1.0)
        k = K.stt(x.t[:, :], x.t[:, :], 0.0, t.t[:, :], ALU.min, ALU.subtract, k)
        t.free = [k]
        k = K.ts(x.t[:, :], x.t[:, :], 1.0 / TEMP, ALU.mult, k)
        for n in range(NCH):
            ks = K.dve.do(lambda e, n=n, x=x, j=j: e.tensor_tensor_scan(
                L[:, j, n, 1:GC + 1], ones[:, 0:GC], x.t[:, n * GC:(n + 1) * GC], 0.0, ALU.mult, ALU.add),
                k, ones_ready, ready0)
        x.free = [ks]
        k = K.tt(Lc[:, j, :, :], L[:, j, :, :], L[:, j, :, 32:33].broadcast_to([P, NCH, GC + 1]), ALU.subtract, ks)
        e1 = K.a(E1[:, j, :, :], Lc[:, j, :, :], ACT.Exp, k)
        e2 = K.a(E2[:, j, :, :], Lc[:, j, :, :], ACT.Exp, k, scale=-1.0)
        v8 = lambda y: y.rearrange("p (n t) -> p n t", n=NCH)
        qt_r = K.tt(v8(qt[:, j, :]), v8(qT[:, j, :]), E1[:, j, :, 1:GC + 1], ALU.mult, e1, qk_ready)
        kt_r = K.tt(v8(kt[:, j, :]), v8(kT[:, j, :]), E2[:, j, :, 1:GC + 1], ALU.mult, e2, qk_ready)
        zs_r = K.tt(zs[:, j, 0:NCH - 1], E1[:, j, 0:NCH - 1, GC:GC + 1].rearrange("p n o -> p (n o)"),
                    E2[:, j, 1:NCH, 0:1].rearrange("p n o -> p (n o)"), ALU.mult, e1, e2)
        b = K.banks.take()
        for n in range(TT):
            m = K.tr(b.t[:, n * P:(n + 1) * P], kt[:, j, n * P:(n + 1) * P], kt_r, b.free, signal=(n == TT - 1))
        ktm_r = K.a(ktm[:, j, :, :], b.t[:, :].rearrange("p (n t) -> p n t", n=TT), ACT.Copy, m)
        b.free = [ktm_r]
        for hh in range(2):
            hp = slice(hh * BK, (hh + 1) * BK)
            b = K.banks.take()
            for n in range(TT):
                ts_ = slice(n * P, (n + 1) * P)
                m = K.mm(b.t[:, ts_], kt[hp, j, ts_], qt[hp, j, ts_], kt_r, qt_r, b.free, signal=(n == TT - 1))
            a_r = K.dve.do(lambda e, b=b, j=j, hh=hh: e.copy_predicated(
                A[:, j, hh, :, :], c("mask_gla").bitcast(I32).rearrange("p (x t) -> p x t", x=4),
                b.t[:, :].rearrange("p (x t) -> p x t", x=4)), m, ready0)
            b.free = [a_r]
        pair.append((qt_r, zs_r, ktm_r, a_r))
    s, v, got = K.weights(w_in, COL2_VB, 512)
    for t in range(TT):
        b = K.banks.take()
        m = K.project(b, b.t[:, :], lambda k: hT[:, k, t * P:(t + 1) * P], lambda k: v[:, k, :], KD, got)
        vb_ready = K.a(vb[:, t, :], b.t[:, :], ACT.Copy, m)
        b.free = [vb_ready]
    s.free = [m]
    s, v, got = K.weights(w_in, COL2_RG, 512)
    for f in range(4):
        b, t = K.banks.take(), tmp.take()
        m = K.project(b, b.t[:, :], lambda k: v[:, k, f * P:(f + 1) * P], lambda k: hT[:, k, :], KD, got)
        e = K.a(t.t[:, :], b.t[:, :], ACT.Sigmoid, m, t.free)
        rg_ready = K.tt(rg[:, f, :], b.t[:, :], t.t[:, :], ALU.mult, m, e)
        b.free = t.free = [rg_ready]
    s.free = [m]
    Z = K.sb(ctx, "gla_Z", [P, 2, 2 * BV])
    z_r = [K.zero(Z[:, j, :]) for j in range(2)]
    o = K.sb(ctx, "gla_o", [P, TT, RW])
    o_r = {}
    for n in range(TT):
        for j in range(2):
            qt_r, zs_r, ktm_r, a_r = pair[j]
            b = K.banks.take()
            for hh in range(2):
                h = 2 * j + hh
                K.mm(b.t[:, hh * BV:(hh + 1) * BV], A[:, j, hh, n, :], vb[:, n, h * BV:(h + 1) * BV],
                     a_r, vb_ready, b.free, start=(hh == 0), stop=False, signal=False, loose=True)
            for half in range(2):
                ch = 2 * n + half
                rows = slice(half * GC, (half + 1) * GC)
                m = K.mm(b.t[rows, 0:2 * BV], qt[:, j, n * P + half * GC:n * P + (half + 1) * GC], Z[:, j, :],
                         z_r[j], qt_r, start=False, stop=(half == 1), loose=True)
                if ch < NCH - 1:
                    b2 = K.banks.take()
                    m2 = K.mm(b2.t[:, 0:2 * BV], ktm[rows, j, n, :], vb[rows, n, 2 * j * BV:(2 * j + 2) * BV],
                              ktm_r, b2.free)
                    for hh in range(2):
                        hp, cs = slice(hh * BK, (hh + 1) * BK), slice(hh * BV, (hh + 1) * BV)
                        k = K.tt(Z[hp, j, cs], Z[hp, j, cs], b2.t[hp, cs], ALU.add, m, m2)
                    b2.free = [k]
                    z_r[j] = K.ts(Z[:, j, :], Z[:, j, :], zs[:, j, ch:ch + 1], ALU.mult, k, zs_r)
            e = K.a(o[:, n, j * 2 * BV:(j + 1) * 2 * BV], b.t[:, 0:2 * BV], ACT.Copy, m)
            b.free = [e]
            o_r[n] = e
    st = K.sb(ctx, "gla_st", [P, TT, 3, BH])
    for n in range(TT):
        t = tmp.take()
        sq = t.t[:, :].rearrange("p (h d) -> p h d", h=BH)
        o3 = o[:, n, :].rearrange("p (h d) -> p h d", h=BH)
        ms, rc, rs = (st[:, n, q, :] for q in range(3))
        k = K.a(sq, o3, ACT.Square, o_r[n], t.free)
        k = K.red(ms, sq, ALU.add, k)
        t.free = [k]
        k = K.ts(ms, ms, 1.0 / BV, ALU.mult, k, s2=RMS_EPS, op1=ALU.add)
        k = K.recip(rc, ms, k)
        k = K.a(rs, rc, ACT.Sqrt, k)
        o_r[n] = K.tt(o3, o3, spread(rs, BV), ALU.mult, k)
    for f in range(4):
        b = K.banks.take()
        for n in range(TT):
            m = K.tr(b.t[:, n * P:(n + 1) * P], o[:, n, f * P:(f + 1) * P], o_r[n], b.free, signal=(n == TT - 1))
        k = K.stt(oT[:, f, :], b.t[:, :], cols[:, 2:3], rg[:, f, :], ALU.mult, ALU.mult, m, rg_ready)
        b.free = [k]
    return k


def add_mixed(K, ctx, o1T, o2T, ready, x):
    K.cut_ring(ctx, 5)
    oT = tuple(K.sb(ctx, f"o_{n}", [P, KD, S], F32R) for n in ("hi", "lo"))
    o_ready = [K.halves(oT[0][:, k, :], oT[1][:, k, :], (o1T if k < 4 else o2T)[:, k % 4, :], ready[k // 4])
               for k in range(KD)]
    return add_product(K, K.w["w_out_2"], oT, KD, o_ready, x)


def moe(K, ctx, hT, ready, h_dram, h_stored, x, x_ready, out):
    nc, w, c = K.nc, K.w, K.c
    sm = K.channel("moe_small")
    wr = K.sb(ctx, "w_router", [P, KD, XG + NE])
    br = K.sb(ctx, "b_router", [P, XG + NE])
    small = sm.dma(K.act, wr[:, :, 0:XG], w["w_router_group_2"].rearrange("(k p) n -> p k n", p=P))
    small = sm.dma(K.act, wr[:, :, XG:], w["w_router_expert_2"].rearrange("(k p) n -> p k n", p=P))
    small = sm.dma(K.act, br[:, 0:XG], w["b_router_group_2"].rearrange("o n -> (o n)").partition_broadcast(P))
    small = sm.dma(K.act, br[:, XG:], w["b_router_expert_2"].rearrange("o n -> (o n)").partition_broadcast(P))
    lg = K.sb(ctx, "logits", [P, TT, XG + NE])
    pad = K.sb(ctx, "group_pad", [P, TT, XE])
    z = K.zero(pad[:, :, :], value=NEG)
    b = K.banks.take()
    for t in range(TT):
        m = K.project(b, b.t[:, t * 36:(t + 1) * 36], lambda k: hT[:, k, t * P:(t + 1) * P], lambda k: wr[:, k, :],
                      KD, small, ready)
    k = K.tt(lg[:, :, :], b.t[:, 0:TT * 36].rearrange("p (t n) -> p t n", t=TT), spread(br[:, :], TT, 1), ALU.add, m)
    b.free = [k]
    lg_r = k
    k = K.cp(pad[:, :, 0:XG], lg[:, :, 0:XG], k, z)
    top = K.sb(ctx, "mx", [P, 2, TT, 8])
    idx = K.sb(ctx, "mi", [P, 2, TT, 8], U32)
    idf = K.sb(ctx, "mif", [P, 2, TT, 8])
    esel = K.sb(ctx, "esel", [P, TT, XE])
    t8 = K.sb(ctx, "moe_t8", [P, TT, XE])
    g1h = K.sb(ctx, "g1h", [P, TT, XE])
    e1h = K.sb(ctx, "e1h", [P, 2, TT, XE])
    s4 = K.sb(ctx, "moe_s4", [P, 8, TT])

    def best(j, src, k):
        for t in range(TT):
            k1 = K.dve.do(lambda e, t=t: e.max(top[:, j, t, :], src[:, t, :]), k)
            k1 = K.dve.do(lambda e, t=t: e.max_index(idx[:, j, t, :], top[:, j, t, :], src[:, t, :]), k1)
        return K.cp(idf[:, j, :, :], idx[:, j, :, :], k1)

    iota = spread(c("iota"), TT, 1)
    k = best(0, pad, k)
    k = K.tt(g1h[:, :, :], iota, idf[:, 0, :, 0:1].broadcast_to([P, TT, XE]), ALU.is_equal, k)
    g_r = k
    k = K.tt(t8[:, :, :], pad[:, :, :], top[:, 0, :, 0:1].broadcast_to([P, TT, XE]), ALU.subtract, k)
    k = K.a(t8[:, :, :], t8[:, :, :], ACT.Exp, k)
    k = K.red(s4[:, 0, :], t8[:, :, :], ALU.add, k)
    gw_r = K.recip(s4[:, 1, :], s4[:, 0, :], k)
    for g in range(XG):
        src = lg[:, :, XG + g * XE:XG + (g + 1) * XE]
        on = g1h[:, :, g:g + 1].broadcast_to([P, TT, XE])
        if g == 0:
            k = K.tt(esel[:, :, :], src, on, ALU.mult, g_r)
        else:
            k1 = K.tt(t8[:, :, :], src, on, ALU.mult, k, gw_r)
            k = K.tt(esel[:, :, :], esel[:, :, :], t8[:, :, :], ALU.add, k1)
    k = best(1, esel, k)
    for j in range(2):
        e_r = K.tt(e1h[:, j, :, :], iota, idf[:, 1, :, j:j + 1].broadcast_to([P, TT, XE]), ALU.is_equal, k)
    d = s4[:, 2, :]
    k = K.tt(d, top[:, 1, :, 1], top[:, 1, :, 0], ALU.subtract, k)
    k = K.a(d, d, ACT.Exp, k)
    k = K.ts(s4[:, 3, :], d, 1.0, ALU.add, k)
    k = K.recip(s4[:, 4, :], s4[:, 3, :], k)
    k = K.tt(s4[:, 5, :], s4[:, 4, :], s4[:, 1, :], ALU.mult, k)
    wt_r = K.tt(s4[:, 6, :], s4[:, 5, :], d, ALU.mult, k)
    weight = (s4[:, 5, :], s4[:, 6, :])
    mem = K.sb(ctx, "member", [P, 2, TT, NE])
    both = K.sb(ctx, "member2", [P, TT, NE])
    for j in range(2):
        for g in range(XG):
            k = K.tt(mem[:, j, :, g * XE:(g + 1) * XE], e1h[:, j, :, :], g1h[:, :, g:g + 1].broadcast_to([P, TT, XE]),
                     ALU.mult, e_r)
    k = K.tt(both[:, :, :], mem[:, 0, :, :], mem[:, 1, :, :], ALU.add, k)
    b = K.banks.take()
    for t in range(TT):
        m = K.mm(b.t[:, t * NE:(t + 1) * NE], c("before"), both[:, t, :], k, b.free, start=True, stop=(t == 0))
        for u in range(t):
            m = K.mm(b.t[:, t * NE:(t + 1) * NE], c("allones"), both[:, u, :], start=False, stop=(u == t - 1))
    for t in range(TT):
        m = K.mm(b.t[:, TT * NE:(TT + 1) * NE], c("allones"), both[:, t, :], start=(t == 0), stop=(t == TT - 1))
    cnt = K.sb(ctx, "counts", [P, 4, NE])
    n_e, tl, end, base = (cnt[:, q, :] for q in range(4))
    rank = K.sb(ctx, "rank", [P, TT, NE])
    kr = K.cp(rank[:, :, :], b.t[:, 0:TT * NE].rearrange("p (t n) -> p t n", t=TT), m)
    k = K.cp(n_e, b.t[:, TT * NE:(TT + 1) * NE], m)
    b.free = [k]
    k = K.ts(tl, n_e, 0.5, ALU.is_gt, k)
    for q in range(1, TT):
        k = K.stt(tl, n_e, P * q + 0.5, tl, ALU.is_gt, ALU.add, k)
    onesr = K.sb(ctx, "moe_ones", [P, NE])
    z = K.zero(onesr[:, :], value=1.0)
    k = K.dve.do(lambda e: e.tensor_tensor_scan(end, onesr[:, :], tl, 0.0, ALU.mult, ALU.add), k, z)
    end_r = k
    k = K.tt(base, end, tl, ALU.subtract, k)
    tile_ = K.sb(ctx, "tile_of", [P, TT, NE])
    where_ = K.sb(ctx, "slot_where", [P, 2, TT, NE])
    prod = K.sb(ctx, "pos_prod", [P, TT, NE])
    posf = K.sb(ctx, "posf", [P, 2, 2, TT])
    posi = K.sb(ctx, "posi", [P, 2, 2, TT], U32)
    kb = k
    k = K.ts(tile_[:, :, :], rank[:, :, :], P - 0.5, ALU.is_gt, kr)
    for q in range(2, TT):
        k = K.stt(tile_[:, :, :], rank[:, :, :], P * q - 0.5, tile_[:, :, :], ALU.is_gt, ALU.add, k)
    k = K.stt(rank[:, :, :], tile_[:, :, :], -float(P), rank[:, :, :], ALU.mult, ALU.add, k)
    k = K.tt(tile_[:, :, :], tile_[:, :, :], spread(base, TT, 1), ALU.add, k, kb)
    k = K.stt(where_[:, 0, :, :], tile_[:, :, :], float(P), rank[:, :, :], ALU.mult, ALU.add, k)
    k = K.stt(where_[:, 1, :, :], rank[:, :, :], float(NTILE), tile_[:, :, :], ALU.mult, ALU.add, k)
    for q in range(2):
        for j in range(2):
            k = K.tt(prod[:, :, :], mem[:, j, :, :], where_[:, q, :, :], ALU.mult, k)
            k = K.red(posf[:, q, j, :], prod[:, :, :], ALU.add, k)
    pos_r = K.cp(posi[:, :, :, :], posf[:, :, :, :], k)
    cmp_ = K.sb(ctx, "tile_cmp", [P, NTILE, NE])
    tef = K.sb(ctx, "tile_ef", [P, NTILE])
    tei = K.sb(ctx, "tile_ei", [P, NTILE], I32)
    k = K.tt(cmp_[:, :, :], spread(end, NTILE, 1), spread(c("tile_no"), NE, 2), ALU.is_le, end_r)
    k = K.red(tef[:, :], cmp_[:, :, :], ALU.add, k)
    k = K.ts(tef[:, :], tef[:, :], float(NE - 1), ALU.min, k)
    te_r = K.cp(tei[:, :], tef[:, :], k)

    tab = nc.dram_tensor("slot_token", (NTILE * P, 1), U32, kind="Internal").ap()
    zt = K.sb(ctx, "zero_tab", [P, NTILE], U32)
    tok = K.sb(ctx, "tokens", [P, TT], U32)
    slot_tok = K.sb(ctx, "slot_tok", [P, NTILE], U32)
    k = K.zero(zt[:, :], lane=K.dve, value=0)
    z_s = K.store(tab.rearrange("(p t) o -> p (t o)", p=P), zt[:, :], k)
    k = K.cp(tok[:, :], c("token_no"))
    sc = K.channel("scatter")
    K.pool.wait(z_s, k, pos_r)
    for j in range(2):
        for t in range(TT):
            sc.count += 16
            K.pool.queue.append(lambda e, j=j, t=t: e.indirect_dma_start(
                out=tab[:, :], out_offset=bass.IndirectOffsetOnAxis(ap=posi[:, 1, j, t:t + 1], axis=0),
                in_=tok[:, t:t + 1], in_offset=None).then_inc(sc.sem, 16))
    sc_r = (sc.sem, sc.count)
    K.stores.append(sc_r)
    st_r = K.channel("slot_tok_in").dma(K.pool, slot_tok[:, :], tab.rearrange("(p t) o -> p (t o)", p=P), sc_r)

    ys = nc.dram_tensor("slot_out", (NTILE * P, D), F32, kind="Internal").ap()
    wg, wu, wd = w["w_exp_gate_2"], w["w_exp_up_2"], w["w_exp_down_2"]
    gring = K.ring(ctx, "gath", 3, [P, D], channels=True)
    dring = K.ring(ctx, "wd", 4, [P, 2, D], channels=True)
    hgT = K.ring(ctx, "hgT", 2, [P, KD, P])
    hd = K.ring(ctx, "hid", 2, [P, 2, DE])
    hdT = K.ring(ctx, "hidT", 2, [P, 2, P])
    yr = K.ring(ctx, "yout", 2, [P, D], channels=True)
    gathered, wts = {}, {}
    y_stored = []

    def gather(n):
        g = gring.take()
        K.pool.wait(st_r, g.free, h_stored)
        g.channel.count += 16
        K.pool.queue.append(lambda e, g=g, n=n: e.indirect_dma_start(
            out=g.t[:, :], out_offset=None, in_=h_dram[:, :],
            in_offset=bass.IndirectOffsetOnAxis(ap=slot_tok[:, n:n + 1], axis=0)).then_inc(g.channel.sem, 16))
        gathered[n] = (g, (g.channel.sem, g.channel.count))

    def fetch(n):
        s, s2 = K.wring.take(), dring.take()
        K.sp.wait(te_r, s.free, s2.free)
        v = s.t[:, :].rearrange("p (two k n) -> p two k n", two=2, k=KD)
        s.channel.count += 32
        s2.channel.count += 16

        def issue(e, n=n, s=s, s2=s2, v=v):
            r = e.value_load(tei[0:1, n:n + 1], min_val=0, max_val=NE - 1)
            for two, src in ((0, wg), (1, wu)):
                e.dma_start(v[:, two, :, :], src[bass.ds(r, 1), :, :].rearrange("o (p k) n -> p (o k) n", k=KD)
                            ).then_inc(s.channel.sem, 16)
            e.dma_start(s2.t[:, :, :], wd[bass.ds(r, 1), :, :].rearrange("o (p k) n -> p (o k) n", k=2)
                        ).then_inc(s2.channel.sem, 16)
        K.sp.queue.append(issue)
        wts[n] = (s, v, (s.channel.sem, s.channel.count), s2, (s2.channel.sem, s2.channel.count))

    turned, hidden, hidden_t = {}, {}, {}

    def turn(n):
        g, g_r = gathered.pop(n)
        t = hgT.take()
        for half in range(2):
            b = K.banks.take()
            for j in range(4):
                q = half * 4 + j
                m = K.tr(b.t[:, j * P:(j + 1) * P], g.t[:, q:D:KD], g_r, b.free, signal=(j == 3))
            src = b.t[:, :].rearrange("p (k n) -> p k n", k=4)
            e = K.a(t.t[:, half * 4:half * 4 + 4, :], src, ACT.Copy, m, t.free) if half else \
                K.cp(t.t[:, 0:4, :], src, m, t.free)
            b.free = [e]
            if half == 0:
                e0 = e
        g.free = [m]
        turned[n] = (t, e, e0)

    def up(n):
        t, e, e0 = turned.pop(n)
        s, v, w_r, s2, d_r = wts[n]
        b = K.banks.take()
        m = K.project(b, b.t[:, :].rearrange("p (two n) -> p two n", two=2), lambda k: t.t[:, k, :],
                      lambda k: v[:, :, k, :], KD, w_r, e, e0)
        s.free = [m]
        t.free = [m]
        hb = hd.take()
        k = K.a(hb.t[:, 0, :], b.t[:, 0:DE], ACT.Sigmoid, m, hb.free)
        k = K.tt(hb.t[:, 0, :], hb.t[:, 0, :], b.t[:, 0:DE], ALU.mult, k)
        k = K.tt(hb.t[:, 1, :], hb.t[:, 0, :], b.t[:, DE:2 * DE], ALU.mult, k)
        b.free = [k]
        hidden[n] = (hb, k)

    def turn_hidden(n):
        hb, k = hidden.pop(n)
        ht = hdT.take()
        b = K.banks.take()
        for j in range(2):
            m = K.tr(b.t[:, j * P:(j + 1) * P], hb.t[:, 1, j:DE:2], k, b.free, signal=(j == 1))
        hb.free = [m]
        e = K.cp(ht.t[:, :, :], b.t[:, 0:2 * P].rearrange("p (k n) -> p k n", k=2), m, ht.free)
        b.free = [e]
        hidden_t[n] = (ht, e)

    def down(n):
        ht, e = hidden_t.pop(n)
        s, v, w_r, s2, d_r = wts.pop(n)
        yb = yr.take()
        for half in range(2):
            b = K.banks.take()
            m = K.project(b, b.t[:, :], lambda k: ht.t[:, k, :], lambda k: s2.t[:, k, half * 512:(half + 1) * 512],
                          2, d_r, e)
            dst = yb.t[:, half * 512:(half + 1) * 512]
            q = K.a(dst, b.t[:, :], ACT.Copy, m, yb.free) if half else K.cp(dst, b.t[:, :], m, yb.free)
            b.free = [q]
            if half == 0:
                q0 = q
        ht.free = s2.free = [m]
        t = K.store(ys[n * P:(n + 1) * P, :], yb.t[:, :], q, q0, lane=K.act, channel=yb.channel)
        yb.free = [t]
        y_stored.append(t)

    gather(0)
    for n in range(NTILE + 3):
        if n < NTILE:
            fetch(n)
            if n + 1 < NTILE:
                gather(n + 1)
            turn(n)
        if 0 <= n - 3:
            down(n - 3)
        if 0 <= n - 1 < NTILE:
            up(n - 1)
        if 0 <= n - 2 < NTILE:
            turn_hidden(n - 2)

    for t in range(TT):
        s, ch = dring.take(), K.channel(f"fin{t}")
        K.pool.wait(y_stored[-2:], s.free)
        for j in range(2):
            ch.count += 16
            K.pool.queue.append(lambda e, s=s, ch=ch, j=j, t=t: e.indirect_dma_start(
                out=s.t[:, j, :], out_offset=None, in_=ys[:, :],
                in_offset=bass.IndirectOffsetOnAxis(ap=posi[:, 0, j, t:t + 1], axis=0)).then_inc(ch.sem, 16))
        k = (ch.sem, ch.count)
        for j in range(2):
            k = K.stt(x[:, t, :], s.t[:, j, :], weight[j][:, t:t + 1], x[:, t, :], ALU.mult, ALU.add, k, wt_r, x_ready[t])
        s.free = [k]
        K.store(out[t * P:(t + 1) * P, :], x[:, t, :], k)


def build(nc, w, consts, dist, where, out, probes=()):
    with ExitStack() as ctx:
        K = Core(nc, ctx, w)
        K.where = where
        K.probe = dict(probes)
        K.banks = Ring([Slot(ctx.enter_context(nc.psum_tensor(f"bank{i}", [P, 512], F32))) for i in range(8)])
        K.consts = K.sb(ctx, "consts", [P, consts.shape[1]])
        K.dist_dram = dist
        x = K.sb(ctx, "x_res", [P, TT, D])
        K.wring = K.ring(ctx, "w", 3, [P, 8 * 512], channels=True)
        xin = [K.channel(f"x_in{t}").dma(K.sp, x[:, t, :], w["x"][t * P:(t + 1) * P, :]) for t in range(TT)]
        K.consts_ready = K.channel("const_in").dma(K.act, K.consts[:, :], consts)
        for lane in (K.pe, K.act, K.dve, K.pool):
            lane.wait(K.consts_ready)

        gch = K.channel("gain_in")

        def normed(name, gname, ready, hT, keep=None):
            with ExitStack() as c2:
                gain = K.sb(c2, "norm_gain", [P, D])
                g = gch.dma(K.act, gain[:, :], w[gname].rearrange("o n -> (o n)").partition_broadcast(P))
                done = K.norm_to_fm(c2, name, x, gain[:, :], g, ready, hT, K.pe.last(), keep)
                K.meet()
            return done

        def probe(name, ap):
            if name in K.probe:
                K.meet()
                K.sp.wait([t for t in K.met if t])
                K.store(K.probe[name], ap)

        def block_buffers(c1):
            return K.sb(c1, "hT", [P, KD, S]), K.sb(c1, "oaT", [P, 4, S]), K.sb(c1, "obT", [P, 4, S])

        with ExitStack() as c1:
            hT, oaT, obT = block_buffers(c1)
            ready = normed("n1", "attn_norm_g", xin, hT)
            probe("hT", hT[:, :, :])
            with ExitStack() as c2:
                oa = nsa(K, c2, hT, ready, oaT, obT)
                K.meet()
            probe("oaT", oaT[:, :, :])
            with ExitStack() as c2:
                ob = rwkv(K, c2, hT, ready, obT)
                K.meet()
            probe("obT", obT[:, :, :])
            with ExitStack() as c2:
                done = merge(K, c2, hT, oaT, obT, oa, ob, x)
                K.meet()
        probe("x1", x[:, :, :])
        with ExitStack() as c1:
            hp = tuple(K.sb(c1, f"h2_{n}", [P, KD, S], F32R) for n in ("hi", "lo"))
            ready = normed("n2", "ffn_norm_g", done, hp)
            with ExitStack() as c2:
                done = ffn(K, c2, hp, ready, x)
                K.meet()
        probe("x2", x[:, :, :])
        with ExitStack() as c1:
            hT, oaT, obT = block_buffers(c1)
            ready = normed("n3", "norm1_g_2", done, hT)
            with ExitStack() as c2:
                K.more_weights(c2)
                oa = selected_attention(K, c2, hT, ready, oaT, obT)
                K.meet()
            probe("o2aT", oaT[:, :, :])
            with ExitStack() as c2:
                K.more_weights(c2)
                ob = gla(K, c2, hT, ready, obT)
                K.meet()
            probe("o2bT", obT[:, :, :])
            with ExitStack() as c2:
                done = add_mixed(K, c2, oaT, obT, [oa, ob], x)
                K.meet()
            probe("x3", x[:, :, :])
            h_dram = nc.dram_tensor("h_rows", (S, D), F32, kind="Internal").ap()
            n_stores = len(K.stores)
            ready = normed("n4", "norm2_g_2", done, hT, keep=h_dram)
            h_stored = K.stores[n_stores:]
            with ExitStack() as c2:
                K.more_weights(c2)
                moe(K, c2, hT, ready, h_dram, h_stored, x, done, out)
                K.meet()
        K.sp.wait(K.stores)

        block = ctx.enter_context(nc.Block())
        block.sync(K.sp.run)
        block.scalar(K.act.run)
        block.gpsimd(K.pool.run)
        block.vector(K.dve.run)
        block.tensor(K.pe.run)


_INS = [
    "x", "attn_norm_g", "w_in", "rel_bias", "q_norm_g", "k_norm_g", "cmp_pe_k", "cmp_w1_k", "cmp_w2_k",
    "cmp_pe_v", "cmp_w1_v", "cmp_w2_v", "rwkv_mu", "rwkv_w0", "rwkv_w2", "rwkv_a0", "rwkv_a2", "rwkv_g2",
    "rwkv_k_k", "rwkv_k_a", "rwkv_r_k", "rwkv_ln_g", "rwkv_ln_b", "w_proj_a", "w_proj_b", "w_out",
    "ffn_norm_g", "w_up", "conv_w", "conv_b", "w_down", "norm1_g_2", "w_in_2", "q_norm_g_2", "k_norm_g_2",
    "rel_bias_2", "gla_gate_w2_2", "gla_gate_b_2", "gla_out_norm_g_2", "w_out_2", "norm2_g_2",
    "w_router_group_2", "b_router_group_2", "w_router_expert_2", "b_router_expert_2", "w_exp_gate_2",
    "w_exp_up_2", "w_exp_down_2",
]


def kernel(**inputs):
    import concourse.bacc as _bacc
    from concourse.bass_utils import run_bass_kernel_spmd as _run

    nc = _bacc.Bacc("TRN2", target_bir_lowering=False, num_devices=1)
    arrays, w = {}, {}
    for name in _INS:
        a = np.ascontiguousarray(inputs[name])
        if a.shape[0] == 1 and a.ndim > 2:
            a = a.reshape(a.shape[1:])
        arrays[f"in_{name}"] = a
        w[name] = nc.dram_tensor(f"in_{name}", a.shape, mybir.dt.from_np(a.dtype), kind="ExternalInput").ap()
    table, where = constants()
    for name, a in (("consts", table), ("dist", distance_tables())):
        arrays[f"in_{name}"] = a
        w[name] = nc.dram_tensor(f"in_{name}", a.shape, F32, kind="ExternalInput").ap()
    out = nc.dram_tensor("out_x", (S, D), F32, kind="ExternalOutput").ap()
    build(nc, w, w.pop("consts"), w.pop("dist"), where, out)
    r = _run(nc, [arrays], core_ids=[0])
    return r.results[0]["out_x"].reshape(1, S, D)
```

```python
import math
from contextlib import ExitStack

import numpy as np

import concourse.bass as bass
from concourse import mybir

F32 = mybir.dt.float32
F32R = mybir.dt.float32r
BF16 = mybir.dt.bfloat16
I32 = mybir.dt.int32
U32 = mybir.dt.uint32
ALU = mybir.AluOpType
ACT = mybir.ActivationFunctionType
AX = mybir.AxisListType.X

P = 128
S, D = 512, 1024
TT = S // P
KD = D // P
NEG = -1e30
TAKEN = -3e38
RMS_EPS = 1e-6

DH, NH, NG, NR = 64, 8, 2, 4
KVW = NG * DH
CB, CS, CHID = 32, 16, 256
NC = S // CS - CB // CS + 1
NW = NH * DH
COL_Q, COL_KC = 0, NW
COL_VC, COL_KS, COL_VS, COL_KW, COL_VW = (COL_KC + i * KVW for i in range(1, 6))
COL_GATE = COL_KC + 6 * KVW
COL_R = COL_GATE + 3 * NH
RW = 512
COL_K, COL_V, COL_LORA = COL_R + RW, COL_R + 2 * RW, COL_R + 3 * RW
COL_GA = COL_LORA + 256
COL_GB = COL_GA + D
DFF = 2816
FT = DFF // P
GN_EPS = 64e-5
DECAY = math.exp(-0.5)
NORM_FLOOR = 1e-24
LN_SHIFT = 20
IH, ID, TOPK = 8, 32, 128
COL2_Q, COL2_K, COL2_V, COL2_IQ = 0, 512, 1024, 1536
COL2_IK = COL2_IQ + IH * ID
COL2_IW = COL2_IK + ID
COL2_QB = COL2_IW + IH
COL2_KB = COL2_QB + 256
COL2_VB = COL2_KB + 256
COL2_LR = COL2_VB + 512
COL2_RG = COL2_LR + 16
BH, BK, BV, RANK, TEMP, GC = 4, 64, 128, 16, 16.0, 64
XG, XE, NE, DE = 4, 8, 32, 256
NTILE = 2 * S // P + NE - 1


def t5_bucket(n):
    large = 16 + (np.log(np.maximum(n, 1).astype(np.float32) / np.float32(16)) / np.float32(math.log(8))
                  * np.float32(16)).astype(np.int32)
    return np.where(n < 16, n, np.minimum(large, 31))


def level_mask(m):
    i = np.arange(P)
    return ((i[:, None] // (2 * m) == i[None, :] // (2 * m))
            & (i[:, None] // m % 2 == 1) & (i[None, :] // m % 2 == 0)).astype(np.float32)


def constants():
    i = np.arange(P)
    parts = {}
    parts["ident"] = np.eye(P)
    parts["ones64"] = (i[:, None] // 64 == i[None, :] // 64) * 1.0
    parts["allones"] = np.ones((P, P))
    parts["before"] = (i[:, None] < i[None, :]) * 1.0
    strict, upto = (i[:, None] < i[None, :]) * 1.0, (i[:, None] <= i[None, :]) * 1.0
    parts["mask_rw"] = np.concatenate([strict, upto, strict, upto], 1)
    parts["mask_low"] = strict.T
    same = i[:, None] // GC == i[None, :] // GC
    parts["mask_gla"] = upto * same
    parts["lev0u"] = level_mask(1).T
    for lv in range(7):
        parts[f"lev{lv}"] = level_mask(1 << lv)
    parts["valid_c"] = np.stack([(i + P * t >= CB - 1) * 1.0 for t in range(TT)], 1)
    parts["iota"] = np.tile(np.arange(XE * 1.0), (P, 1))
    parts["slot_no"] = np.tile(np.arange(P * 1.0), (P, 1))
    parts["tile_no"] = np.tile(np.arange(NTILE * 1.0), (P, 1))
    parts["token_no"] = i[:, None] + P * np.arange(TT)[None, :] * 1.0
    parts["eps"] = np.full((P, 1), RMS_EPS)
    parts["ln_back"] = np.full((P, 1), 0.5 * LN_SHIFT * math.log(2.0))
    where, at = {}, 0
    for k, v in parts.items():
        where[k] = (at, at + v.shape[1])
        at += v.shape[1]
    return np.concatenate(list(parts.values()), 1).astype(np.float32), where


def distance_tables():
    def one_hot(n):
        t = np.zeros((33, n.size), np.float32)
        t[t5_bucket(np.maximum(n, 0)), np.arange(n.size)] = n >= 0
        t[32] = np.where(n < 0, np.float32(NEG), 0)
        return t
    return np.concatenate([one_hot(np.arange(1024) - 511), one_hot(np.arange(640) - 127)], 1)


class Lane:

    def __init__(self, sem, one_at_a_time=False):
        self.sem, self.count, self.queue, self.seen = sem, 0, [], {}
        self.one_at_a_time = one_at_a_time

    def wait(self, *tokens):
        for t in tokens:
            if t is None:
                continue
            if isinstance(t, list):
                self.wait(*t)
                continue
            sem, value = t
            if self.seen.get(id(sem), 0) < value:
                self.seen[id(sem)] = value
                self.queue.append(lambda eng, s=sem, v=value: eng.wait_ge(s, v))

    def do(self, make, *after, signal=True):
        self.wait(*after)
        if self.one_at_a_time:
            self.wait(self.last())
        if not signal:
            self.queue.append(make)
            return None
        self.count += 1
        self.queue.append(lambda eng, m=make, s=self.sem: m(eng).then_inc(s, 1))
        return (self.sem, self.count)

    def last(self):
        return (self.sem, self.count) if self.count else None

    def run(self, eng):
        for f in self.queue:
            f(eng)


class Channel:

    def __init__(self, sem):
        self.sem, self.count = sem, 0

    def dma(self, lane, out, in_, *after, slow=False):
        lane.wait(*after)
        self.count += 16
        lane.queue.append(lambda eng, s=self.sem: eng.dma_start(
            out, in_, allow_slow_non_contiguous=slow).then_inc(s, 16))
        return (self.sem, self.count)


class Slot:
    def __init__(self, t, channel=None):
        self.t, self.channel, self.free = t, channel, []


class Ring:

    def __init__(self, slots):
        self.slots, self.n = slots, 0

    def take(self):
        s = self.slots[self.n % len(self.slots)]
        self.n += 1
        return s


class Core:

    def __init__(self, nc, ctx, w):
        self.nc, self.ctx, self.w = nc, ctx, w
        self.names = {}
        self.pe, self.act, self.dve, self.pool, self.sp = (
            Lane(self.sem(f"done_{n}"), one_at_a_time=(n == "pool")) for n in ("pe", "act", "dve", "pool", "sp"))
        self.stores, self.deferred, self.side = [], [], []
        self.more_channel = self.channel("in_w_more")

    def fresh(self, name):
        self.names[name] = self.names.get(name, 0) + 1
        return name if self.names[name] == 1 else f"{name}_{self.names[name]}"

    def sem(self, name):
        name = self.fresh("sem " + name).replace("sem ", "")
        return self.ctx.enter_context(self.nc.semaphore(name))

    def channel(self, name):
        return Channel(self.sem(name))

    def sb(self, ctx, name, shape, dt=F32):
        name = self.fresh(name)
        return ctx.enter_context(self.nc.sbuf_tensor(name, shape, dt))

    def ring(self, ctx, name, n, shape, dt=F32, channels=False):
        return Ring([Slot(self.sb(ctx, f"{name}{i}", shape, dt),
                          self.channel(f"in_{name}{i}") if channels else None) for i in range(n)])

    def mm(self, out, lhsT, rhs, *after, start=True, stop=True, signal=True, loose=False):
        return self.pe.do(lambda e: e.matmul(out, lhsT, rhs, start=start, stop=stop, skip_group_check=loose),
                          *after, signal=signal)

    def tr(self, out, in_, *after, signal=True):
        n = in_.shape[0]
        return self.pe.do(lambda e: e.transpose(out, in_, self.c("ident")[0:n, 0:n]), *after, signal=signal)

    def a(self, out, in_, func, *after, bias=None, scale=None, accum=None):
        kw = {k: v for k, v in (("bias", bias), ("scale", scale), ("accum_out", accum)) if v is not None}
        return self.act.do(lambda e: e.activation(out, in_, func, **kw), *after)

    def tt(self, out, x, y, op, *after, lane=None):
        return (lane or self.dve).do(lambda e: e.tensor_tensor(out, x, y, op), *after)

    def ts(self, out, x, s1, op0, *after, s2=None, op1=None, lane=None):
        if op1 is None:
            return (lane or self.dve).do(lambda e: e.tensor_scalar(out, x, s1, None, op0), *after)
        return (lane or self.dve).do(lambda e: e.tensor_scalar(out, x, s1, s2, op0, op1), *after)

    def stt(self, out, x, s, y, op0, op1, *after):
        return self.dve.do(lambda e: e.scalar_tensor_tensor(out=out, in0=x, scalar=s, in1=y, op0=op0, op1=op1),
                           *after)

    def cp(self, out, x, *after, lane=None):
        return (lane or self.dve).do(lambda e: e.tensor_copy(out, x), *after)

    def red(self, out, x, op, *after):
        return self.dve.do(lambda e: e.tensor_reduce(out, x, AX, op), *after)

    def recip(self, out, x, *after):
        return self.dve.do(lambda e: e.reciprocal(out, x), *after)

    def zero(self, out, *after, lane=None, value=0.0):
        return (lane or self.pool).do(lambda e: e.memset(out, value), *after)

    def c(self, name):
        lo, hi = self.where[name]
        return self.consts[:, lo:hi]

    def store(self, out, in_, *after, lane=None, channel=None):
        ch = channel or self.channel(f"store{len(self.stores)}")
        t = ch.dma(lane or self.sp, out, in_, *after)
        self.stores.append(t)
        return t

    def meet(self):
        self.flush()
        tokens = [x.last() for x in (self.pe, self.act, self.dve, self.pool)]
        for lane in (self.pe, self.act, self.dve, self.pool):
            lane.wait([t for t in tokens if t])
        self.met = tokens

    def load_distances(self, ctx, rel_bias, relb_tile):
        z = self.zero(relb_tile[32:33, :], value=1.0)
        self.relb_ready = [z, self.channel("relb").dma(self.act, relb_tile[0:32, :], rel_bias)]
        self.dist = self.sb(ctx, "dist", list(self.dist_dram.shape))
        self.dist_ready = self.channel("dist_in").dma(self.act, self.dist[:, :], self.dist_dram, self.dve.last())

    def more_weights(self, ctx):
        s = Slot(self.sb(ctx, "w_more", [P, 8 * 512]), self.more_channel)
        s.free = [t for t in self.met if t]
        ring, base = self.wring, list(self.wring.slots)
        at = ring.n % len(base)
        self.wring = Ring(base[at:] + base[:at] + [s])
        ctx.callback(self.fewer_weights)

    def fewer_weights(self):
        ring = self.wring
        at = ring.n % 4
        order = ring.slots[at:] + ring.slots[:at]
        self.wring = Ring([s for s in order if s.channel is not self.more_channel])

    def load(self, slot, parts, *after):
        for out, in_ in parts:
            t = slot.channel.dma(self.sp, out, in_, slot.free, *after)
        slot.free = []
        return t

    def weights(self, src, at, n, ktiles=KD):
        s = self.wring.take()
        v = s.t[:, 0:ktiles * n].rearrange("p (k n) -> p k n", k=ktiles)
        return s, v, self.load(s, [(v, src.rearrange("(k p) n -> p k n", p=P)[:, :, at:at + n])])

    def later(self, make):
        out = []
        self.deferred.append((make, out))
        return out

    def flush(self):
        jobs, self.deferred = self.deferred, []
        for make, out in jobs:
            out.append(make())

    def fill(self, steps):
        while steps and self.side:
            try:
                next(self.side[0])
                steps -= 1
            except StopIteration:
                self.side.pop(0)

    def drain_side(self):
        while self.side:
            self.fill(1)

    def project(self, bank, out, lhs, rhs, n, *after):
        for k in range(n):
            t = self.mm(out, lhs(k), rhs(k), *((bank.free,) + after if k == 0 else ()),
                        start=(k == 0), stop=(k == n - 1), signal=(k == n - 1))
        bank.free = []
        self.flush()
        return t

    def halves(self, hi, lo, src, *after):
        k = self.a(hi, src, ACT.Copy, *after)
        return self.tt(lo, src, hi, ALU.subtract, k)

    def cut_ring(self, ctx, n):
        self.cuts = self.ring(ctx, "cut", n, [P, 2, 1024], F32R)

    def cut(self, src, *after):
        s = self.cuts.take()
        a, b = src.shape[1:]
        hi, lo = (s.t[:, j, 0:a * b].rearrange("p (a b) -> p a b", a=a) for j in range(2))
        return s, (hi, lo), self.halves(hi, lo, src, s.free, *after)

    def mm3(self, out, lhsT, rhs, *after, start, stop, signal):
        self.mm(out, lhsT[0], rhs[0], *after, start=start, stop=False, signal=False)
        self.mm(out, lhsT[0], rhs[1], start=False, stop=False, signal=False)
        return self.mm(out, lhsT[1], rhs[0], start=False, stop=stop, signal=signal)

    def project3(self, bank, out, lhs, rhs, n, *after):
        for k in range(n):
            t = self.mm3(out, lhs(k), rhs(k), *((bank.free,) + after if k == 0 else ()),
                         start=(k == 0), stop=(k == n - 1), signal=(k == n - 1))
        bank.free = []
        self.flush()
        return t

    def few_columns(self, ctx, name, lhs, m, hT, *after):
        b, rows = self.banks.take(), self.sb(ctx, name, [m, S])
        t = self.project(b, b.t[0:m, :], lhs, lambda k: hT[:, k, :], KD, *after)
        e = self.a(rows[:, :], b.t[0:m, :], ACT.Copy, t)
        b.free = [e]
        b = self.banks.take()
        for t in range(TT):
            k = self.tr(b.t[:, t * m:(t + 1) * m], rows[:, t * P:(t + 1) * P], e, b.free)
        b.free = []
        return b, k

    def norm_to_fm(self, ctx, name, x, gain, gain_ready, ready, hT, hT_free, keep=None):
        rows = self.norm_rows = self.ring(ctx, f"{name}_h", TT, [P, D])
        st = self.sb(ctx, f"{name}_st", [P, 4 * TT])
        done, scale = [], []
        for t, s in enumerate(rows.slots):
            ss, ms, rc, rs = (st[:, 4 * t + j:4 * t + j + 1] for j in range(4))
            k = self.a(s.t[:, :], x[:, t, :], ACT.Square, ready[t], accum=ss)
            k = self.ts(ms, ss, 1.0 / D, ALU.mult, k, s2=RMS_EPS, op1=ALU.add)
            k = self.recip(rc, ms, k)
            scale.append((rs, self.a(rs, rc, ACT.Sqrt, k)))

        def turn(t, s, k):
            for half in range(2):
                b = self.banks.take()
                for j in range(4):
                    f = half * 4 + j
                    m = self.tr(b.t[:, j * P:(j + 1) * P], s.t[:, f * P:(f + 1) * P], k,
                                b.free if j == 0 else None, signal=(j == 3))
                src = b.t[:, :].rearrange("p (k n) -> p k n", k=4)
                at = (slice(None), slice(half * 4, half * 4 + 4), slice(t * P, (t + 1) * P))
                e = self.halves(hT[0][at], hT[1][at], src, m, hT_free) if isinstance(hT, tuple) else \
                    self.cp(hT[at], src, m, hT_free)
                b.free = [e]
                done.append(e)

        for t, s in enumerate(rows.slots):
            rs, k = scale[t]
            k = self.stt(s.t[:, :], x[:, t, :], rs, gain, ALU.mult, ALU.mult, k, gain_ready)
            if keep:
                self.store(keep[t * P:(t + 1) * P, :], s.t[:, :], k)
            if t:
                turn(t - 1, *before)
            before = (s, k)
        turn(TT - 1, *before)
        return done

    def to_fm(self, o, o_ready, oT):
        for f in range(4):
            b = self.banks.take()
            for t in range(TT):
                m = self.tr(b.t[:, t * P:(t + 1) * P], o[:, t, f * P:(f + 1) * P], o_ready[t], b.free,
                            signal=(t == TT - 1))
            k = self.a(oT[:, f, :], b.t[:, :], ACT.Copy, m)
            b.free = [k]
        return k

    def head_norm(self, tmp, bank, got, out, gain, n=S):
        raw, sq, e = tmp.take(), tmp.take(), tmp.take()
        k0 = self.cp(raw.t[:, 0:n], bank.t[:, 0:n], got, raw.free)
        k1 = self.a(sq.t[:, 0:n], raw.t[:, 0:n], ACT.Square, k0, sq.free)
        bank.free = [k0]

        def rest():
            b = self.banks.take()
            m = self.mm(b.t[:, 0:n], self.c("ones64"), sq.t[:, 0:n], k1, b.free)
            sq.free = [m]
            k = self.a(e.t[:, 0:n], b.t[:, 0:n], ACT.Ln, m, e.free, scale=1.0 / DH, bias=self.c("eps"))
            b.free = [k]
            k = self.a(e.t[:, 0:n], e.t[:, 0:n], ACT.Exp, k, scale=-0.5)
            k = self.stt(out, raw.t[:, 0:n], gain, e.t[:, 0:n], ALU.mult, ALU.mult, k, k0)
            raw.free = e.free = [k]
            return k
        return self.later(rest)

    def bias_table(self, ctx, name, big, relb_tile):
        row = self.sb(ctx, f"{name}_row", [NH, 640])
        for lo, hi in ((0, 512), (512, 640)):
            b = self.banks.take()
            m = self.mm(b.t[0:NH, 0:hi - lo], relb_tile[:, :], self.dist[:, 1024 + lo:1024 + hi],
                        b.free, self.relb_ready, self.dist_ready)
            k = self.cp(row[:, lo:hi], b.t[0:NH, 0:hi - lo], m)
            b.free = [k]
        dram = self.nc.dram_tensor(f"{name}_dram", (NH, 640), F32, kind="Internal").ap()
        k = self.store(dram, row[:, :], k, lane=self.pool)
        skew = bass.AP(tensor=dram.tensor, offset=0, ap=[[1, P], [640, NH], [1, 512]])
        return self.channel(f"{name}_skew").dma(self.pool, big[:, :, :], skew, k)

    def attention(self, ctx, name, branches, big):
        sc, pr, pt = (self.ring(ctx, f"{name}_{x}", n, [P, S]) for x, n in (("s", 3), ("p", 4), ("t", 3)))
        st = self.sb(ctx, f"{name}_stat", [P, len(branches), TT, 2, NH])
        ring_s, ring_t, ring_o = (Ring([self.banks.slots[j] for j in js]) for js in ((0, 1, 2), (3, 4, 5), (6, 7)))
        units = [(b, i, h) for b in range(len(branches)) for pair in ((3, 0), (2, 1)) for h in range(NH) for i in pair]
        probs, turned, outs, sums = {}, {}, {}, {}

        def score(br, i, h):
            q, kk, v, ready, finish, extra = branches[br]
            n = (i + 1) * P
            b, s, p = ring_s.take(), sc.take(), pr.take()
            got = self.mm(b.t[:, 0:n], q(h)[:, i * P:(i + 1) * P], kk(h)[:, 0:n], b.free, ready,
                          start=True, stop=not extra or i == 0)
            if extra and i:
                got = extra(i, b.t[:, 0:n])
            low = st[:, br, i, 0, h:h + 1]
            k = self.dve.do(lambda e: e.tensor_tensor_reduce(
                out=s.t[:, 0:n], in0=b.t[:, 0:n], in1=reversed_(big[:, h, 0:n]), scale=-1.0, scalar=3e38,
                op0=ALU.add, op1=ALU.min, accum_out=low), got, s.free)
            b.free = [k]
            k = self.a(p.t[:, 0:n], s.t[:, 0:n], ACT.Exp, k, p.free, scale=-1.0, bias=low,
                       accum=st[:, br, i, 1, h:h + 1])
            s.free = [k]
            sums[br, i] = k
            probs[br, i, h] = (p, k)

        def turn(br, i, h):
            n = (i + 1) * P
            p, k = probs.pop((br, i, h))
            b, w = ring_t.take(), pt.take()
            for j in range(i + 1):
                m = self.tr(b.t[:, j * P:(j + 1) * P], p.t[:, j * P:(j + 1) * P], k, b.free, signal=(j == i))
            p.free = [m]
            if h % 2:
                k = self.a(w.t[:, 0:n], b.t[:, 0:n], ACT.Copy, m, w.free)
            else:
                k = self.cp(w.t[:, 0:n], b.t[:, 0:n], m, w.free)
            b.free = [k]
            turned[br, i, h] = (w, k)

        def combine(br, i, h):
            v, finish = branches[br][2], branches[br][4]
            w, k = turned.pop((br, i, h))
            if h == 0:
                outs[br, i] = ring_o.take()
            b = outs[br, i]
            for j in range(i + 1):
                m = self.mm(b.t[:, h * DH:(h + 1) * DH], w.t[:, j * P:(j + 1) * P], v(h, j), k, b.free,
                            start=(j == 0), stop=(j == i), signal=(j == i))
            b.free = []
            w.free = [m]
            if h == NH - 1:
                b.free = [finish(i, b, m, st[:, br, i, 1, :], sums[br, i])]

        for n in range(len(units) + 4):
            if n < len(units):
                score(*units[n])
            if 0 <= n - 3 < len(units):
                turn(*units[n - 3])
            if 0 <= n - 4 < len(units):
                combine(*units[n - 4])


def finish(steps):
    while True:
        try:
            next(steps)
        except StopIteration as end:
            return end.value


def spread(ap, m, axis=2):
    shape = list(ap.shape)
    return ap.unsqueeze(axis).broadcast_to(shape[:axis] + [m] + shape[axis:])


def reversed_(ap):
    (pstep, p), (step, n) = ap.ap
    return bass.AP(tensor=ap.tensor, offset=ap.offset + step * (n - 1), ap=[[pstep, p], [-step, n]])


def nsa(K, outer, hT, ready, oT, spare):
    w, c = K.w, K.c
    w_in = w["w_in"]
    sm = K.channel("nsa_small")
    ctx = ExitStack()
    qT = K.sb(outer, "qT", [P, NR, S])
    ksT, kwT = K.sb(outer, "ksT", [P, S]), K.sb(outer, "kwT", [P, S])
    vs, vw = K.sb(outer, "vs", [P, TT, KVW]), K.sb(outer, "vw", [P, TT, KVW])
    x2 = oT[:, :, :].rearrange("p (j g) t -> p j g t", j=2)
    gate = K.sb(outer, "nsa_gate", [P, TT, 3 * NH])
    big = K.sb(outer, "nsa_bias", [P, NH, 512])
    relb = K.sb(outer, "nsa_relb", [33, NH])
    raw = K.sb(ctx, "cmp_raw", [P, 2, S])
    o = spare
    tmp = K.ring(ctx, "nsa_tmp", 6, [P, S])
    gains = K.sb(ctx, "nsa_gains", [P, 2])
    pe_in = K.sb(ctx, "pe_in", [16, 2, P])
    peT = K.sb(ctx, "peT", [P, 2, 16])
    w2k, w2v = K.sb(ctx, "w2k", [P, 2, 2, DH]), K.sb(ctx, "w2v", [P, 2, DH])

    for half in range(2):
        for j, name in enumerate(("q_norm_g", "k_norm_g")):
            small = sm.dma(K.act, gains[half * DH:(half + 1) * DH, j:j + 1], w[name].rearrange("o d -> d o"), slow=True)
        small = sm.dma(K.act, w2k[:, :, half, :], w["cmp_w2_k"].rearrange("(k p) d -> p k d", p=P))
    small = sm.dma(K.act, w2v[:, :, :], w["cmp_w2_v"].rearrange("(k p) d -> p k d", p=P))
    for j, name in enumerate(("cmp_pe_k", "cmp_pe_v")):
        small = sm.dma(K.act, pe_in[:, j, :], w[name].rearrange("(m two) d -> m (two d)", two=2))
    K.load_distances(ctx, w["rel_bias"], relb)
    K.ts(gains[:, 0:1], gains[:, 0:1], DH ** -0.5, ALU.mult, small)

    s, v, got = K.weights(w_in, COL_KC, 512)
    raw_ready = []
    for j in range(2):
        b = K.banks.take()
        m = K.project(b, b.t[:, :], lambda k: v[:, k, j * P:(j + 1) * P], lambda k: hT[:, k, :], KD, got, ready)
        e = K.a(raw[:, j, :], b.t[:, :], ACT.Copy, m)
        b.free = [e]
        raw_ready.append(e)
    b = K.banks.take()
    m = K.project(b, b.t[:, :], lambda k: v[:, k, 2 * P:3 * P], lambda k: hT[:, k, :], KD, got)
    ks_ready = K.head_norm(tmp, b, m, ksT[:, :], gains[:, 1:2])

    def values(dst, v, at):
        b = K.banks.take()
        for t in range(TT):
            m = K.project(b, b.t[:, t * P:(t + 1) * P], lambda k: hT[:, k, t * P:(t + 1) * P],
                          lambda k: v[:, k, at:at + P], KD)
        e = K.a(dst[:, :, :], b.t[:, :].rearrange("p (t n) -> p t n", t=TT), ACT.Copy, m)
        b.free = [e]
        return m, e

    m, vs_ready = values(vs, v, 3 * P)
    s.free = [m]

    sh = K.channel("cmp_shift")
    for j in range(2):
        for g in range(NG):
            src = raw[g * DH:(g + 1) * DH, j, :]
            shifted = sh.dma(K.sp, x2[0:DH, j, g, :], src, raw_ready[j])
            shifted = sh.dma(K.sp, x2[DH:P, j, g, 0:S - 1], src[:, 1:S])

    s, v, got = K.weights(w_in, COL_KW, 2 * KVW + 3 * NH)
    b = K.banks.take()
    m = K.project(b, b.t[:, :], lambda k: v[:, k, 0:P], lambda k: hT[:, k, :], KD, got)
    kw_ready = K.head_norm(tmp, b, m, kwT[:, :], gains[:, 1:2])
    m, vw_ready = values(vw, v, P)
    b, m = K.few_columns(ctx, "gate_rows", lambda k: v[:, k, 2 * P:2 * P + 24], 24, hT)
    s.free = [m]
    gate_ready = K.a(gate[:, :, :], b.t[:, 0:96].rearrange("p (t n) -> p t n", t=TT), ACT.Sigmoid, m)
    b.free = [gate_ready]

    big_ready = K.bias_table(ctx, "nsa", big, relb)

    NB = NG * NC
    win = K.sb(ctx, "cmp_win", [P, 2, NG, NC, CB // 2])
    hid = K.sb(ctx, "cmp_hid", [NB, 4, 512])
    actT = K.sb(ctx, "cmp_actT", [P, 4, NB])
    b = K.banks.take()
    for j in range(2):
        m = K.tr(b.t[:, j * 16:(j + 1) * 16], pe_in[:, j, :], small, b.free, K.consts_ready)
    pe_ready = K.cp(peT[:, :, :], b.t[:, 0:32].rearrange("p (j m) -> p j m", j=2), m)
    b.free = [pe_ready]
    b = K.banks.take()
    for j, name in enumerate(("cmp_w1_k", "cmp_w1_v")):
        for g in range(NG):
            row = x2[:, j, g, :]
            (pstep, p_), _ = row.ap
            windows = bass.AP(tensor=row.tensor, offset=row.offset, ap=[[pstep, p_], [CS, NC], [2, CB // 2]])
            win_ready = K.tt(win[:, j, g, :, :], windows, spread(peT[:, j, :], NC, 1), ALU.add, pe_ready, shifted)
        s = K.wring.take()
        v1 = s.t[:, :].rearrange("p (m n) -> p m n", m=16)
        got = K.load(s, [(v1, w[name].rearrange("(m p) n -> p m n", p=P))])
        wj = win[:, j, :, :, :].rearrange("p g n m -> p (g n) m")
        for k in range(CB // 2):
            m = K.mm(b.t[0:NB, j * 256:(j + 1) * 256], wj[:, :, k], v1[:, k, :], b.free, got, win_ready,
                     start=(k == 0), stop=(k == CB // 2 - 1), signal=(k == CB // 2 - 1))
        s.free = [m]
    K.flush()
    x, x3, inner, act = (hid[:, i, :] for i in range(4))
    k = K.cp(x, b.t[0:NB, :], m)
    b.free = [k]
    k = K.tt(x3, x, x, ALU.mult, k)
    k = K.tt(x3, x3, x, ALU.mult, k)
    k = K.stt(inner, x3, 0.044715, x, ALU.mult, ALU.add, k)
    k = K.a(x3, inner, ACT.Tanh, k, scale=math.sqrt(2 / math.pi))
    k = K.stt(act, x3, 1.0, x, ALU.add, ALU.mult, k)
    hid_ready = K.ts(act, act, 0.5, ALU.mult, k)

    s = K.wring.take()
    v = s.t[:, :].rearrange("p (k r g d) -> p k r g d", k=KD, r=NR, g=NG)
    src = w_in.rearrange("(k p) n -> p k n", p=P)
    got = K.load(s, [(v[:, :, r, g, :], src[:, :, COL_Q + (g * NR + r) * DH:COL_Q + (g * NR + r + 1) * DH])
                     for r in range(NR) for g in range(NG)])
    q_ready = []
    for r in range(NR):
        b = K.banks.take()
        m = K.project(b, b.t[:, :], lambda k: v[:, k, r, :, :].rearrange("p g d -> p (g d)"),
                      lambda k: hT[:, k, :], KD, got, ready)
        q_ready.append(K.head_norm(tmp, b, m, qT[:, r, :], gains[:, 0:1]))
    s.free = [m]

    b = K.banks.take()
    for u in range(4):
        m = K.tr(b.t[:, u * NB:(u + 1) * NB], act[:, u * P:(u + 1) * P], hid_ready, b.free)
    act = actT
    act_ready = K.cp(act[:, :, :], b.t[:, 0:4 * NB].rearrange("p (u n) -> p u n", u=4), m)
    b.free = [act_ready]
    kcT = K.sb(ctx, "kcT", [P, NB])
    vc = K.sb(ctx, "vc", [P, NG, DH])
    b = K.banks.take()
    m = K.project(b, b.t[:, 0:NB], lambda k: w2k[:, k, :, :], lambda k: act[:, k, :], 2, act_ready)
    kc_ready = K.head_norm(tmp, b, m, kcT[:, :], gains[:, 1:2], n=NB)
    z = K.zero(vc[:, :, :])
    b = K.banks.take()
    for r in range(NR):
        for g in range(NG):
            m = K.project(b, b.t[32 * r:32 * r + NC, g * DH:(g + 1) * DH], lambda k: act[:, 2 + k, g * NC:(g + 1) * NC],
                          lambda k: w2v[:, k, :], 2)
    for r in range(NR):
        vc_ready = K.cp(vc[32 * r:32 * r + NC, :, :],
                        b.t[32 * r:32 * r + NC, 0:P].rearrange("p (g d) -> p g d", g=NG), m, z)
    b.free = [vc_ready]

    bias_c = K.sb(ctx, "bias_c", [P, TT, NH, 32])
    z = K.zero(bias_c[:, :, :, :], value=NEG)
    for i in range(TT):
        at = P * i + P - CB
        n = min(NC, at // CS + 1)
        (pstep, p_), (hstep, h_), _ = big[:, :, :].ap
        first = big[:, :, at:at + 1]
        src = bass.AP(tensor=first.tensor, offset=first.offset, ap=[[pstep, p_], [hstep, h_], [-CS, n]])
        bias_ready = K.cp(bias_c[:, i, :, 0:n], src, z, big_ready)

    pc = K.ring(ctx, "cmp_p", TT, [P, NH, 32])
    pcT = K.ring(ctx, "cmp_pT", TT, [P, 2, P])
    st = K.sb(ctx, "cmp_stat", [P, TT, 3, NH])
    coef = K.sb(ctx, "cmp_coef", [P, TT, NH])
    o_ready, soft, turned = {}, {}, {}
    for i in range(TT):
        s = pc.take()
        z = K.cp(s.t[:, :, NC:32], bias_c[:, i, :, NC:32], s.free, bias_ready)
        for g in range(NG):
            b = K.banks.take()
            half = slice(g * DH, (g + 1) * DH)
            for r in range(NR):
                m = K.mm(b.t[:, r * 32:r * 32 + NC], qT[half, r, i * P:(i + 1) * P],
                         kcT[half, g * NC:(g + 1) * NC], b.free, q_ready, kc_ready, signal=(r == NR - 1))
            v3 = b.t[:, 0:P].rearrange("p (h n) -> p h n", h=NR)[:, :, 0:NC]
            hs = slice(g * NR, (g + 1) * NR)
            k = K.tt(s.t[:, hs, 0:NC], v3, bias_c[:, i, hs, 0:NC], ALU.add, m, s.free, bias_ready)
            b.free = [k]
        mx, sm_, rc = (st[:, i, j, :] for j in range(3))
        k = K.red(mx, s.t[:, :, :], ALU.max, k, z)
        k = K.tt(s.t[:, :, :], s.t[:, :, :], spread(mx, 32), ALU.subtract, k)
        k = K.a(s.t[:, :, :], s.t[:, :, :], ACT.Exp, k)
        p_ready = k
        k = K.red(sm_, s.t[:, :, :], ALU.add, k)
        k = K.ts(sm_, sm_, 1e-30, ALU.max, k)
        k = K.recip(rc, sm_, k)
        k = K.stt(coef[:, i, :], rc, c("valid_c")[:, i:i + 1], gate[:, i, 0:3 * NH:3], ALU.mult, ALU.mult, k, gate_ready)
        soft[i] = (s, p_ready, k)
    for i in range(TT):
        s, p_ready, k = soft[i]
        t2 = pcT.take()
        b = K.banks.take()
        for g in range(NG):
            m = K.tr(b.t[:, g * P:(g + 1) * P], s.t[:, g * NR:(g + 1) * NR, :].rearrange("p h n -> p (h n)"),
                     p_ready, b.free)
        e = K.cp(t2.t[:, :, :], b.t[:, 0:2 * P].rearrange("p (g n) -> p g n", g=2), m, t2.free)
        s.free, b.free = [m, k], [e]
        turned[i] = (t2, e, k)
    for i in range(TT):
        t2, e, coef_ready = turned[i]
        for r in range(NR):
            b = K.banks.take()
            rows = slice(32 * r, 32 * r + NC)
            for g in range(NG):
                m = K.mm(b.t[:, g * DH:(g + 1) * DH], t2.t[rows, g, :], vc[rows, g, :], e, b.free, vc_ready)
            k = K.tt(o[:, i, :].rearrange("p (g r d) -> p g r d", g=NG, r=NR)[:, :, r, :],
                     b.t[:, 0:P].rearrange("p (g d) -> p g d", g=NG),
                     spread(coef[:, i, r:NH:NR], DH), ALU.mult, m, coef_ready)
            b.free = [k]
        t2.free = [m]
        o_ready[i] = k

    K.meet()
    ctx.close()
    scratch = K.ring(outer, "att_o", 2, [P, NW])
    branches = []
    for j, (kT, vv, k_ready, v_ready) in enumerate(((ksT, vs, ks_ready, vs_ready), (kwT, vw, kw_ready, vw_ready))):
        cf = K.sb(outer, f"coef{j}", [P, TT, 2, NH])

        def finish(i, b, got, sums, sums_ready, j=j, cf=cf):
            k = K.recip(cf[:, i, 0, :], sums, sums_ready)
            k = K.tt(cf[:, i, 1, :], cf[:, i, 0, :], gate[:, i, 1 + j:3 * NH:3], ALU.mult, k, gate_ready)
            s = scratch.take()
            e = K.tt(s.t[:, :].rearrange("p (h d) -> p h d", h=NH), b.t[:, :].rearrange("p (h d) -> p h d", h=NH),
                     spread(cf[:, i, 1, :], DH), ALU.mult, k, got, s.free)
            k = K.tt(o[:, i, :], o[:, i, :], s.t[:, :], ALU.add, e, o_ready[i])
            s.free = [k]
            o_ready[i] = k
            return e

        branches.append((lambda h: qT[(h // NR) * DH:(h // NR + 1) * DH, h % NR, :],
                         lambda h, kT=kT: kT[(h // NR) * DH:(h // NR + 1) * DH, :],
                         lambda h, j2, vv=vv: vv[:, j2, (h // NR) * DH:(h // NR + 1) * DH],
                         [q_ready, k_ready, v_ready, big_ready], finish, None))
    K.attention(outer, "nsa", branches, big)
    return K.to_fm(o, o_ready, oT)


def mix(K, p1, d, mu, out, ready, out_free):
    k = K.tt(d, p1[:, 0:S], p1[:, 1:S + 1], ALU.subtract, ready)
    return K.stt(out, d, mu, p1[:, 1:S + 1], ALU.mult, ALU.add, k, out_free)


def rwkv(K, ctx, hT, ready, oT):
    w, c = K.w, K.c
    w_in = w["w_in"]
    sm = K.channel("rwkv_small")
    mu = K.sb(ctx, "mu", [P, 14])
    vec = K.sb(ctx, "rwkv_vec", [P, 8, 4])
    w2a2, g2 = K.sb(ctx, "w2a2", [P, RW]), K.sb(ctx, "g2", [P, RW])
    rows = K.sb(ctx, "rwkv_rows", [46, P])
    small = sm.dma(K.act, rows[0:14, :], w["rwkv_mu"].rearrange("o (k p) -> (o k) p", p=P))
    names = ("rwkv_w0", "rwkv_a0", "rwkv_k_k", "rwkv_k_a", "rwkv_r_k", "rwkv_ln_g", "rwkv_ln_b")
    for j, name in enumerate(names):
        src = w[name].rearrange("(k two) d -> k (two d)", two=2) if name == "rwkv_r_k" else \
            w[name].rearrange("o (k p) -> (o k) p", p=P)
        small = sm.dma(K.act, rows[14 + 4 * j:18 + 4 * j, :], src)
    small = sm.dma(K.act, w2a2[0:64, :], w["rwkv_w2"])
    small = sm.dma(K.act, w2a2[64:P, :], w["rwkv_a2"])
    small = sm.dma(K.act, g2[:, :], w["rwkv_g2"])
    p1 = K.ring(ctx, "p1", 3, [P, S + 1])
    for s in p1.slots:
        s.free = [K.zero(s.t[:, 0:1])]
    tmp = K.ring(ctx, "rw_tmp", 3, [P, S])
    lor, xg = K.sb(ctx, "lor", [P, S]), K.sb(ctx, "xg", [P, S])
    thw = K.sb(ctx, "thw", [DH, S])

    all_banks = K.banks
    K.banks, side_banks = Ring(all_banks.slots[0:6]), Ring(all_banks.slots[6:8])

    def mixed(v, at, got, muc, out, out_free=None):
        b, s, d = side_banks.take(), p1.take(), tmp.take()
        for k in range(KD):
            m = K.mm(b.t[:, :], v[:, k, at:at + P], hT[:, k, :], b.free, got, ready,
                     start=(k == 0), stop=(k == KD - 1), signal=(k == KD - 1))
            if k % 2:
                yield
        e = K.a(s.t[:, 1:S + 1], b.t[:, :], ACT.Copy, m, s.free)
        b.free = [e]
        k = mix(K, s.t, d.t[:, :], mu[:, muc:muc + 1], out, [e, d.free, vec_ready], out_free)
        s.free = d.free = [k]
        return m, k

    s, v, got = K.weights(w_in, COL_LORA, 256)
    first = mixed(v, 0, got, 12, lor[:, :])
    for _ in range(KD // 2):
        next(first)
    b = K.banks.take()
    m = K.tr(b.t[:, 0:42], rows[0:42, :], small, b.free, K.consts_ready)
    k = K.cp(mu[:, :], b.t[:, 0:14], m)
    vec_ready = K.cp(vec[:, 0:7, :], b.t[:, 14:42].rearrange("p (j k) -> p j k", j=7), m)
    b.free = [vec_ready]
    w0, a0, kkg, kag, rkg, lng, lnb = (vec[:, j, :] for j in range(7))

    m, lor_ready = finish(first)
    m, k = finish(mixed(v, P, got, 13, xg[:, :]))
    s.free = [m]
    thw_ready = K.a(thw[:, :], lor[0:DH, :], ACT.Tanh, lor_ready)
    sg_ready = K.a(xg[:, :], xg[:, :], ACT.Sigmoid, k)

    names = ("rT", "kT", "vT", "lw", "aT")
    buf = {n: K.sb(ctx, f"rw_{n}", [P, S]) for n in names}
    rT, kT, vT, lw, aT = (buf[n][:, :] for n in names)
    kk, kp = lw, kT
    L, E1, E2 = (K.sb(ctx, f"rw_{n}", [P, TT, P + 1]) for n in ("L", "E1", "E2"))
    kt, bt = K.sb(ctx, "rw_kt", [P, TT, P]), K.sb(ctx, "rw_bt", [P, TT, P])
    kept = [dict([("ra", K.sb(ctx, "rw_ra", [P, TT, 2, P])), ("zs", K.sb(ctx, "rw_zs", [P, TT]))]
                 + [(n, K.sb(ctx, f"rw_{n}", [P, TT, P])) for n in ("Kt", "Bt", "Vt")]
                 + [(n, K.sb(ctx, f"rw_{n}", [P, S])) for n in ("gT", "bv", "y")]) for _ in range(2)]
    AM = K.sb(ctx, "rw_AM", [P, 8, 4, P])
    ready0 = [K.zero(AM[:, :, :, :]), K.zero(L[:, :, 0:1])]
    Alow = [K.sb(ctx, f"rw_low{g}", [P, 4, P]) for g in range(2)]
    ready0 += [K.zero(x[:, :, :]) for x in Alow]
    lent = K.wring.take()
    parts = [lent.t[:, q * S:(q + 1) * S].rearrange("p (x t) -> p x t", x=4) for q in range(8)]
    all_slots = K.wring
    K.wring = Ring([s for s in all_slots.slots if s is not lent])
    level = Ring([Slot(parts[0]), Slot(parts[1])])
    WU = [parts[2:5], parts[5:8]]
    Z = K.sb(ctx, "rw_Z", [P, P])
    step = K.ring(ctx, "rw_step", 4, [P, P])
    yst = K.sb(ctx, "rw_yst", [P, 4, 4, 8])
    ones = K.sb(ctx, "rw_ones", [P, P])
    ones_ready = K.zero(ones[:, :], value=1.0)
    def load_pair(f):
        s = K.wring.take()
        v = s.t[:, 0:8 * 384].rearrange("p (k n) -> p k n", k=KD)
        got = K.load(s, [(v[:, :, j * P:(j + 1) * P], w_in.rearrange("(k p) n -> p k n", p=P)[:, :, at + f * P:at + (f + 1) * P])
                         for j, at in enumerate((COL_R, COL_K, COL_V))])
        tokens[f]["weights"] = (s, v, got)

    def project(f, free):
        s, v, got = tokens[f]["weights"]
        m, r_ready = yield from mixed(v, 0, got, f, rT, free)
        m, k_ready = yield from mixed(v, P, got, 4 + f, kT, free)
        m, v_ready = yield from mixed(v, 2 * P, got, 8 + f, vT, free)
        s.free = [m]
        tokens[f].update(rkv=(r_ready, k_ready, v_ready))

    def prepare(f):
        now = kept[f % 2]
        ra, zs, Kt, Bt, Vt = (now[n] for n in ("ra", "zs", "Kt", "Bt", "Vt"))
        gT, bv = now["gT"][:, :], now["bv"][:, :]
        cols = slice(f * P, (f + 1) * P)
        free = [lane.last() for lane in (K.pe, K.act, K.dve)]
        banks = side_banks if f else K.banks
        b = banks.take()
        m = K.mm(b.t[:, :], w2a2[0:DH, cols], thw[:, :], b.free, thw_ready)
        k = K.a(lw, b.t[:, :], ACT.Sigmoid, m, free, bias=w0[:, f:f + 1])
        b.free = [k]
        k = K.ts(lw, lw, -DECAY, ALU.mult, k)
        lw_ready = k
        yield
        b = banks.take()
        m = K.mm(b.t[:, :], w2a2[DH:P, cols], lor[DH:P, :], b.free, lor_ready)
        a_ready = K.a(aT, b.t[:, :], ACT.Sigmoid, m, free, bias=a0[:, f:f + 1])
        b.free = [a_ready]
        yield
        b = banks.take()
        m = K.mm(b.t[:, :], g2[:, cols], xg[:, :], b.free, sg_ready)
        g_ready = K.a(gT, b.t[:, :], ACT.Copy, m, free)
        b.free = [g_ready]
        yield
        for n in range(TT):
            k = K.dve.do(lambda e, n=n: e.tensor_tensor_scan(
                L[:, n, 1:P + 1], ones[:, :], buf["lw"][:, n * P:(n + 1) * P], 0.0, ALU.mult, ALU.add),
                lw_ready, ones_ready, ready0, free)
        scanned = k
        k = K.tt(E1[:, :, :], L[:, :, :], L[:, :, 64:65].broadcast_to([P, TT, P + 1]), ALU.subtract, k)
        e2 = K.a(E2[:, :, :], E1[:, :, :], ACT.Exp, k, scale=-1.0)
        e1 = K.a(E1[:, :, :], E1[:, :, :], ACT.Exp, e2)
        yield
        r_ready, k_ready, v_ready = tokens[f]["rkv"]
        k0 = K.ts(kk, kT, kkg[:, f:f + 1], ALU.mult, k_ready, vec_ready, scanned)
        t1, t2 = tmp.take(), tmp.take()
        k = K.a(t1.t[:, :], kk, ACT.Square, k0, t1.free)
        yield
        b = banks.take()
        m = K.mm(b.t[:, :], c("ones64"), t1.t[:, :], k, b.free)
        k = K.ts(t2.t[:, :], b.t[:, :], NORM_FLOOR, ALU.max, m, t2.free)
        b.free, t1.free = [k], [m]
        yield
        k = K.a(t2.t[:, :], t2.t[:, :], ACT.Ln, k, scale=2.0 ** LN_SHIFT)
        k = K.a(t2.t[:, :], t2.t[:, :], ACT.Exp, k, scale=-0.5, bias=c("ln_back"))
        kk_ready = K.tt(kk, kk, t2.t[:, :], ALU.mult, k)
        t2.free = [kk_ready]
        yield
        t1 = tmp.take()
        k = K.ts(t1.t[:, :], aT, -1.0, ALU.add, a_ready, t1.free, s2=kag[:, f:f + 1], op1=ALU.mult)
        kp_ready = K.stt(kp, t1.t[:, :], 1.0, kT, ALU.add, ALU.mult, k, k0)
        t1.free = [kp_ready]
        yield
        v4 = lambda x: x.rearrange("p (n t) -> p n t", n=TT)
        k = K.stt(ra[:, :, 0, :], v4(kk), -1.0, E1[:, :, 0:P], ALU.mult, ALU.mult, kk_ready, e1)
        ra_ready = K.tt(ra[:, :, 1, :], v4(rT), E1[:, :, 1:P + 1], ALU.mult, e1, r_ready)
        kt_ready = K.tt(kt[:, :, :], v4(kp), E2[:, :, 1:P + 1], ALU.mult, kp_ready, e2)
        t1 = tmp.take()
        k = K.tt(t1.t[:, :], kk, aT, ALU.mult, kk_ready, a_ready, t1.free)
        bt_ready = K.tt(bt[:, :, :], v4(t1.t[:, :]), E2[:, :, 1:P + 1], ALU.mult, k)
        t1.free = [bt_ready]
        yield
        t1 = tmp.take()
        k = K.stt(t1.t[:, :], rT, rkg[:, f:f + 1], kp, ALU.mult, ALU.mult, kp_ready, r_ready, t1.free)
        yield
        b = banks.take()
        m = K.mm(b.t[:, :], c("ones64"), t1.t[:, :], k, b.free)
        t1.free = [m]
        bv_ready = K.tt(bv, b.t[:, :], vT, ALU.mult, m, v_ready)
        b.free = [bv_ready]
        yield
        zs_ready = K.tt(zs[:, 0:TT - 1], E1[:, 0:TT - 1, P:P + 1].rearrange("p n o -> p (n o)"),
                        E2[:, 1:TT, 0:1].rearrange("p n o -> p (n o)"), ALU.mult, e1, e2, bv_ready)
        tm_ready = []
        for dst, src, r0 in ((Kt, kt[:, :, :], kt_ready), (Bt, bt[:, :, :], bt_ready), (Vt, v4(vT), v_ready)):
            b = banks.take()
            for n in range(TT):
                m = K.tr(b.t[:, n * P:(n + 1) * P], src[:, n, :], r0, b.free, signal=(n == TT - 1))
            k = K.a(dst[:, :, :], b.t[:, :].rearrange("p (n t) -> p n t", n=TT), ACT.Copy, m, free)
            b.free = [k]
            tm_ready.append(k)
            yield
        places_free.append([lane.last() for lane in (K.pe, K.act, K.dve)])
        tokens[f].update(ra=ra_ready, kt=kt_ready, bt=bt_ready, tm=tm_ready, zs=zs_ready, bv=bv_ready, g=g_ready)

    def norm(f, y_ready, done):
        now = kept[f % 2]
        y = now["y"][:, :].rearrange("p (h d) -> p h d", h=8)
        gT, bv, g_ready, bv_ready = now["gT"][:, :], now["bv"][:, :], done["g"], done["bv"]
        t1 = tmp.take()
        sq = t1.t[:, :].rearrange("p (h d) -> p h d", h=8)
        s1, s2, s3, s4 = (yst[:, f, j, :] for j in range(4))
        k = K.red(s1, y[:, :, :], ALU.add, y_ready)
        k = K.ts(s2, s1, 1.0 / DH, ALU.mult, k)
        k = K.tt(y[:, :, :], y[:, :, :], spread(s2, DH), ALU.subtract, k)
        k1 = K.a(sq, y[:, :, :], ACT.Square, k, t1.free)
        k = K.red(s3, sq, ALU.add, k1)
        t1.free = [k]
        k = K.ts(s3, s3, 1.0 / DH, ALU.mult, k, s2=GN_EPS, op1=ALU.add)
        k = K.recip(s4, s3, k)
        k = K.a(s4, s4, ACT.Sqrt, k)
        k = K.tt(y[:, :, :], y[:, :, :], spread(s4, DH), ALU.mult, k)
        yield
        b = side_banks.take()
        for n in range(TT):
            m = K.tr(b.t[:, n * P:(n + 1) * P], y[:, 2 * n:2 * n + 2, :].rearrange("p h d -> p (h d)"), k, b.free,
                     signal=(n == TT - 1))
        t1 = tmp.take()
        k = K.ts(t1.t[:, :], b.t[:, :], lng[:, f:f + 1], ALU.mult, m, t1.free, s2=lnb[:, f:f + 1], op1=ALU.add)
        b.free = [k]
        k = K.tt(t1.t[:, :], t1.t[:, :], bv, ALU.add, k, bv_ready)
        k = K.tt(oT[:, f, :], t1.t[:, :], gT, ALU.mult, k, g_ready)
        t1.free = [k]
        outs.append(k)

    outs, tokens, places_free = [], [{} for _ in range(4)], []
    load_pair(0)
    load_pair(1)
    early = prepare(0)
    for step_no, _ in enumerate(project(0, None)):
        if step_no in (2, 4, 6, 8):
            next(early)
    finish(early)
    finish(project(1, places_free[0]))
    for f in range(4):
        now, own = kept[f % 2], tokens[f]
        ra, zs, Kt, Bt, Vt = (now[n] for n in ("ra", "zs", "Kt", "Bt", "Vt"))
        y = now["y"][:, :].rearrange("p (h d) -> p h d", h=8)
        ra_ready, kt_ready, bt_ready, tm_ready, zs_ready = (own[n] for n in ("ra", "kt", "bt", "tm", "zs"))
        free = [lane.last() for lane in (K.pe, K.act, K.dve, K.pool)]
        if f < 2:
            load_pair(f + 2)
        am_ready = {}
        for u in range(8):
            hh, n = divmod(u, TT)
            hp = slice(hh * DH, (hh + 1) * DH)
            b = K.banks.take()
            K.mm(b.t[:, 0:256].rearrange("p (x t) -> p x t", x=2), kt[hp, n, :], ra[hp, n, :, :], b.free, kt_ready, ra_ready, signal=False)
            m = K.mm(b.t[:, 256:512].rearrange("p (x t) -> p x t", x=2), bt[hp, n, :], ra[hp, n, :, :], bt_ready)
            k = K.dve.do(lambda e, u=u, b=b: e.copy_predicated(
                AM[:, u, :, :], c("mask_rw").bitcast(I32).rearrange("p (x t) -> p x t", x=4),
                b.t[:, :].rearrange("p (x t) -> p x t", x=4)), m, ready0, free)
            b.free = [k]
            am_ready[u] = k
        inv_ready = []
        state = []
        for g in range(2):
            b = K.banks.take()
            for i in range(4):
                n, hh = i, g
                hp = slice(hh * DH, (hh + 1) * DH)
                m = K.mm(b.t[:, i * P:(i + 1) * P], ra[hp, n, 0, :], bt[hp, n, :], b.free, ra_ready, bt_ready,
                         signal=(i == 3))
            A = Alow[g]
            a_low = K.dve.do(lambda e, A=A, b=b: e.copy_predicated(
                A[:, :, :], spread(c("mask_low").bitcast(I32), 4, 1),
                b.t[:, :].rearrange("p (x t) -> p x t", x=4)), m, ready0, free)
            b.free = [a_low]
            W, U, Y = WU[g]
            eye = spread(c("ident"), 4, 1)
            k = K.tt(W[:, :, :], AM[:, 4 * g:4 * g + 4, 2, :], spread(c("lev0u"), 4, 1), ALU.mult, am_ready[4 * g + 3], free)
            w_r = K.tt(W[:, :, :], W[:, :, :], eye, ALU.add, k)
            k = K.tt(U[:, :, :], A[:, :, :], spread(c("lev0"), 4, 1), ALU.mult, a_low, free)
            u_r = K.tt(U[:, :, :], U[:, :, :], eye, ALU.add, k)
            state.append((A, W, U, Y, a_low, w_r, u_r))
        if f:
            K.side.append(norm(f - 1, y_done, tokens[f - 1]))
        if f < 3:
            K.side.append(prepare(f + 1))
        for lv in range(1, 7):
            for g in range(2):
                A, W, U, Y, a_low, w_r, u_r = state[g]
                s = level.take()
                am = K.tt(s.t[:, :, :], A[:, :, :], spread(c(f"lev{lv}"), 4, 1), ALU.mult, a_low, s.free, lane=K.pool)
                b = K.banks.take()
                for i in range(4):
                    m = K.mm(b.t[:, i * P:(i + 1) * P], s.t[:, i, :], W[:, i, :], am, w_r, b.free, signal=(i == 3))
                s.free = [m]
                y_r = K.a(Y[:, :, :], b.t[:, :].rearrange("p (x t) -> p x t", x=4), ACT.Copy, m, free)
                b.free = [y_r]
                K.fill(1)
                b1 = K.banks.take()
                for i in range(4):
                    m1 = K.mm(b1.t[:, i * P:(i + 1) * P], U[:, i, :], Y[:, i, :], y_r, u_r, b1.free, signal=(i == 3))
                m2 = None
                if lv < 6:
                    b2 = K.banks.take()
                    for i in range(4):
                        m2 = K.mm(b2.t[:, i * P:(i + 1) * P], Y[:, i, :], U[:, i, :], b2.free, signal=(i == 3))
                w_r = K.tt(W[:, :, :], W[:, :, :], b1.t[:, :].rearrange("p (x t) -> p x t", x=4), ALU.add, m1)
                b1.free = [w_r]
                if lv < 6:
                    u_r = K.tt(U[:, :, :], U[:, :, :], b2.t[:, :].rearrange("p (x t) -> p x t", x=4), ALU.add, m2)
                    b2.free = [u_r]
                state[g] = (A, W, U, Y, a_low, w_r, u_r)
        K.drain_side()
        if f < 2:
            K.side.append(project(f + 2, places_free[f + 1]))
        z_r = K.zero(Z[:, :], free)
        for n in range(TT):
            units = [n, TT + n]
            b, sa, rhs = K.banks.take(), step.take(), step.take()
            K.mm(b.t[:, 0:P], ra[:, n, 0, :], Z[:, :], z_r, b.free, ra_ready, signal=False, stop=False, loose=True)
            for hh, u in enumerate(units):
                m = K.mm(b.t[:, hh * DH:(hh + 1) * DH], AM[:, u, 0, :], Vt[:, n, hh * DH:(hh + 1) * DH],
                         am_ready[u], tm_ready, start=False, loose=True)
            k = K.a(rhs.t[:, :], b.t[:, 0:P], ACT.Copy, m, rhs.free)
            b.free = [k]
            K.fill(1)
            b = K.banks.take()
            for hh, u in enumerate(units):
                m = K.mm(b.t[:, hh * DH:(hh + 1) * DH], state[hh][1][:, n, :], rhs.t[:, hh * DH:(hh + 1) * DH],
                         k, state[hh][5], b.free)
            rhs.free = [m]
            sa_r = K.cp(sa.t[:, :], b.t[:, 0:P], m, sa.free)
            b.free = [sa_r]
            K.fill(1)
            if n < TT - 1:
                b = K.banks.take()
                K.mm(b.t[:, 0:P], Kt[:, n, :], Vt[:, n, :], b.free, signal=False, stop=False)
                mz = K.mm(b.t[:, 0:P], Bt[:, n, :], sa.t[:, :], sa_r, start=False)
                bz = b
            b = K.banks.take()
            K.mm(b.t[:, 0:P], ra[:, n, 1, :], Z[:, :], b.free, signal=False, stop=False, loose=True)
            for hh, u in enumerate(units):
                cs = slice(hh * DH, (hh + 1) * DH)
                K.mm(b.t[:, cs], AM[:, u, 1, :], Vt[:, n, cs], start=False, stop=False, signal=False, loose=True)
                m = K.mm(b.t[:, cs], AM[:, u, 3, :], sa.t[:, cs], sa_r, start=False, loose=True)
            y_ready = K.a(y[:, 2 * n:2 * n + 2, :], b.t[:, 0:P].rearrange("p (h d) -> p h d", h=2), ACT.Copy, m, free)
            b.free = [y_ready]
            sa.free = [m]
            K.fill(1)
            if n < TT - 1:
                for hh in range(2):
                    hp = slice(hh * DH, (hh + 1) * DH)
                    k = K.tt(Z[hp, hp], Z[hp, hp], bz.t[hp, hp], ALU.add, mz, m)
                bz.free = [k]
                z_r = K.ts(Z[:, :], Z[:, :], zs[:, n:n + 1], ALU.mult, k, zs_ready)
        K.drain_side()
        y_done = y_ready
    finish(norm(3, y_done, tokens[3]))
    K.banks, K.wring = all_banks, all_slots
    lent.free = [lane.last() for lane in (K.pe, K.act, K.dve, K.pool)]
    return outs


def merge(K, ctx, hT, oaT, obT, oa_ready, ob_ready, x):
    w = K.w
    K.cut_ring(ctx, 4)
    h = tuple(K.sb(ctx, f"h_{n}", [P, KD, S], F32R) for n in ("hi", "lo"))
    mT = tuple(K.sb(ctx, f"merged_{n}", [P, KD, S], F32R) for n in ("hi", "lo"))
    sg = Ring([Slot(hT[:, k, :]) for k in range(KD)])
    m_ready = []
    for quarter in range(4):
        slots = []
        gs = K.wring.take()
        gv = gs.t[:, :].rearrange("p (j k n) -> p j k n", j=2, k=KD)
        ggot = K.load(gs, [(gv[:, j, :, :], w["w_in"].rearrange("(k p) n -> p k n", p=P)[
            :, :, at + quarter * 256:at + (quarter + 1) * 256]) for j, at in enumerate((COL_GA, COL_GB))])
        if quarter % 2 == 0:
            ps = K.wring.take()
            pv = ps.t[:, :].rearrange("p (j k n) -> p j k n", j=2, k=4)
            pgot = K.load(ps, [(pv[:, j, :, :], w[n].rearrange("(k p) n -> p k n", p=P)[
                :, :, quarter * 256:quarter * 256 + 512]) for j, n in enumerate(("w_proj_a", "w_proj_b"))])
        for i in range(2):
            f, part = quarter * 2 + i, []
            cut = [K.cut(gv[:, j, :, i * P:(i + 1) * P], ggot) for j in range(2)]
            if f == 0:
                h_ready = [K.halves(h[0][:, k, :], h[1][:, k, :], hT[:, k, :]) for k in range(KD)]
                for s, k in zip(sg.slots, h_ready):
                    s.free = [k]
            if i == 1:
                gs.free = [cut[1][2]]
            if f == KD - 1:
                product = Product(K, w["w_out"], KD).begin()
            for j, (oT, o_ready) in enumerate(((oaT, oa_ready), (obT, ob_ready))):
                b = K.banks.take()
                m = K.project(b, b.t[:, :], lambda k: pv[:, j, k, (f % 4) * P:(f % 4 + 1) * P],
                              lambda k: oT[:, k, :], 4, pgot, o_ready)
                part.append((b, m))
            if quarter % 2 and i:
                ps.free = [m]
            for j in range(2):
                c, cols, c_ready = cut[j]
                b, s = K.banks.take(), sg.take()
                m = K.project3(b, b.t[:, :], lambda k: (cols[0][:, k, :], cols[1][:, k, :]),
                               lambda k: (h[0][:, k, :], h[1][:, k, :]), KD, c_ready, h_ready)
                c.free = [m]
                e = K.a(s.t[:, :], b.t[:, :], ACT.Sigmoid, m, s.free)
                b.free = [e]
                pb, pm = part[j]
                k = K.tt(s.t[:, :], s.t[:, :], pb.t[:, :], ALU.mult, e, pm)
                pb.free = [k]
                part[j] = (s, k)
            (s0, k0), (s1, k1) = part
            k = K.tt(s0.t[:, :], s0.t[:, :], s1.t[:, :], ALU.add, k0, k1)
            s1.free = [k]
            k = K.halves(mT[0][:, f, :], mT[1][:, f, :], s0.t[:, :], k)
            s0.free = [k]
            m_ready.append(k)
    return product.run(mT, lambda k: m_ready[k], x)


class Product:

    def __init__(self, K, w, n):
        self.K, self.n = K, n
        self.jobs = [(half, k0, slot0) for half in range(2) for slot0 in range(0, n, 8)
                     for k0 in range(slot0, min(slot0 + 8, n), 2)]
        self.src = w.rearrange("(k p) n -> p k n", p=P)
        self.pieces = {}

    def prepare(self, half, k0, slot0):
        K, n = self.K, self.n
        if k0 == slot0:
            m, s = min(8, n - slot0), K.wring.take()
            v = s.t[:, 0:m * 512].rearrange("p (k n) -> p k n", k=m)
            self.slot = (s, v, K.load(s, [(v, self.src[:, slot0:slot0 + m, half * 512:(half + 1) * 512])]))
        s, v, got = self.slot
        two = min(2, n - k0)
        c = K.cut(v[:, k0 - slot0:k0 - slot0 + two, :], got)
        if k0 + two in (slot0 + 8, n):
            s.free = [c[2]]
        self.pieces[half, k0] = (two, c)

    def begin(self):
        for job in self.jobs[0:2]:
            self.prepare(*job)
        return self

    def run(self, aT, ready, x, before_last=None):
        K, n, jobs = self.K, self.n, self.jobs
        done = [[] for _ in range(TT)]
        for job in jobs[0:2]:
            ready(job[1])
        for i, (half, k0, slot0) in enumerate(jobs):
            if i + 2 < len(jobs):
                self.prepare(*jobs[i + 2])
                ready(jobs[i + 2][1])
            elif i + 1 == len(jobs) and before_last:
                before_last()
            two, (c, cols, c_ready) = self.pieces.pop((half, k0))
            if k0 == 0:
                acc = [K.banks.take() for _ in range(TT)]
            for t in range(TT):
                for q in range(two):
                    k, ts_ = k0 + q, slice(t * P, (t + 1) * P)
                    m = K.mm3(acc[t].t[:, :], (aT[0][:, k, ts_], aT[1][:, k, ts_]), (cols[0][:, q, :], cols[1][:, q, :]),
                              c_ready, acc[t].free, ready(k), start=(k == 0), stop=(k == n - 1), signal=(q == two - 1))
                acc[t].free = []
                if k0 + two == n:
                    xs = x[:, t, half * 512:(half + 1) * 512]
                    e = K.tt(xs, xs, acc[t].t[:, :], ALU.add, m)
                    acc[t].free = [e]
                    done[t].append(e)
            c.free = [m]
        return done


def ffn(K, ctx, h2T, ready, x):
    w = K.w
    conv_rows = K.sb(ctx, "conv_rows", [4 * 2 * FT // 2, 2, P])
    cv = K.sb(ctx, "conv_cols", [P, 4, 2 * FT])
    sm = K.channel("ffn_small")
    for j in range(4):
        src = w["conv_b"] if j == 3 else w["conv_w"][j:j + 1, :]
        small = sm.dma(K.act, conv_rows[FT * j:FT * (j + 1), :, :],
                       src.rearrange("o (two k p) -> (o k) two p", two=2, p=P))
    for two in range(2):
        b = K.banks.take()
        m = K.tr(b.t[:, 0:4 * FT], conv_rows[:, two, :], small, b.free)
        cv_ready = K.cp(cv[:, :, two * FT:(two + 1) * FT], b.t[:, 0:4 * FT].rearrange("p (j k) -> p j k", j=4), m)
        b.free = [cv_ready]
    FH = 8
    fT = tuple(K.sb(ctx, f"ffn_{n}", [P, FH, S], F32R) for n in ("hi", "lo"))
    ub = K.ring(ctx, "ffn_u", 4, [P, S + 2])
    cb = K.ring(ctx, "ffn_c", 4, [P, S])
    K.cut_ring(ctx, 6)
    for s in ub.slots:
        s.free = [K.zero(s.t[:, 0:2])]
    w_up = w["w_up"].rearrange("(k p) n -> p k n", p=P)
    pieces, held = {}, {}

    def prepare(f):
        j, i = divmod(f, 2)
        if i == 0:
            s = K.wring.take()
            v = s.t[:, :].rearrange("p (k two n) -> p k two n", k=KD, two=2)
            held["w"] = (s, v, K.load(s, [(v[:, :, two, :], w_up[:, :, two * DFF + j * 256:two * DFF + (j + 1) * 256])
                                          for two in range(2)]))
        s, v, got = held["w"]
        pieces[f] = [K.cut(v[:, :, two, i * P:(i + 1) * P], got) for two in range(2)]
        if i == 1:
            s.free = [pieces[f][1][2]]

    f_free, f_ready = None, []
    for f in range(FT):
        if f == 0:
            prepare(0)
            prepare(1)
        if f % FH + 2 < FH and f + 2 < FT:
            prepare(f + 2)
        n = f % FH + 1
        last = n == FH or f + 1 == FT
        if last:
            product = Product(K, w["w_down"][(f + 1 - n) * P:(f + 1) * P, :], n).begin()
        conv = []
        for two in range(2):
            b, u, cbuf = K.banks.take(), ub.take(), cb.take()
            c, wc, c_ready = pieces[f][two]
            col = two * FT + f
            m = K.project3(b, b.t[:, :], lambda k: (wc[0][:, k, :], wc[1][:, k, :]),
                           lambda k: (h2T[0][:, k, :], h2T[1][:, k, :]), KD, c_ready, ready)
            c.free = [m]
            e = K.a(u.t[:, 2:S + 2], b.t[:, :], ACT.Copy, m, u.free)
            k = K.a(cbuf.t[:, :], b.t[:, :], ACT.Identity, m, cbuf.free, cv_ready,
                    scale=cv[:, 2, col:col + 1], bias=cv[:, 3, col:col + 1])
            b.free = [k]
            for tap in (1, 0):
                k = K.stt(cbuf.t[:, :], u.t[:, tap:tap + S], cv[:, tap, col:col + 1], cbuf.t[:, :],
                          ALU.mult, ALU.add, k, e)
            u.free = [k]
            conv.append((cbuf, k))
        (val, kv), (gt, kg) = conv
        sgm = ub.take()
        k = K.a(sgm.t[:, 2:S + 2], gt.t[:, :], ACT.Sigmoid, kg, sgm.free)
        k2 = K.tt(gt.t[:, :], gt.t[:, :], val.t[:, :], ALU.mult, kv, k, lane=K.pool)
        val.free = [k2]
        k = K.tt(gt.t[:, :], gt.t[:, :], sgm.t[:, 2:S + 2], ALU.mult, k, k2)
        sgm.free = [k]
        k = K.halves(fT[0][:, f % FH, :], fT[1][:, f % FH, :], gt.t[:, :], k, f_free)
        gt.free = [k]
        f_ready.append(k)
        if last:
            def next_part(f=f):
                if f + 1 < FT:
                    prepare(f + 1)
                    prepare(f + 2)

            done = product.run(fT, lambda k: f_ready[k], x, next_part)
            f_free, f_ready = K.pe.last(), []
    return done


def selected_attention(K, ctx, hT, ready, oT, spare):
    w, c = K.w, K.c
    w_in = w["w_in_2"]
    sm = K.channel("dsa_small")
    qT, kT = K.sb(ctx, "q2T", [P, 4, S]), K.sb(ctx, "k2T", [P, 4, S])
    va = K.sb(ctx, "va", [P, TT, NW])
    iqT, ikT = K.sb(ctx, "iqT", [P, 2, S]), K.sb(ctx, "ikT", [P, S])
    iw = K.sb(ctx, "iw", [P, TT, IH])
    big = K.sb(ctx, "dsa_bias", [P, NH, 512])
    gains = K.sb(ctx, "dsa_gains", [P, 2])
    score = K.sb(ctx, "score", [P, TT, S])
    masks = K.sb(ctx, "selmask", [P, TT, S], BF16)
    top = K.sb(ctx, "top8", [P, TT, 8])
    eye = K.sb(ctx, "eye_bf", [P, P], BF16)
    outer, ctx = ctx, ExitStack()
    relb = K.sb(ctx, "dsa_relb", [33, NH])
    tmp = K.ring(ctx, "dsa_tmp", 5, [P, S])
    eye_ready = K.cp(eye[:, :], c("ident"))
    for half in range(2):
        for j, name in enumerate(("q_norm_g_2", "k_norm_g_2")):
            small = sm.dma(K.act, gains[half * DH:(half + 1) * DH, j:j + 1], w[name].rearrange("o d -> d o"), slow=True)
    K.ts(gains[:, 0:1], gains[:, 0:1], DH ** -0.5, ALU.mult, small)
    K.load_distances(ctx, w["rel_bias_2"], relb)
    s = K.wring.take()
    width = IH * ID + 4 * ID + IH
    v = s.t[:, 0:KD * width].rearrange("p (k n) -> p k n", k=KD)
    src = w_in.rearrange("(k p) n -> p k n", p=P)
    got = K.load(s, [(v[:, :, 0:IH * ID + ID], src[:, :, COL2_IQ:COL2_IW])]
                 + [(v[:, :, 256 + q * ID:256 + (q + 1) * ID], src[:, :, COL2_IK:COL2_IW]) for q in range(1, 4)]
                 + [(v[:, :, 256 + 4 * ID:width], src[:, :, COL2_IW:COL2_QB])])
    for j in range(2):
        b = K.banks.take()
        m = K.project(b, b.t[:, :], lambda k: v[:, k, j * P:(j + 1) * P], lambda k: hT[:, k, :], KD, got, ready)
        iq_ready = K.a(iqT[:, j, :], b.t[:, :], ACT.Copy, m)
        b.free = [iq_ready]
    b = K.banks.take()
    m = K.project(b, b.t[:, :], lambda k: v[:, k, 256:256 + 4 * ID], lambda k: hT[:, k, :], KD)
    ik_ready = K.a(ikT[:, :], b.t[:, :], ACT.Copy, m)
    b.free = [ik_ready]
    b, m = K.few_columns(ctx, "iw_rows", lambda k: v[:, k, 256 + 4 * ID:width], IH, hT)
    s.free = [m]
    iw_ready = K.ts(iw[:, :, :], b.t[:, 0:TT * IH].rearrange("p (t h) -> p t h", t=TT), IH ** -0.5, ALU.mult, m)
    b.free = [iw_ready]

    big_ready = K.bias_table(ctx, "dsa", big, relb)
    rel = K.ring(ctx, "idx_r", 3, [P, S])
    mask_ready = {}

    def select():
        chain = {}
        for i in range(1, TT):
            n = (i + 1) * P
            for h in range(IH):
                rows = slice((h % 4) * ID, (h % 4 + 1) * ID)
                b, r = K.banks.take(), rel.take()
                m = K.mm(b.t[:, 0:n], iqT[rows, h // 4, i * P:(i + 1) * P], ikT[rows, 0:n], b.free, iq_ready, ik_ready)
                e = K.a(r.t[:, 0:n], b.t[:, 0:n], ACT.Relu, m, r.free, scale=ID ** -0.5)
                b.free = [e]
                if h == 0:
                    k = K.ts(score[:, i, 0:n], r.t[:, 0:n], iw[:, i, h:h + 1], ALU.mult, e, iw_ready)
                else:
                    k = K.stt(score[:, i, 0:n], r.t[:, 0:n], iw[:, i, h:h + 1], score[:, i, 0:n], ALU.mult, ALU.add, e, k)
                r.free = [k]
                yield
            diag = score[:, i, i * P:n]
            chain[i] = K.pool.do(lambda e, d=diag: e.affine_select(
                out=d, in_=d, compare_op=ALU.is_ge, fill=NEG, base=0, pattern=[[-1, P]], channel_multiplier=1), k)
        for last in [False] * (TOPK // 8 - 1) + [True]:
            for i in range(1, TT):
                n = (i + 1) * P
                sc, t8 = score[:, i, 0:n], top[:, i, :]
                k = K.dve.do(lambda e, sc=sc, t8=t8: e.max(t8, sc), chain[i])
                chain[i] = K.dve.do(lambda e, sc=sc, t8=t8: e.match_replace(sc, t8, sc, TAKEN), k)
                if last:
                    mask_ready[i] = K.ts(masks[:, i, 0:n], sc, 0.5 * TAKEN, ALU.is_gt, chain[i], s2=NEG, op1=ALU.mult)
                yield

    K.side.append(select())
    per_product = -(-((TT - 1) * (IH + TOPK // 8)) // (3 * TT))

    def feature_major(dst, at, gain):
        s, v, got = K.weights(w_in, at, 512)
        for f in range(4):
            b = K.banks.take()
            m = K.project(b, b.t[:, :], lambda k: v[:, k, f * P:(f + 1) * P], lambda k: hT[:, k, :], KD, got)
            r = K.head_norm(tmp, b, m, dst[:, f, :], gain)
            K.fill(per_product)
        s.free = [m]
        return r

    q_ready = feature_major(qT, COL2_Q, gains[:, 0:1])
    k_ready = feature_major(kT, COL2_K, gains[:, 1:2])
    s, v, got = K.weights(w_in, COL2_V, 512)
    for t in range(TT):
        b = K.banks.take()
        m = K.project(b, b.t[:, :], lambda k: hT[:, k, t * P:(t + 1) * P], lambda k: v[:, k, :], KD, got)
        v_ready = K.a(va[:, t, :], b.t[:, :], ACT.Copy, m)
        b.free = [v_ready]
        K.fill(per_product)
    s.free = [m]

    K.drain_side()
    K.meet()
    ctx.close()
    ctx = outer

    def extra(i, out):
        return K.mm(out, eye[:, :], masks[:, i, 0:(i + 1) * P], mask_ready[i], eye_ready, start=False)

    o = spare
    rc = K.sb(ctx, "dsa_rc", [P, TT, NH])
    o_ready = {}

    def finish(i, b, got, sums, sums_ready):
        k = K.recip(rc[:, i, :], sums, sums_ready)
        k = K.tt(o[:, i, :].rearrange("p (h d) -> p h d", h=NH), b.t[:, :].rearrange("p (h d) -> p h d", h=NH),
                 spread(rc[:, i, :], DH), ALU.mult, k, got)
        o_ready[i] = k
        return k

    K.attention(ctx, "dsa", [(lambda h: qT[(h % 2) * DH:(h % 2 + 1) * DH, h // 2, :],
                              lambda h: kT[(h % 2) * DH:(h % 2 + 1) * DH, h // 2, :],
                              lambda h, j: va[:, j, h * DH:(h + 1) * DH],
                              [q_ready, k_ready, v_ready, big_ready], finish, extra)], big)
    return K.to_fm(o, o_ready, oT)


def gla(K, ctx, hT, ready, oT):
    w, c = K.w, K.c
    w_in = w["w_in_2"]
    sm = K.channel("gla_small")
    w2 = K.sb(ctx, "gla_w2", [RANK, 2 * P])
    cols = K.sb(ctx, "gla_cols", [P, 3])
    small = sm.dma(K.act, w2[:, :], w["gla_gate_w2_2"])
    small = sm.dma(K.act, cols[:, 0:2], w["gla_gate_b_2"].rearrange("o (k p) -> p (o k)", p=P), slow=True)
    small = sm.dma(K.act, cols[:, 2:3], w["gla_out_norm_g_2"].rearrange("o d -> d o"), slow=True)
    NCH = S // GC
    ones = K.sb(ctx, "gla_ones", [P, P])
    ones_ready = K.zero(ones[:, :], value=1.0)
    tmp = K.ring(ctx, "gla_tmp", 4, [P, S])
    rg = K.sb(ctx, "rgT", [P, 4, S])
    vb = K.sb(ctx, "vb", [P, TT, RW])
    qT, kT = K.sb(ctx, "gla_qT", [P, 2, S]), K.sb(ctx, "gla_kT", [P, 2, S])
    glr = K.sb(ctx, "glr", [RANK, S])

    s, v, got = K.weights(w_in, COL2_QB, 512)
    for j in range(4):
        b = K.banks.take()
        m = K.project(b, b.t[:, :], lambda k: v[:, k, j * P:(j + 1) * P], lambda k: hT[:, k, :], KD, got, ready)
        if j < 2:
            qk_ready = K.a(qT[:, j, :], b.t[:, :], ACT.Copy, m, scale=BK ** -0.5)
        else:
            qk_ready = K.a(kT[:, j - 2, :], b.t[:, :], ACT.Copy, m)
        b.free = [qk_ready]
    s.free = [m]
    s, v, got = K.weights(w_in, COL2_LR, RANK)
    b = K.banks.take()
    m = K.project(b, b.t[0:RANK, :], lambda k: v[:, k, :], lambda k: hT[:, k, :], KD, got)
    s.free = [m]
    glr_ready = K.a(glr[:, :], b.t[0:RANK, :], ACT.Copy, m)
    b.free = [glr_ready]
    L, Lc, E1, E2 = (K.sb(ctx, f"gla_{n}", [P, 2, NCH, GC + 1]) for n in ("L", "Lc", "E1", "E2"))
    ready0 = K.zero(L[:, :, :, 0:1])
    qt, kt = K.sb(ctx, "gla_qt", [P, 2, S]), K.sb(ctx, "gla_kt", [P, 2, S])
    ktm = K.sb(ctx, "gla_ktm", [P, 2, TT, P])
    A = K.sb(ctx, "gla_A", [P, 2, 2, TT, P])
    ready0 = [ready0, K.zero(A[:, :, :, :, :])]
    zs = K.sb(ctx, "gla_zs", [P, 2, NCH])
    pair = {}

    def prepare(j):
        b = K.banks.take()
        m = K.mm(b.t[:, :], w2[:, j * P:(j + 1) * P], glr[:, :], glr_ready, small, b.free)
        x, t = tmp.take(), tmp.take()
        kx = K.ts(x.t[:, :], b.t[:, :], cols[:, j:j + 1], ALU.add, m, x.free)
        b.free = [kx]
        k = K.a(t.t[:, :], x.t[:, :], ACT.Abs, kx, t.free)
        k = K.a(t.t[:, :], t.t[:, :], ACT.Exp, k, scale=-1.0)
        k = K.a(t.t[:, :], t.t[:, :], ACT.Ln, k, bias=1.0)
        k = K.stt(x.t[:, :], x.t[:, :], 0.0, t.t[:, :], ALU.min, ALU.subtract, k)
        t.free = [k]
        k = K.ts(x.t[:, :], x.t[:, :], 1.0 / TEMP, ALU.mult, k)
        for n in range(NCH):
            ks = K.dve.do(lambda e, n=n, x=x, j=j: e.tensor_tensor_scan(
                L[:, j, n, 1:GC + 1], ones[:, 0:GC], x.t[:, n * GC:(n + 1) * GC], 0.0, ALU.mult, ALU.add),
                k, ones_ready, ready0)
        x.free = [ks]
        k = K.tt(Lc[:, j, :, :], L[:, j, :, :], L[:, j, :, 32:33].broadcast_to([P, NCH, GC + 1]), ALU.subtract, ks)
        e1 = K.a(E1[:, j, :, :], Lc[:, j, :, :], ACT.Exp, k)
        e2 = K.a(E2[:, j, :, :], Lc[:, j, :, :], ACT.Exp, k, scale=-1.0)
        v8 = lambda y: y.rearrange("p (n t) -> p n t", n=NCH)
        qt_r = K.tt(v8(qt[:, j, :]), v8(qT[:, j, :]), E1[:, j, :, 1:GC + 1], ALU.mult, e1, qk_ready)
        kt_r = K.tt(v8(kt[:, j, :]), v8(kT[:, j, :]), E2[:, j, :, 1:GC + 1], ALU.mult, e2, qk_ready)
        zs_r = K.tt(zs[:, j, 0:NCH - 1], E1[:, j, 0:NCH - 1, GC:GC + 1].rearrange("p n o -> p (n o)"),
                    E2[:, j, 1:NCH, 0:1].rearrange("p n o -> p (n o)"), ALU.mult, e1, e2)
        yield
        b = K.banks.take()
        for n in range(TT):
            m = K.tr(b.t[:, n * P:(n + 1) * P], kt[:, j, n * P:(n + 1) * P], kt_r, b.free, signal=(n == TT - 1))
        ktm_r = K.a(ktm[:, j, :, :], b.t[:, :].rearrange("p (n t) -> p n t", n=TT), ACT.Copy, m)
        b.free = [ktm_r]
        for hh in range(2):
            yield
            hp = slice(hh * BK, (hh + 1) * BK)
            b = K.banks.take()
            for n in range(TT):
                ts_ = slice(n * P, (n + 1) * P)
                m = K.mm(b.t[:, ts_], kt[hp, j, ts_], qt[hp, j, ts_], kt_r, qt_r, b.free, signal=(n == TT - 1))
            a_r = K.dve.do(lambda e, b=b, j=j, hh=hh: e.copy_predicated(
                A[:, j, hh, :, :], spread(c("mask_gla").bitcast(I32), 4, 1),
                b.t[:, :].rearrange("p (x t) -> p x t", x=4)), m, ready0)
            b.free = [a_r]
        pair[j] = (qt_r, zs_r, ktm_r, a_r)
        yield

    K.side.append(step for steps in zip(prepare(0), prepare(1)) for step in steps)
    s, v, got = K.weights(w_in, COL2_VB, 512)
    for t in range(TT):
        b = K.banks.take()
        m = K.project(b, b.t[:, :], lambda k: hT[:, k, t * P:(t + 1) * P], lambda k: v[:, k, :], KD, got)
        vb_ready = K.a(vb[:, t, :], b.t[:, :], ACT.Copy, m)
        b.free = [vb_ready]
        if t == 0:
            K.fill(2)
    s.free = [m]
    K.drain_side()
    all_banks = K.banks
    K.banks, side_banks = Ring(all_banks.slots[0:6]), Ring(all_banks.slots[6:8])
    rg_ready = []

    def gates():
        s, v, got = K.weights(w_in, COL2_RG, 512)
        for f in range(4):
            b, t = side_banks.take(), tmp.take()
            for k in range(KD):
                m = K.mm(b.t[:, :], v[:, k, f * P:(f + 1) * P], hT[:, k, :], b.free, got,
                         start=(k == 0), stop=(k == KD - 1), signal=(k == KD - 1))
                if k % 2:
                    yield
            e = K.a(t.t[:, :], b.t[:, :], ACT.Sigmoid, m, t.free)
            k = K.tt(rg[:, f, :], b.t[:, :], t.t[:, :], ALU.mult, m, e)
            rg_ready.append(k)
            b.free = t.free = [k]
        s.free = [m]

    K.side.append(gates())
    Z = K.sb(ctx, "gla_Z", [P, 2, 2 * BV])
    z_r = [K.zero(Z[:, j, :]) for j in range(2)]
    o = K.sb(ctx, "gla_o", [P, TT, RW])
    o_r = {}
    st = K.sb(ctx, "gla_st", [P, TT, 3, BH])

    def norm(n):
        t = tmp.take()
        sq = t.t[:, :].rearrange("p (h d) -> p h d", h=BH)
        o3 = o[:, n, :].rearrange("p (h d) -> p h d", h=BH)
        ms, rc, rs = (st[:, n, q, :] for q in range(3))
        k = K.a(sq, o3, ACT.Square, o_r[n], t.free)
        k = K.red(ms, sq, ALU.add, k)
        t.free = [k]
        k = K.ts(ms, ms, 1.0 / BV, ALU.mult, k, s2=RMS_EPS, op1=ALU.add)
        k = K.recip(rc, ms, k)
        k = K.a(rs, rc, ACT.Sqrt, k)
        o_r[n] = K.tt(o3, o3, spread(rs, BV), ALU.mult, k)

    for n in range(TT):
        for j in range(2):
            qt_r, zs_r, ktm_r, a_r = pair[j]
            b = K.banks.take()
            for hh in range(2):
                h = 2 * j + hh
                K.mm(b.t[:, hh * BV:(hh + 1) * BV], A[:, j, hh, n, :], vb[:, n, h * BV:(h + 1) * BV],
                     a_r, vb_ready, b.free, start=(hh == 0), stop=False, signal=False, loose=True)
            for half in range(2):
                ch = 2 * n + half
                rows = slice(half * GC, (half + 1) * GC)
                m = K.mm(b.t[rows, 0:2 * BV], qt[:, j, n * P + half * GC:n * P + (half + 1) * GC], Z[:, j, :],
                         z_r[j], qt_r, start=False, stop=(half == 1), loose=True)
                if ch < NCH - 1:
                    b2 = K.banks.take()
                    m2 = K.mm(b2.t[:, 0:2 * BV], ktm[rows, j, n, :], vb[rows, n, 2 * j * BV:(2 * j + 2) * BV],
                              ktm_r, b2.free)
                    for hh in range(2):
                        hp, cs = slice(hh * BK, (hh + 1) * BK), slice(hh * BV, (hh + 1) * BV)
                        k = K.tt(Z[hp, j, cs], Z[hp, j, cs], b2.t[hp, cs], ALU.add, m, m2)
                    K.fill(1)
                    b2.free = [k]
                    z_r[j] = K.ts(Z[:, j, :], Z[:, j, :], zs[:, j, ch:ch + 1], ALU.mult, k, zs_r)
            e = K.a(o[:, n, j * 2 * BV:(j + 1) * 2 * BV], b.t[:, 0:2 * BV], ACT.Copy, m)
            b.free = [e]
            o_r[n] = e
        if n:
            norm(n - 1)
    norm(TT - 1)
    K.drain_side()
    K.banks = all_banks
    for f in range(4):
        b = K.banks.take()
        for n in range(TT):
            m = K.tr(b.t[:, n * P:(n + 1) * P], o[:, n, f * P:(f + 1) * P], o_r[n], b.free, signal=(n == TT - 1))
        k = K.stt(oT[:, f, :], b.t[:, :], cols[:, 2:3], rg[:, f, :], ALU.mult, ALU.mult, m, rg_ready)
        b.free = [k]
    return k


def add_mixed(K, ctx, o1T, o2T, ready, x):
    K.cut_ring(ctx, 5)
    oT = tuple(K.sb(ctx, f"o_{n}", [P, KD, S], F32R) for n in ("hi", "lo"))
    o_ready = {}

    def halves_of(k):
        if k not in o_ready:
            o_ready[k] = K.halves(oT[0][:, k, :], oT[1][:, k, :], (o1T if k < 4 else o2T)[:, k % 4, :], ready[k // 4])
        return o_ready[k]

    return Product(K, K.w["w_out_2"], KD).begin().run(oT, halves_of, x)


def load_router(K, ctx):
    sm = K.channel("moe_small")
    wr = K.sb(ctx, "w_router", [P, KD, XG + NE])
    br = K.sb(ctx, "b_router", [P, XG + NE])
    small = sm.dma(K.sp, wr[:, :, 0:XG], K.w["w_router_group_2"].rearrange("(k p) n -> p k n", p=P))
    small = sm.dma(K.sp, wr[:, :, XG:], K.w["w_router_expert_2"].rearrange("(k p) n -> p k n", p=P))
    small = sm.dma(K.sp, br[:, 0:XG], K.w["b_router_group_2"].rearrange("o n -> (o n)").partition_broadcast(P))
    small = sm.dma(K.sp, br[:, XG:], K.w["b_router_expert_2"].rearrange("o n -> (o n)").partition_broadcast(P))
    return wr, br, small


class ExpertWeights:

    def __init__(self, K, ctx):
        self.K, self.up, self.down, self.n = K, {}, {}, [0, 0]
        self.dring = K.ring(ctx, "wd", 4, [P, 2, D], channels=True)
        for s in self.dring.slots:
            s.free = [t for t in K.met if t]

    def fetch(self, down, further=None, ready=None):
        K, n = self.K, self.n[down]
        self.n[down] += 1
        s = (self.dring if down else K.wring).take()
        K.sp.wait(ready if n >= NE else None, s.free)
        s.free = []
        if down:
            v = s.t[:, :, :]
            parts = [(v, K.w["w_exp_down_2"], 2)]
        else:
            v = s.t[:, :].rearrange("p (two k n) -> p two k n", two=2, k=KD)
            parts = [(v[:, 0, :, :], K.w["w_exp_gate_2"], KD), (v[:, 1, :, :], K.w["w_exp_up_2"], KD)]
        s.channel.count += 16 * len(parts)

        def issue(e):
            at = slice(n, n + 1) if n < NE else \
                bass.ds(e.value_load(further[0:1, n - NE:n - NE + 1], min_val=0, max_val=NE - 1), 1)
            for dst, src, k in parts:
                e.dma_start(dst, src[at, :, :].rearrange("o (p k) n -> p (o k) n", k=k)).then_inc(s.channel.sem, 16)
        K.sp.queue.append(issue)
        (self.down if down else self.up)[n] = (s, v, (s.channel.sem, s.channel.count))


def moe(K, ctx, ew, router, rows, spare, hT, ready, h_dram, h_stored, x, x_ready, out):
    nc, w, c = K.nc, K.w, K.c
    wr, br, small = router
    K.cut_ring(ctx, 4)
    halved = {}

    def cut(n, q):
        s, v, w_r = ew.up[n]
        c = K.cuts.take()
        hi, lo = (c.t[:, j, :].rearrange("p (k two n) -> p two k n", k=2, two=2) for j in range(2))
        k = K.halves(hi, lo, v[:, :, 2 * q:2 * q + 2, :], c.free, w_r)
        c.free = []
        halved[n, q] = (c, k)
        if q == KD // 2 - 1:
            s.free = [k]

    for q in range(4):
        cut(0, q)
    NF = NTILE - NE
    s4 = K.sb(ctx, "moe_s4", [P, 8, TT])
    posi = K.sb(ctx, "posi", [P, 2, TT], U32)
    slot_tok = K.sb(ctx, "slot_tok", [P, NTILE], U32)
    tei = K.sb(ctx, "tile_ei", [P, NF], I32)
    keep, ctx = ctx, ExitStack()
    lg = K.sb(ctx, "logits", [P, TT, XG + NE])
    pad = K.sb(ctx, "group_pad", [P, TT, XE])
    z = K.zero(pad[:, :, :], value=NEG)
    b, m = K.few_columns(ctx, "logit_rows", lambda k: wr[:, k, :], XG + NE, hT, small, ready)
    k = K.tt(lg[:, :, :], b.t[:, 0:TT * 36].rearrange("p (t n) -> p t n", t=TT), spread(br[:, :], TT, 1), ALU.add, m)
    b.free = [k]
    lg_r = k
    k = K.cp(pad[:, :, 0:XG], lg[:, :, 0:XG], k, z)
    top = K.sb(ctx, "mx", [P, 2, TT, 8])
    idx = K.sb(ctx, "mi", [P, 2, TT, 8], U32)
    idf = K.sb(ctx, "mif", [P, 2, TT, 8])
    esel = K.sb(ctx, "esel", [P, TT, XE])
    t8 = K.sb(ctx, "moe_t8", [P, TT, XE])
    g1h = K.sb(ctx, "g1h", [P, TT, XE])
    e1h = K.sb(ctx, "e1h", [P, 2, TT, XE])

    def best(j, src, k):
        for t in range(TT):
            k1 = K.dve.do(lambda e, t=t: e.max(top[:, j, t, :], src[:, t, :]), k)
            k1 = K.dve.do(lambda e, t=t: e.max_index(idx[:, j, t, :], top[:, j, t, :], src[:, t, :]), k1)
        return K.cp(idf[:, j, :, :], idx[:, j, :, :], k1)

    iota = spread(c("iota"), TT, 1)
    k = best(0, pad, k)
    k = K.tt(g1h[:, :, :], iota, idf[:, 0, :, 0:1].broadcast_to([P, TT, XE]), ALU.is_equal, k)
    g_r = k
    k = K.tt(t8[:, :, :], pad[:, :, :], top[:, 0, :, 0:1].broadcast_to([P, TT, XE]), ALU.subtract, k)
    k = K.a(t8[:, :, :], t8[:, :, :], ACT.Exp, k)
    k = K.red(s4[:, 0, :], t8[:, :, :], ALU.add, k)
    gw_r = K.recip(s4[:, 1, :], s4[:, 0, :], k)
    for g in range(XG):
        src = lg[:, :, XG + g * XE:XG + (g + 1) * XE]
        on = g1h[:, :, g:g + 1].broadcast_to([P, TT, XE])
        if g == 0:
            k = K.tt(esel[:, :, :], src, on, ALU.mult, g_r)
        else:
            k1 = K.tt(t8[:, :, :], src, on, ALU.mult, k, gw_r)
            k = K.tt(esel[:, :, :], esel[:, :, :], t8[:, :, :], ALU.add, k1)
    k = best(1, esel, k)
    for j in range(2):
        e_r = K.tt(e1h[:, j, :, :], iota, idf[:, 1, :, j:j + 1].broadcast_to([P, TT, XE]), ALU.is_equal, k)
    d = s4[:, 2, :]
    k = K.tt(d, top[:, 1, :, 1], top[:, 1, :, 0], ALU.subtract, k)
    k = K.a(d, d, ACT.Exp, k)
    k = K.ts(s4[:, 3, :], d, 1.0, ALU.add, k)
    k = K.recip(s4[:, 4, :], s4[:, 3, :], k)
    k = K.tt(s4[:, 5, :], s4[:, 4, :], s4[:, 1, :], ALU.mult, k)
    wt_r = K.tt(s4[:, 6, :], s4[:, 5, :], d, ALU.mult, k)
    weight = (s4[:, 5, :], s4[:, 6, :])
    mem = K.sb(ctx, "member", [P, 2, TT, NE])
    both = K.sb(ctx, "member2", [P, TT, NE])
    for j in range(2):
        for g in range(XG):
            k = K.tt(mem[:, j, :, g * XE:(g + 1) * XE], e1h[:, j, :, :], g1h[:, :, g:g + 1].broadcast_to([P, TT, XE]),
                     ALU.mult, e_r)
    k = K.tt(both[:, :, :], mem[:, 0, :, :], mem[:, 1, :, :], ALU.add, k)
    b = K.banks.take()
    for t in range(TT):
        m = K.mm(b.t[:, t * NE:(t + 1) * NE], c("before"), both[:, t, :], k, b.free, start=True, stop=(t == 0))
        for u in range(t):
            m = K.mm(b.t[:, t * NE:(t + 1) * NE], c("allones"), both[:, u, :], start=False, stop=(u == t - 1))
    for t in range(TT):
        m = K.mm(b.t[:, TT * NE:(TT + 1) * NE], c("allones"), both[:, t, :], start=(t == 0), stop=(t == TT - 1))
    cnt = K.sb(ctx, "counts", [P, 4, NE])
    n_e, tl, end, base = (cnt[:, q, :] for q in range(4))
    rank = K.sb(ctx, "rank", [P, TT, NE])
    kr = K.cp(rank[:, :, :], b.t[:, 0:TT * NE].rearrange("p (t n) -> p t n", t=TT), m)
    k = K.cp(n_e, b.t[:, TT * NE:(TT + 1) * NE], m)
    b.free = [k]
    k = K.ts(tl, n_e, P + 0.5, ALU.is_gt, k)
    for q in range(2, TT):
        k = K.stt(tl, n_e, P * q + 0.5, tl, ALU.is_gt, ALU.add, k)
    onesr = K.sb(ctx, "moe_ones", [P, NE])
    z = K.zero(onesr[:, :], value=1.0)
    k = K.dve.do(lambda e: e.tensor_tensor_scan(end, onesr[:, :], tl, 0.0, ALU.mult, ALU.add), k, z)
    end_r = k
    k = K.tt(base, end, tl, ALU.subtract, k)
    tile_ = K.sb(ctx, "tile_of", [P, TT, NE])
    beyond = K.sb(ctx, "beyond", [P, TT, NE])
    prod = K.sb(ctx, "pos_prod", [P, TT, NE])
    posf = K.sb(ctx, "posf", [P, 3, 2, TT])
    own = c("tile_no")[:, 0:NE]
    k = K.stt(base, base, float(NE - 1), own, ALU.add, ALU.subtract, k)
    k = K.ts(tile_[:, :, :], rank[:, :, :], P - 0.5, ALU.is_gt, kr)
    k = K.tt(beyond[:, :, :], tile_[:, :, :], spread(base, TT, 1), ALU.mult, k)
    for q in range(2, TT):
        k = K.stt(tile_[:, :, :], rank[:, :, :], P * q - 0.5, tile_[:, :, :], ALU.is_gt, ALU.add, k)
    k = K.stt(rank[:, :, :], tile_[:, :, :], -float(P), rank[:, :, :], ALU.mult, ALU.add, k)
    k = K.tt(tile_[:, :, :], tile_[:, :, :], beyond[:, :, :], ALU.add, k)
    k = K.tt(tile_[:, :, :], tile_[:, :, :], spread(own, TT, 1), ALU.add, k)
    for q, src in enumerate((tile_, rank)):
        for j in range(2):
            k = K.tt(prod[:, :, :], mem[:, j, :, :], src[:, :, :], ALU.mult, k)
            k = K.red(posf[:, q, j, :], prod[:, :, :], ALU.add, k)
    pair_tile, pair_slot = posf[:, 0, :, :], posf[:, 1, :, :]
    in_slot = K.sb(ctx, "in_slot", [P, 2, TT, P])
    in_tile = K.sb(ctx, "in_tile", [P, 2, TT, NTILE])
    for j in range(2):
        last = lambda y, n: y[:, j, :].unsqueeze(2).broadcast_to([P, TT, n])
        k = K.tt(in_slot[:, j, :, :], spread(c("slot_no"), TT, 1), last(pair_slot, P), ALU.is_equal, k)
        k = K.tt(in_tile[:, j, :, :], spread(c("tile_no"), TT, 1), last(pair_tile, NTILE), ALU.is_equal, k)
        k = K.tt(in_tile[:, j, :, :], in_tile[:, j, :, :], spread(c("token_no"), NTILE), ALU.mult, k)
    b = K.banks.take()
    for j in range(2):
        for t in range(TT):
            m = K.mm(b.t[:, 0:NTILE], in_slot[:, j, t, :], in_tile[:, j, t, :], k, b.free,
                     start=(j + t == 0), stop=(j == 1 and t == TT - 1))
    st_r = K.cp(slot_tok[:, :], b.t[:, 0:NTILE], m)
    b.free = [st_r]
    gring = Ring([Slot(sp.rearrange("p k n -> p (k n)")[:, q * D:(q + 1) * D], K.channel("in_gath"))
                  for sp in spare for q in range(2)])
    gathered = {}

    def gather(n):
        g = gring.take()
        K.pool.wait(st_r, g.free, h_stored)
        g.channel.count += 16
        K.pool.queue.append(lambda e, g=g, n=n: e.indirect_dma_start(
            out=g.t[:, :], out_offset=None, in_=h_dram[:, :],
            in_offset=bass.IndirectOffsetOnAxis(ap=slot_tok[:, n:n + 1], axis=0)).then_inc(g.channel.sem, 16))
        gathered[n] = (g, (g.channel.sem, g.channel.count))

    for n in range(3):
        gather(n)
    k = K.stt(posf[:, 2, :, :], pair_tile, float(P), pair_slot, ALU.mult, ALU.add, k)
    pos_r = K.cp(posi[:, :, :], posf[:, 2, :, :], k)
    cmp_ = K.sb(ctx, "tile_cmp", [P, NF, NE])
    tef = K.sb(ctx, "tile_ef", [P, NF])
    k = K.tt(cmp_[:, :, :], spread(end, NF, 1), spread(own[:, 0:NF], NE, 2), ALU.is_le, end_r)
    k = K.red(tef[:, :], cmp_[:, :, :], ALU.add, k)
    k = K.ts(tef[:, :], tef[:, :], float(NE - 1), ALU.min, k)
    te_r = K.cp(tei[:, :], tef[:, :], k)

    K.meet()
    ctx.close()
    ctx = keep
    ys = nc.dram_tensor("slot_out", (NTILE * P, D), F32, kind="Internal").ap()
    hgT = K.ring(ctx, "hgT", 2, [P, 2, KD, P], F32R)
    hd = Ring([Slot(hT[:, i, :].rearrange("p (q n) -> p q n", q=2)) for i in range(2)])
    hdT = Ring([Slot(hT[:, 2 + i, 0:2 * P].rearrange("p (q n) -> p q n", q=2)) for i in range(2)])
    yr = Ring([Slot(s.t, K.channel("store_y")) for s in rows])
    for s, t in zip(yr.slots, h_stored):
        s.free = [t]
    y_stored = []

    turned, hidden, hidden_t = {}, {}, {}

    def turn(n):
        g, g_r = gathered.pop(n)
        t = hgT.take()
        for half in range(2):
            b = K.banks.take()
            for j in range(4):
                q = half * 4 + j
                m = K.tr(b.t[:, j * P:(j + 1) * P], g.t[:, q:D:KD], g_r, b.free, signal=(j == 3))
            src = b.t[:, :].rearrange("p (k n) -> p k n", k=4)
            at = slice(half * 4, half * 4 + 4)
            e = K.halves(t.t[:, 0, at, :], t.t[:, 1, at, :], src, m, t.free)
            b.free = [e]
        g.free = [m]
        turned[n] = (t, e)

    def up(n):
        t, e = turned.pop(n)
        b = K.banks.take()
        for q in range(4):
            c, c_ready = halved.pop((n, q))
            for i in range(2):
                k = 2 * q + i
                m = K.mm3(b.t[:, :], (t.t[:, 0, k, :], t.t[:, 1, k, :]),
                          (c.t[:, 0, i * 512:(i + 1) * 512], c.t[:, 1, i * 512:(i + 1) * 512]), c_ready, e, b.free,
                          start=(k == 0), stop=(k == KD - 1), signal=(i == 1))
            b.free, c.free = [], [m]
            if n + 1 < NTILE:
                cut(n + 1, q)
        t.free = [m]
        hb = hd.take()
        k = K.a(hb.t[:, 0, :], b.t[:, 0:DE], ACT.Sigmoid, m, hb.free)
        k = K.tt(hb.t[:, 0, :], hb.t[:, 0, :], b.t[:, 0:DE], ALU.mult, k)
        k = K.tt(hb.t[:, 1, :], hb.t[:, 0, :], b.t[:, DE:2 * DE], ALU.mult, k)
        b.free = [k]
        hidden[n] = (hb, k)

    def turn_hidden(n):
        hb, k = hidden.pop(n)
        ht = hdT.take()
        b = K.banks.take()
        for j in range(2):
            m = K.tr(b.t[:, j * P:(j + 1) * P], hb.t[:, 1, j:DE:2], k, b.free, signal=(j == 1))
        hb.free = [m]
        e = K.cp(ht.t[:, :, :], b.t[:, 0:2 * P].rearrange("p (k n) -> p k n", k=2), m, ht.free)
        b.free = [e]
        hidden_t[n] = (ht, e)

    def down(n):
        ht, e = hidden_t.pop(n)
        s2, v, d_r = ew.down[n]
        yb = yr.take()
        for half in range(2):
            b = K.banks.take()
            m = K.project(b, b.t[:, :], lambda k: ht.t[:, k, :], lambda k: s2.t[:, k, half * 512:(half + 1) * 512],
                          2, d_r, e)
            dst = yb.t[:, half * 512:(half + 1) * 512]
            q = K.a(dst, b.t[:, :], ACT.Copy, m, yb.free) if half else K.cp(dst, b.t[:, :], m, yb.free)
            b.free = [q]
            if half == 0:
                q0 = q
        ht.free = s2.free = [m]
        t = K.store(ys[n * P:(n + 1) * P, :], yb.t[:, :], q, q0, lane=K.act, channel=yb.channel)
        yb.free = [t]
        y_stored.append(t)

    for n in range(NTILE + 3):
        if n + 3 < NTILE:
            gather(n + 3)
        if n < NTILE:
            turn(n)
        if 0 <= n - 3:
            down(n - 3)
            if ew.n[1] < NTILE:
                ew.fetch(1, tei, te_r)
        if 0 <= n - 2 < NTILE:
            turn_hidden(n - 2)
        if 0 <= n - 1 < NTILE:
            up(n - 1)
        if ew.n[0] < NTILE:
            ew.fetch(0, tei, te_r)

    for t in range(TT):
        s, ch = ew.dring.take(), K.channel(f"fin{t}")
        K.pool.wait(y_stored[-2:], s.free, pos_r)
        for j in range(2):
            ch.count += 16
            K.pool.queue.append(lambda e, s=s, ch=ch, j=j, t=t: e.indirect_dma_start(
                out=s.t[:, j, :], out_offset=None, in_=ys[:, :],
                in_offset=bass.IndirectOffsetOnAxis(ap=posi[:, j, t:t + 1], axis=0)).then_inc(ch.sem, 16))
        k = (ch.sem, ch.count)
        for j in range(2):
            k = K.stt(x[:, t, :], s.t[:, j, :], weight[j][:, t:t + 1], x[:, t, :], ALU.mult, ALU.add, k, wt_r, x_ready[t])
        s.free = [k]
        K.store(out[t * P:(t + 1) * P, :], x[:, t, :], k)


def build(nc, w, consts, dist, where, out, probes=()):
    with ExitStack() as ctx:
        K = Core(nc, ctx, w)
        K.where = where
        K.probe = dict(probes)
        K.banks = Ring([Slot(ctx.enter_context(nc.psum_tensor(f"bank{i}", [P, 512], F32))) for i in range(8)])
        K.consts = K.sb(ctx, "consts", [P, consts.shape[1]])
        K.dist_dram = dist
        x = K.sb(ctx, "x_res", [P, TT, D])
        K.wring = K.ring(ctx, "w", 3, [P, 8 * 512], channels=True)
        xin = []
        for t in range(TT):
            xin.append(K.channel(f"x_in{t}").dma(K.sp, x[:, t, :], w["x"][t * P:(t + 1) * P, :]))
            if t == 0:
                K.consts_ready = K.channel("const_in").dma(K.sp, K.consts[:, :], consts)
        K.pe.wait(K.consts_ready)

        gch = K.channel("gain_in")

        def load_gain(ctx, gname, lane):
            gain = K.sb(ctx, "norm_gain", [P, D])
            return gain, gch.dma(lane, gain[:, :], w[gname].rearrange("o n -> (o n)").partition_broadcast(P))

        def normed(name, gname, ready, hT, keep=None, ctx=None, loaded=None):
            with ExitStack() as c2:
                c2 = ctx or c2
                gain, g = loaded or load_gain(c2, gname, K.act)
                done = K.norm_to_fm(c2, name, x, gain[:, :], g, ready, hT, K.pe.last(), keep)
                K.meet()
            return done

        def probe(name, ap):
            if name in K.probe:
                K.meet()
                K.sp.wait([t for t in K.met if t])
                K.store(K.probe[name], ap)

        def block_buffers(c1):
            return K.sb(c1, "hT", [P, KD, S]), K.sb(c1, "oaT", [P, 4, S]), K.sb(c1, "obT", [P, 4, S])

        with ExitStack() as c1:
            hT, oaT, obT = block_buffers(c1)
            ready = normed("n1", "attn_norm_g", xin, hT)
            for lane in (K.act, K.dve, K.pool):
                lane.wait(K.consts_ready)
            probe("hT", hT[:, :, :])
            with ExitStack() as c2:
                oa = nsa(K, c2, hT, ready, oaT, obT)
                K.meet()
            probe("oaT", oaT[:, :, :])
            with ExitStack() as c2:
                ob = rwkv(K, c2, hT, ready, obT)
                K.meet()
            probe("obT", obT[:, :, :])
            with ExitStack() as c2:
                done = merge(K, c2, hT, oaT, obT, oa, ob, x)
                K.meet()
        probe("x1", x[:, :, :])
        with ExitStack() as c1:
            hp = tuple(K.sb(c1, f"h2_{n}", [P, KD, S], F32R) for n in ("hi", "lo"))
            ready = normed("n2", "ffn_norm_g", done, hp)
            with ExitStack() as c2:
                done = ffn(K, c2, hp, ready, x)
                K.meet()
        probe("x2", x[:, :, :])
        with ExitStack() as c1:
            hT, oaT, obT = block_buffers(c1)
            ready = normed("n3", "norm1_g_2", done, hT)
            with ExitStack() as c2:
                K.more_weights(c2)
                oa = selected_attention(K, c2, hT, ready, oaT, obT)
                K.meet()
            probe("o2aT", oaT[:, :, :])
            with ExitStack() as c2:
                K.more_weights(c2)
                ob = gla(K, c2, hT, ready, obT)
                K.meet()
            probe("o2bT", obT[:, :, :])
            with ExitStack() as c2:
                done = add_mixed(K, c2, oaT, obT, [oa, ob], x)
                K.meet()
            probe("x3", x[:, :, :])
            h_dram = nc.dram_tensor("h_rows", (S, D), F32, kind="Internal").ap()
            with ExitStack() as c2:
                K.sp.wait([t for t in K.met if t])
                gain = load_gain(c2, "norm2_g_2", K.sp)
                router = load_router(K, c2)
                ew = ExpertWeights(K, c2)
                for down in (0, 0, 0, 1, 1, 1, 1):
                    ew.fetch(down)
                n_stores = len(K.stores)
                ready = normed("n4", "norm2_g_2", done, hT, keep=h_dram, ctx=c2, loaded=gain)
                h_stored = K.stores[n_stores:]
                moe(K, c2, ew, router, K.norm_rows.slots, (oaT[:, :, :], obT[:, :, :]), hT, ready, h_dram, h_stored, x, done, out)
                K.meet()
        K.sp.wait(K.stores)

        block = ctx.enter_context(nc.Block())
        block.sync(K.sp.run)
        block.scalar(K.act.run)
        block.gpsimd(K.pool.run)
        block.vector(K.dve.run)
        block.tensor(K.pe.run)


_INS = [
    "x", "attn_norm_g", "w_in", "rel_bias", "q_norm_g", "k_norm_g", "cmp_pe_k", "cmp_w1_k", "cmp_w2_k",
    "cmp_pe_v", "cmp_w1_v", "cmp_w2_v", "rwkv_mu", "rwkv_w0", "rwkv_w2", "rwkv_a0", "rwkv_a2", "rwkv_g2",
    "rwkv_k_k", "rwkv_k_a", "rwkv_r_k", "rwkv_ln_g", "rwkv_ln_b", "w_proj_a", "w_proj_b", "w_out",
    "ffn_norm_g", "w_up", "conv_w", "conv_b", "w_down", "norm1_g_2", "w_in_2", "q_norm_g_2", "k_norm_g_2",
    "rel_bias_2", "gla_gate_w2_2", "gla_gate_b_2", "gla_out_norm_g_2", "w_out_2", "norm2_g_2",
    "w_router_group_2", "b_router_group_2", "w_router_expert_2", "b_router_expert_2", "w_exp_gate_2",
    "w_exp_up_2", "w_exp_down_2",
]


def kernel(**inputs):
    import concourse.bacc as _bacc
    from concourse.bass_utils import run_bass_kernel_spmd as _run

    nc = _bacc.Bacc("TRN2", target_bir_lowering=False, num_devices=1)
    arrays, w = {}, {}
    for name in _INS:
        a = np.ascontiguousarray(inputs[name])
        if a.shape[0] == 1 and a.ndim > 2:
            a = a.reshape(a.shape[1:])
        arrays[f"in_{name}"] = a
        w[name] = nc.dram_tensor(f"in_{name}", a.shape, mybir.dt.from_np(a.dtype), kind="ExternalInput").ap()
    table, where = constants()
    for name, a in (("consts", table), ("dist", distance_tables())):
        arrays[f"in_{name}"] = a
        w[name] = nc.dram_tensor(f"in_{name}", a.shape, F32, kind="ExternalInput").ap()
    out = nc.dram_tensor("out_x", (S, D), F32, kind="ExternalOutput").ap()
    build(nc, w, w.pop("consts"), w.pop("dist"), where, out)
    r = _run(nc, [arrays], core_ids=[0])
    return r.results[0]["out_x"].reshape(1, S, D)
```
